# Optimizing a Trainium2 kernel written in Bass

```python
import jax
import jax.numpy as jnp
from jax import lax
import numpy as np

D_MODEL = 1024
BATCH = 1
SEQ = 256
DEPTH = 2

HEAD_DIM = 64
D_MIX = D_MODEL
D_CONV = D_MIX // 4
D_RWKV = D_MIX // 4
D_NSA = D_MIX - D_CONV - D_RWKV
CONV_WIDTH = 31
CONV_GROUPS = D_CONV // HEAD_DIM
CONV_EPS = 1e-5
RWKV_HEADS = D_RWKV // HEAD_DIM
LORA_W = 64
LORA_A = 64
LORA_G = 128
RWKV_GN_EPS = 64e-5
NSA_HEADS = D_NSA // HEAD_DIM
NSA_KV_HEADS = 2
NSA_GROUP = NSA_HEADS // NSA_KV_HEADS
CMP_BLOCK = 32
CMP_STRIDE = 16
CMP_HIDDEN = 2 * HEAD_DIM
SEL_BLOCK = 64
N_SEL = 16
WINDOW = 512
Q_BLOCK = 128
FORCE_SCORE = 1e4
NEG_INF = -1e30
PEER_HEADS = 8
PEER_KEYS = 128
PEER_TOPK = 16
PEER_QDIM = 256
N_EXPERTS = PEER_KEYS * PEER_KEYS
PEER_CHUNK = 128
RMS_EPS = 1e-6
N_CONV_IN = 2 * D_CONV
N_RWKV_IN = 3 * D_RWKV + LORA_W + LORA_A + LORA_G
N_Q_IN = D_NSA
N_KV_IN = 6 * NSA_KV_HEADS * HEAD_DIM
N_GATE_IN = 3 * NSA_HEADS
N_IN = N_CONV_IN + N_RWKV_IN + N_Q_IN + N_KV_IN + N_GATE_IN

kernel_name = 'hymba_conv_rwkv7_nsa_peer_adaln'

def _rmsnorm(x, g):
    x32 = x.astype(jnp.float32)
    y = x32 * lax.rsqrt(jnp.mean(x32 * x32, axis=-1, keepdims=True) + RMS_EPS)
    return (y * g.astype(jnp.float32)).astype(x.dtype)

def _group_norm(y, n_groups, g, b, eps):
    shp = y.shape
    y32 = y.astype(jnp.float32).reshape(shp[:-1] + (n_groups, shp[-1] // n_groups))
    mu = jnp.mean(y32, axis=-1, keepdims=True)
    var = jnp.mean(jnp.square(y32 - mu), axis=-1, keepdims=True)
    yn = ((y32 - mu) * lax.rsqrt(var + eps)).reshape(shp)
    return (yn * g.astype(jnp.float32) + b.astype(jnp.float32)).astype(y.dtype)

def _conv_mixer(p, dw_w, dw_b, gn_g, gn_b):
    val, gate = jnp.split(p, 2, axis=-1)
    u = val * jax.nn.sigmoid(gate)
    y = lax.conv_general_dilated(u, dw_w.astype(u.dtype), window_strides=(1,),
                                 padding=((CONV_WIDTH - 1, 0),),
                                 dimension_numbers=('NWC', 'WIO', 'NWC'),
                                 feature_group_count=D_CONV) + dw_b
    y = _group_norm(y, CONV_GROUPS, gn_g, gn_b, CONV_EPS)
    return jax.nn.silu(y)

def _rwkv_mixer(p, mu, w0, w_up, a0, a_up, g_up, k_k, k_a, r_k, ln_g, ln_b):
    B, T, _ = p.shape
    f32 = jnp.float32
    prev = jnp.pad(p, ((0, 0), (1, 0), (0, 0)))[:, :-1]
    p = p + (prev - p) * mu
    r, k, v, xw, xa, xg = jnp.split(
        p, [D_RWKV, 2 * D_RWKV, 3 * D_RWKV, 3 * D_RWKV + LORA_W, 3 * D_RWKV + LORA_W + LORA_A], axis=-1)
    w_log = -jax.nn.softplus(-(w0 + jnp.tanh(xw) @ w_up).astype(f32)) - 0.5
    decay = jnp.exp(-jnp.exp(w_log))
    a = jax.nn.sigmoid((a0 + xa @ a_up).astype(f32))
    g = (jax.nn.sigmoid(xg) @ g_up).astype(f32)

    def heads(z):
        return z.astype(f32).reshape(B, T, RWKV_HEADS, HEAD_DIM)

    kk = heads(k * k_k)
    kk = kk / jnp.maximum(jnp.linalg.norm(kk, axis=-1, keepdims=True), 1e-12)
    k_eff = k.astype(f32) * (1.0 + (a - 1.0) * k_a.astype(f32))
    r_h, k_h, v_h, w_h, a_h = heads(r), heads(k_eff), heads(v), heads(decay), heads(a)

    def step(S, inp):
        r_t, w_t, k_t, v_t, kk_t, a_t = inp
        sa = jnp.einsum('bhvk,bhk->bhv', S, -kk_t)
        S = (S * w_t[:, :, None, :] + sa[..., None] * (kk_t * a_t)[:, :, None, :]
             + v_t[..., None] * k_t[:, :, None, :])
        return S, jnp.einsum('bhvk,bhk->bhv', S, r_t)

    def tm(z):
        return z.transpose(1, 0, 2, 3)

    S0 = jnp.zeros((B, RWKV_HEADS, HEAD_DIM, HEAD_DIM), f32)
    _, ys = lax.scan(step, S0, (tm(r_h), tm(w_h), tm(k_h), tm(v_h), tm(kk), tm(a_h)))
    y = ys.transpose(1, 0, 2, 3).reshape(B, T, D_RWKV)
    y = _group_norm(y, RWKV_HEADS, ln_g, ln_b, RWKV_GN_EPS)
    bonus = jnp.sum(r_h * k_h * r_k.astype(f32), axis=-1, keepdims=True) * v_h
    y = (y + bonus.reshape(B, T, D_RWKV)) * g
    return y.astype(p.dtype)

def _nsa_mixer(p_q, p_kv, p_gate, ck_pos, ck_w1, ck_w2, cv_pos, cv_w1, cv_w2):
    B, T, _ = p_q.shape
    G, R, dk = NSA_KV_HEADS, NSA_GROUP, HEAD_DIM
    f32 = jnp.float32
    scale = HEAD_DIM ** -0.5

    def kv_heads(z):
        return z.reshape(B, T, G, dk).transpose(0, 2, 1, 3)

    k_cmp, v_cmp, k_sel, v_sel, k_win, v_win = [kv_heads(z) for z in jnp.split(p_kv, 6, axis=-1)]

    n_c = (T - CMP_BLOCK) // CMP_STRIDE + 1
    cmp_idx = jnp.arange(n_c)[:, None] * CMP_STRIDE + jnp.arange(CMP_BLOCK)[None, :]

    def compress(z, pos, w1, w2):
        blk = (z[:, :, cmp_idx] + pos).reshape(B, G, n_c, CMP_BLOCK * dk)
        return jax.nn.silu(blk @ w1) @ w2

    kc = compress(k_cmp, ck_pos, ck_w1, ck_w2)
    vc = compress(v_cmp, cv_pos, cv_w1, cv_w2)
    cmp_end = cmp_idx[:, -1]

    n_s = T // SEL_BLOCK
    n_sel = min(N_SEL, n_s)
    ks = k_sel.reshape(B, G, n_s, SEL_BLOCK, dk)
    vs = v_sel.reshape(B, G, n_s, SEL_BLOCK, dk)
    cmp_start = jnp.arange(n_c) * CMP_STRIDE
    sel_start = jnp.arange(n_s) * SEL_BLOCK
    overlap = ((cmp_start[:, None] < sel_start[None, :] + SEL_BLOCK)
               & (cmp_start[:, None] + CMP_BLOCK > sel_start[None, :])).astype(f32)

    kw = jnp.pad(k_win, ((0, 0), (0, 0), (WINDOW, 0), (0, 0)))
    vw = jnp.pad(v_win, ((0, 0), (0, 0), (WINDOW, 0), (0, 0)))

    n_qb = T // Q_BLOCK
    q_all = p_q.reshape(B, n_qb, Q_BLOCK, G, R, dk).transpose(1, 0, 3, 4, 2, 5)
    g_all = jax.nn.sigmoid(p_gate.astype(f32)).reshape(B, n_qb, Q_BLOCK, 3, G, R).transpose(1, 0, 4, 5, 2, 3)
    b_ix = jnp.arange(B)[:, None, None, None]
    g_ix = jnp.arange(G)[None, :, None, None]

    def block(args):
        qi, q, gate = args
        t = qi * Q_BLOCK + jnp.arange(Q_BLOCK)
        valid_c = cmp_end[None, :] <= t[:, None]
        s_c = jnp.einsum('bgrqd,bgnd->bgrqn', q, kc).astype(f32) * scale
        p_c = jax.nn.softmax(jnp.where(valid_c, s_c, NEG_INF), axis=-1) * jnp.any(valid_c, axis=-1)[:, None]
        o_c = jnp.einsum('bgrqn,bgnd->bgrqd', p_c.astype(vc.dtype), vc)
        imp = jnp.einsum('bgrqn,ns->bgqs', p_c, overlap)
        blk_j = jnp.arange(n_s)[None, :]
        cur = (t // SEL_BLOCK)[:, None]
        forced = (blk_j == 0) | (blk_j == cur) | (blk_j == cur - 1)
        imp = jnp.where(forced, FORCE_SCORE, jnp.where(blk_j <= cur, imp, -1.0))
        _, sel = lax.top_k(imp, n_sel)
        k_g = ks[b_ix, g_ix, sel]
        v_g = vs[b_ix, g_ix, sel]
        key_pos = sel[..., None] * SEL_BLOCK + jnp.arange(SEL_BLOCK)
        valid_s = (key_pos <= t[None, None, :, None, None]).reshape(B, G, Q_BLOCK, n_sel * SEL_BLOCK)[:, :, None]
        s_s = jnp.einsum('bgrqd,bgqnld->bgrqnl', q, k_g).astype(f32).reshape(
            B, G, R, Q_BLOCK, n_sel * SEL_BLOCK) * scale
        p_s = jax.nn.softmax(jnp.where(valid_s, s_s, NEG_INF), axis=-1).reshape(
            B, G, R, Q_BLOCK, n_sel, SEL_BLOCK)
        o_s = jnp.einsum('bgrqnl,bgqnld->bgrqd', p_s.astype(v_g.dtype), v_g)
        start = qi * Q_BLOCK
        k_w = lax.dynamic_slice_in_dim(kw, start, WINDOW + Q_BLOCK, axis=2)
        v_w = lax.dynamic_slice_in_dim(vw, start, WINDOW + Q_BLOCK, axis=2)
        key_w = start - WINDOW + jnp.arange(WINDOW + Q_BLOCK)
        dist = t[:, None] - key_w[None, :]
        valid_w = (dist >= 0) & (dist < WINDOW) & (key_w[None, :] >= 0)
        s_w = jnp.einsum('bgrqd,bgkd->bgrqk', q, k_w).astype(f32) * scale
        p_w = jax.nn.softmax(jnp.where(valid_w, s_w, NEG_INF), axis=-1)
        o_w = jnp.einsum('bgrqk,bgkd->bgrqd', p_w.astype(v_w.dtype), v_w)
        o = gate[..., 0, None] * o_c + gate[..., 1, None] * o_s + gate[..., 2, None] * o_w
        return o.astype(q.dtype)

    out = lax.map(block, (jnp.arange(n_qb), q_all, g_all))
    return out.transpose(1, 0, 4, 2, 3, 5).reshape(B, T, D_NSA)

def _peer(h, wq, k1, k2, u, v):
    B, T, D = h.shape
    half = PEER_QDIM // 2
    tok = h.reshape(-1, PEER_CHUNK, D)

    def chunk(hc):
        q = (hc @ wq).reshape(PEER_CHUNK, PEER_HEADS, PEER_QDIM)
        s1 = jnp.einsum('chd,nd->chn', q[..., :half], k1).astype(jnp.float32)
        s2 = jnp.einsum('chd,nd->chn', q[..., half:], k2).astype(jnp.float32)
        v1, i1 = lax.top_k(s1, PEER_TOPK)
        v2, i2 = lax.top_k(s2, PEER_TOPK)
        cand = (v1[..., :, None] + v2[..., None, :]).reshape(PEER_CHUNK, PEER_HEADS, PEER_TOPK * PEER_TOPK)
        sc, ci = lax.top_k(cand, PEER_TOPK)
        e = (jnp.take_along_axis(i1, ci // PEER_TOPK, axis=-1) * PEER_KEYS
             + jnp.take_along_axis(i2, ci % PEER_TOPK, axis=-1))
        gw = jax.nn.softmax(sc, axis=-1)
        hid = jnp.einsum('chkd,cd->chk', u[e], hc).astype(jnp.float32)
        act = (jax.nn.gelu(hid, approximate=False) * gw).astype(hc.dtype)
        return jnp.einsum('chk,chkd->cd', act, v[e])

    return lax.map(chunk, tok).reshape(B, T, D)

def setup_inputs(seed: int = 0) -> dict:
    key = jax.random.key(seed)
    keys = iter(jax.random.split(key, 64))
    L, D = DEPTH, D_MODEL

    def nrm(shape, s):
        return jax.random.normal(next(keys), shape, jnp.float32) * s

    return {
        'x': nrm((BATCH, SEQ, D), 1.0),
        'c': nrm((BATCH, D), 1.0),
        'ada_w': nrm((L, D, 6 * D), 0.5 * D ** -0.5),
        'ada_b': nrm((L, 6 * D), 0.01),
        'norm1_g': 1.0 + nrm((L, D), 0.02),
        'norm2_g': 1.0 + nrm((L, D), 0.02),
        'w_in': nrm((L, D, N_IN), D ** -0.5),
        'conv_dw_w': nrm((L, CONV_WIDTH, 1, D_CONV), CONV_WIDTH ** -0.5),
        'conv_dw_b': nrm((L, D_CONV), 0.01),
        'conv_gn_g': 1.0 + nrm((L, D_CONV), 0.02),
        'conv_gn_b': nrm((L, D_CONV), 0.01),
        'rwkv_mu': jax.random.uniform(next(keys), (L, N_RWKV_IN), jnp.float32),
        'rwkv_w0': nrm((L, D_RWKV), 1.0) - 1.0,
        'rwkv_w_up': nrm((L, LORA_W, D_RWKV), LORA_W ** -0.5),
        'rwkv_a0': nrm((L, D_RWKV), 0.5),
        'rwkv_a_up': nrm((L, LORA_A, D_RWKV), LORA_A ** -0.5),
        'rwkv_g_up': nrm((L, LORA_G, D_RWKV), LORA_G ** -0.5),
        'rwkv_k_k': 0.85 + nrm((L, D_RWKV), 0.1),
        'rwkv_k_a': 1.0 + nrm((L, D_RWKV), 0.1),
        'rwkv_r_k': nrm((L, RWKV_HEADS, HEAD_DIM), 0.1),
        'rwkv_ln_g': 1.0 + nrm((L, D_RWKV), 0.02),
        'rwkv_ln_b': nrm((L, D_RWKV), 0.01),
        'nsa_ck_pos': nrm((L, CMP_BLOCK, HEAD_DIM), 0.1),
        'nsa_ck_w1': nrm((L, CMP_BLOCK * HEAD_DIM, CMP_HIDDEN), (CMP_BLOCK * HEAD_DIM) ** -0.5),
        'nsa_ck_w2': nrm((L, CMP_HIDDEN, HEAD_DIM), CMP_HIDDEN ** -0.5),
        'nsa_cv_pos': nrm((L, CMP_BLOCK, HEAD_DIM), 0.1),
        'nsa_cv_w1': nrm((L, CMP_BLOCK * HEAD_DIM, CMP_HIDDEN), (CMP_BLOCK * HEAD_DIM) ** -0.5),
        'nsa_cv_w2': nrm((L, CMP_HIDDEN, HEAD_DIM), CMP_HIDDEN ** -0.5),
        'w_out': nrm((L, D_MIX, D), D_MIX ** -0.5),
        'peer_wq': nrm((L, D, PEER_HEADS * PEER_QDIM), D ** -0.5),
        'peer_k1': nrm((L, PEER_KEYS, PEER_QDIM // 2), (PEER_QDIM // 2) ** -0.5),
        'peer_k2': nrm((L, PEER_KEYS, PEER_QDIM // 2), (PEER_QDIM // 2) ** -0.5),
        'peer_u': nrm((L, N_EXPERTS, D), D ** -0.5),
        'peer_v': nrm((L, N_EXPERTS, D), 1.0),
        'final_g': 1.0 + nrm((D,), 0.02),
    }

def reference(x, c, ada_w, ada_b, norm1_g, norm2_g, w_in, conv_dw_w, conv_dw_b, conv_gn_g, conv_gn_b,
              rwkv_mu, rwkv_w0, rwkv_w_up, rwkv_a0, rwkv_a_up, rwkv_g_up, rwkv_k_k, rwkv_k_a, rwkv_r_k,
              rwkv_ln_g, rwkv_ln_b, nsa_ck_pos, nsa_ck_w1, nsa_ck_w2, nsa_cv_pos, nsa_cv_w1, nsa_cv_w2,
              w_out, peer_wq, peer_k1, peer_k2, peer_u, peer_v, final_g):
    cs = jax.nn.silu(c)
    splits = [N_CONV_IN, N_CONV_IN + N_RWKV_IN, N_CONV_IN + N_RWKV_IN + N_Q_IN,
              N_CONV_IN + N_RWKV_IN + N_Q_IN + N_KV_IN]
    for l in range(DEPTH):
        mod = cs @ ada_w[l] + ada_b[l]
        sh1, sc1, g1, sh2, sc2, g2 = [m[:, None, :] for m in jnp.split(mod, 6, axis=-1)]
        h = _rmsnorm(x, norm1_g[l]) * (1.0 + sc1) + sh1
        p_conv, p_rwkv, p_q, p_kv, p_gate = jnp.split(h @ w_in[l], splits, axis=-1)
        o_conv = _conv_mixer(p_conv, conv_dw_w[l], conv_dw_b[l], conv_gn_g[l], conv_gn_b[l])
        o_rwkv = _rwkv_mixer(p_rwkv, rwkv_mu[l], rwkv_w0[l], rwkv_w_up[l], rwkv_a0[l], rwkv_a_up[l],
                             rwkv_g_up[l], rwkv_k_k[l], rwkv_k_a[l], rwkv_r_k[l], rwkv_ln_g[l], rwkv_ln_b[l])
        o_nsa = _nsa_mixer(p_q, p_kv, p_gate, nsa_ck_pos[l], nsa_ck_w1[l], nsa_ck_w2[l],
                           nsa_cv_pos[l], nsa_cv_w1[l], nsa_cv_w2[l])
        mix = jnp.concatenate([o_conv.astype(x.dtype), o_rwkv.astype(x.dtype), o_nsa.astype(x.dtype)], axis=-1)
        x = x + g1 * (mix @ w_out[l])
        h2 = _rmsnorm(x, norm2_g[l]) * (1.0 + sc2) + sh2
        x = x + g2 * _peer(h2, peer_wq[l], peer_k1[l], peer_k2[l], peer_u[l], peer_v[l])
    return _rmsnorm(x, final_g)


_drawn_inputs = setup_inputs


def setup_inputs(seed=0):
    import zlib

    import numpy as np

    out = dict(_drawn_inputs(seed))
    spreads = {}
    factors = {'norm1_g': 2.667,
     'conv_dw_b': 3.72,
     'conv_gn_g': 3.491,
     'conv_gn_b': 14.174,
     'rwkv_k_k': 2.858,
     'rwkv_ln_g': 3.918,
     'rwkv_ln_b': 16.541,
     'nsa_ck_pos': 6.345,
     'final_g': 8.105}
    for name, (base, spread) in spreads.items():
        noise = np.random.default_rng([zlib.crc32(name.encode()), seed]).standard_normal(out[name].shape)
        drawn = base * np.exp(spread * noise) if base else spread * noise
        out[name] = jnp.asarray(drawn.astype(out[name].dtype))
    for name, factor in factors.items():
        out[name] = (out[name] * factor).astype(out[name].dtype)
    return out
```

```python
from contextlib import ExitStack

import concourse.bass as bass
from concourse import mybir

ALU = mybir.AluOpType
ACT = mybir.ActivationFunctionType
AXX = mybir.AxisListType.X
F32 = mybir.dt.float32
BF16 = mybir.dt.bfloat16
I32 = mybir.dt.int32
U32 = mybir.dt.uint32

P = 128
HD = 64
NEG = -1e30
LOWEST = -3.0e38
RMS_EPS, CONV_EPS, RWKV_EPS = 1e-6, 1e-5, 64e-5
DECAY_RATE = 0.6065306597126334
TAPS = 31
CMP_BLOCK, CMP_STRIDE = 32, 16
TOPK, PEER_HEADS, PEER_KEYS = 16, 8, 128
GROUP = 8
RING = GROUP
NIDX = 3
NSA_HEADS = 8

ROW_MU, ROW_W0, ROW_A0, ROW_KK, ROW_KA, ROW_RK = 0, 8, 10, 12, 14, 16
ROW_LNG, ROW_LNB, ROW_CB, ROW_CGG, ROW_CGB, ROW_TAP = 18, 20, 22, 24, 26, 28
ROW_KPOS, ROW_VPOS, N_ROWS = 90, 106, 122

W_IN_ORDER = [1, 2, 0, 3, 4, 5]
BANKS_AFTER = [*range(1, 13), 14, 16, 18, 20, 23, 25, 26, 28, 30, 32, 34, 36, 38]
B_RWKV, B_CONV, B_Q, B_KV, B_CMP, B_OUT, B_PEER = 12, 16, 18, 20, 25, 26, 30


class Steps:

    def __init__(self, eng, sem):
        self.eng, self.sem, self.n = eng, sem, 0

    def did(self, ins):
        ins.then_inc(self.sem, 1)
        self.n += 1

    def wait(self):
        self.eng.wait_ge(self.sem, self.n)

    def then(self, ins):
        self.did(ins)
        self.wait()


def build_trunk(nc, a, out):
    DEPTH, D, MODS = a["ada_w"].shape
    SEQ = a["x"].shape[1]
    N_IN = a["w_in"].shape[2]
    N_EXPERTS = a["peer_u"].shape[1]
    T = SEQ // P
    KC = D // P
    N_MOD = MODS // 512
    N_C = (SEQ - CMP_BLOCK) // CMP_STRIDE + 1
    NCH = SEQ // HD
    TG = PEER_HEADS * TOPK // GROUP
    NG = T * TG

    u_rows = a["peer_u"].rearrange("l e d -> (l e) d")
    v_rows = a["peer_v"].rearrange("l e d -> (l e) d")

    with ExitStack() as ctx:
        def sb(name, cols, dt=F32):
            return ctx.enter_context(nc.sbuf_tensor(name, [P, cols], dt))

        def cut(t, at, *shape):
            n = 1
            for s in shape:
                n *= s
            v = t[:, at:at + n]
            if len(shape) == 1:
                return v
            names = "abcd"[:len(shape)]
            return v.rearrange(f"p ({' '.join(names)}) -> p {' '.join(names)}", **dict(zip(names, shape)))

        x_sb = sb("x_sb", T * D)
        mod = sb("mod", MODS)
        gain = sb("gain", D)
        tok = sb("tok", T * D)
        hT = sb("hT", KC * SEQ)
        mixT = sb("mixT", KC * SEQ)
        wring = sb("wring", 2 * KC * 512)
        scratch = sb("scratch", 16384)
        work = sb("work", 9 * 512)
        nsa = sb("nsa", 3960)
        conv = sb("conv", 2 * (SEQ + TAPS - 1) + 1024)
        ident = sb("ident", P)
        ident_b = sb("ident_b", P, BF16)
        causal_b = sb("causal_b", P, BF16)
        cmask_b = sb("cmask_b", T * 16, BF16)
        zero_b = sb("zero_b", P, BF16)
        strict = sb("strict", P, BF16)
        incl = sb("incl", P, BF16)
        levels = sb("levels", 6 * P, BF16)
        heads1 = sb("heads1", P)
        heads_mean = sb("heads_mean", P)
        restart = sb("restart", SEQ)
        iota_j = sb("iota_j", TOPK)
        any_cmp = sb("any_cmp", T)
        rows_p = sb("rows_p", P)
        cols_p = sb("cols_p", P)
        lora_wa = sb("lora_wa", 256)
        lora_g = sb("lora_g", 256)
        w2kv = sb("w2kv", 2 * HD)
        cT = sb("cT", KC)
        stat = sb("stat", 96)
        layer_base = sb("layer_base", 1)
        idx_all = sb("idx_all", NG * GROUP, I32)
        idx_cur = sb("idx_cur", NIDX * GROUP, I32)
        wexp = sb("wexp", NG * GROUP)
        hid = sb("hid", 2 * GROUP)
        gel = sb("gel", 2 * GROUP)
        act_w = sb("act_w", 2 * GROUP)
        bank = [ctx.enter_context(nc.psum_tensor(f"bank{i}", [P, 512], F32)) for i in range(8)]

        x3 = cut(x_sb, 0, T, D)
        mod6 = cut(mod, 0, 6, D)
        tok3 = cut(tok, 0, T, D)
        hT3 = cut(hT, 0, KC, SEQ)
        mix3 = cut(mixT, 0, KC, SEQ)
        wslot = [cut(wring, i * KC * 512, KC, 512) for i in range(2)]
        brow = work[0:N_MOD, 0:512]
        crow = cut(work, 512, 3, P)
        prw = cut(scratch, 0, 8, SEQ + 1)
        rw = cut(scratch, 2056, 8, SEQ)
        LT, LTm, U, TM, TT, MT, N1T, N2T = (cut(scratch, 4104 + i * 1024, 8, P) for i in range(8))
        MV = cut(scratch, 4104 + 1024, 8, HD)
        Z = cut(scratch, 12296, T, 4 * HD)
        GT = cut(scratch, 12808, 2, SEQ)
        SA = cut(scratch, 13320, T, 4 * HD)
        BBt, KBt, Vt, QAt = (cut(scratch, 13832 + i * 512, T, 4 * HD) for i in range(4))
        ST = cut(scratch, 15880, 2, P)
        u_ring = cut(scratch, 0, RING, D)
        v_ring = cut(scratch, RING * D, RING, D)
        lw, cum, pcum, pinv, aa, gg, kk, tmp, keff = (cut(work, i * 512, 2, SEQ) for i in range(9))
        qa, qr, kb, bb, bonus, dev = lw, pcum, pinv, aa, cum, kk
        r_, k_, v_ = rw[:, 0:2, :], rw[:, 2:4, :], rw[:, 4:6, :]
        pend = cut(stat, 32, 2, NCH)
        UP = SEQ + TAPS - 1
        upad = cut(conv, 0, 2, UP)
        cval = cut(conv, 2 * UP, 2, SEQ)
        csig = cut(conv, 2 * UP + 512, 2, SEQ)
        qT = cut(nsa, 0, 4, SEQ)
        kselT = cut(nsa, 1024, 2, SEQ)
        kwinT = cut(nsa, 1536, 2, SEQ)
        vtok = cut(nsa, 2048, T, 2 * P)
        kcT = cut(nsa, 2560, 2, N_C)
        vc = cut(nsa, 2592, 2, HD)
        gates = cut(nsa, 2720, T, 24)
        hidk = cut(nsa, 2768, 2, 16)[:, :, 0:N_C]
        hidv = cut(nsa, 2800, 2, 32)
        sigc = cut(nsa, 2864, 2, 32)
        pc = cut(nsa, 2928, T, 2, 4, 32)
        pcT = cut(nsa, 3440, T, 2, P)
        zk = cut(mixT, 4 * SEQ, 3, P)
        zv = cut(mixT, 4 * SEQ + 3 * P, 3, P)
        prob = [cut(tok, i * 512, 512) for i in range(2)]
        probT = [cut(tok, 1024 + i * 512, 512) for i in range(2)]
        topv = cut(work, 0, T, 2, PEER_HEADS, TOPK)
        topi = cut(work, 512, T, 2, PEER_HEADS, TOPK).bitcast(U32)
        topf = cut(work, 1024, T, 2, PEER_HEADS, TOPK)
        best = cut(work, 1536, T, PEER_HEADS, TOPK)
        besti = cut(work, 1792, T, PEER_HEADS, TOPK).bitcast(U32)
        quot = cut(work, 2048, T, PEER_HEADS, TOPK)
        rem = cut(work, 2304, T, PEER_HEADS, TOPK)
        quot_i, rem_i = quot.bitcast(I32), rem.bitcast(I32)
        e1 = cut(work, 2560, T, PEER_HEADS, TOPK)
        e2 = cut(work, 2816, T, PEER_HEADS, TOPK)
        left = cut(work, 3072, 4, P)
        left2 = cut(work, 3584, 2, 256)
        cand = cut(mixT, 0, PEER_HEADS, TOPK, TOPK)
        onehot = cut(scratch, 0, PEER_HEADS, TOPK, TOPK)
        peer_k = cut(conv, 0, 2, P)
        peer_kT = cut(conv, 256, 2, P)
        peer_q = [cut(nsa, i * 512, 2, SEQ) for i in range(2)]
        diag = [cut(nsa, 1024 + i * P, P) for i in range(2)]
        yg = cut(conv, 512, D)

        def sem(name):
            return ctx.enter_context(nc.semaphore(name))

        u_landed = [sem(f"u_landed{i}") for i in range(RING)]
        v_landed = [sem(f"v_landed{i}") for i in range(RING)]
        x_in, c_in, consts, c_done, pe_setup, act_setup, dve_setup = map(sem, (
            "x_in", "c_in", "consts", "c_done", "pe_setup", "act_setup", "dve_setup"))
        final_in, final_ssq, final_root, out_ready, out_done, dve_final = map(sem, (
            "final_in", "final_ssq", "final_root", "out_ready", "out_done", "dve_final"))
        layer_sems = []

        def lsem(name):
            layer_sems.append(sem(name))
            return layer_sems[-1]

        params_in, gain_in, peer_k_in = lsem("params_in"), lsem("gain_in"), lsem("peer_k_in")
        w_landed = [lsem(f"w_landed{i}") for i in range(2)]
        streamed, copied = lsem("streamed"), lsem("copied")
        dve_steps, act_steps, pool_steps = lsem("dve_steps"), lsem("act_steps"), lsem("pool_steps")
        zeros_set, cols_psum, cols_ready, gain_used = map(lsem, ("zeros_set", "cols_psum", "cols_ready", "gain_used"))
        ssq_ready, rms_ready, root_ready, h_ready = map(lsem, ("ssq_ready", "rms_ready", "root_ready", "h_ready"))
        hT_psum, hT_act, hT_dve = map(lsem, ("hT_psum", "hT_act", "hT_dve"))
        lora_in, lora_act, lora_psum, lora_out = map(lsem, ("lora_in", "lora_act", "lora_psum", "lora_out"))
        kk_sq, kk_sum, kk_inv, kk_root = map(lsem, ("kk_sq", "kk_sum", "kk_inv", "kk_root"))
        cum_ready, decays, bonus_in, bonus_psum, bonus_out = map(lsem, (
            "cum_ready", "decays", "bonus_in", "bonus_psum", "bonus_out"))
        chan_ready, tokm_psum, tokm_ready = map(lsem, ("chan_ready", "tokm_psum", "tokm_ready"))
        pair_psum, pair_masked = map(lsem, ("pair_psum", "pair_masked"))
        lt_level, u_psum, u_ready, inv_psum, inv_ready = map(lsem, (
            "lt_level", "u_psum", "u_ready", "inv_psum", "inv_ready"))
        mv_psum, mv_ready, gt_psum, gt_ready, z_psum, z_ready = map(lsem, (
            "mv_psum", "mv_ready", "gt_psum", "gt_ready", "z_psum", "z_ready"))
        sa_psum, sa_ready, st_psum, st_ready, y_psum, y_copied = map(lsem, (
            "sa_psum", "sa_ready", "st_psum", "st_ready", "y_psum", "y_copied"))
        conv_ready, gn_in, gn_psum, gn_inv, gn_root, gn_out, gn_sig = map(lsem, (
            "conv_ready", "gn_in", "gn_psum", "gn_inv", "gn_root", "gn_out", "gn_sig"))
        cmp_sig, cmp_hid, cmp_psum2, cmp_kv = map(lsem, ("cmp_sig", "cmp_hid", "cmp_psum2", "cmp_kv"))
        cmp_scores, cmp_sub, cmp_exp, cmp_prob, cmp_pT, cmp_pTr = map(lsem, (
            "cmp_scores", "cmp_sub", "cmp_exp", "cmp_prob", "cmp_pT", "cmp_pTr"))
        scored, maxed, exped, scaled, turned, pT_ready, attended, o_copied = map(lsem, (
            "scored", "maxed", "exped", "scaled", "turned", "pT_ready", "attended", "o_copied"))
        mix_ready, x_added = lsem("mix_ready"), lsem("x_added")
        kT_psum, kT_ready, q_ready, keys_scored, picked = map(lsem, (
            "kT_psum", "kT_ready", "q_ready", "keys_scored", "picked"))
        wexp_in, wexp_exp, choice_ready = map(lsem, ("wexp_in", "wexp_exp", "choice_ready"))
        idx_ready, u_used, v_used, gel_ready, act_ready, diag_ready, y_ready, y_used, h2cur_ready = map(lsem, (
            "idx_ready", "u_used", "v_used", "gel_ready", "act_ready", "diag_ready", "y_ready", "y_used",
            "h2cur_ready"))
        turns = {e: lsem(f"turns_{e}") for e in ("pool", "dve")}

        def chunk_wait(eng, i):
            eng.wait_ge(w_landed[i % 2], 32 * (i // 2 + 1))

        def gate(eng, name, s, value):
            eng.wait_ge(s, value)
            eng.sem_inc(turns[name], 1)

        UNITS = T * NSA_HEADS

        with nc.Block() as block:
            @block.sync
            def _(sp):
                sp.dma_start(crow[0:KC, 0, :], a["c"].rearrange("a (k p) -> (a k) p", p=P)).then_inc(c_in, 16)
                sp.dma_start(x3, a["x"].rearrange("a (t p) d -> p (a t) d", p=P)).then_inc(x_in, 16)

            @block.gpsimd
            def _(pool):
                s = Steps(pool, consts)

                def select(view, op, fill, base, pattern, cm):
                    s.then(pool.affine_select(out=view, in_=view, compare_op=op, fill=fill, base=base,
                                              pattern=pattern, channel_multiplier=cm))

                for t_, v in ((ident, 0.0), (ident_b, 0.0), (causal_b, 0.0), (cmask_b, 0.0), (zero_b, 0.0),
                              (strict, 1.0), (incl, 1.0), (levels, 0.0), (heads1, 1.0), (heads_mean, 1.0 / HD),
                              (restart, 1.0), (any_cmp, 1.0), (layer_base, 0.0)):
                    s.did(pool.memset(t_[:, :], v))
                lv = levels[:, :].rearrange("p (l t) -> p l t", l=6)
                halves = []
                for i in range(6):
                    b = 1 << i
                    halves.append(lv[:, i, :].rearrange("p (n h b) -> p n h b", h=2, b=b)[:, :, 1, :])
                s.wait()
                s.did(pool.memset(restart[:, :].rearrange("p (c t) -> p c t", t=HD)[:, :, 0:1], 0.0))
                for h_ in halves:
                    s.did(pool.memset(h_, 1.0))
                s.then(pool.iota(iota_j[:, :], pattern=[[1, TOPK]], base=0, channel_multiplier=0,
                                 allow_small_or_imprecise_dtypes=True))
                for m in (ident, ident_b):
                    select(m[:, :], ALU.not_equal, 1.0, 0, [[-1, P]], 1)
                select(causal_b[:, :], ALU.is_ge, NEG, 0, [[-1, P]], 1)
                cm3 = cmask_b[:, :].rearrange("p (t n) -> p t n", t=T)
                select(cm3, ALU.is_ge, NEG, -(CMP_BLOCK - 1), [[P, T], [-CMP_STRIDE, 16]], 1)
                s.then(pool.memset(cm3[:, :, N_C:16], NEG))
                select(any_cmp[:, :], ALU.is_ge, 0.0, -(CMP_BLOCK - 1), [[P, T]], 1)
                for m, base in ((strict, -1), (incl, 0)):
                    v = m[:, :].rearrange("p (c t) -> p c t", c=2)
                    select(v, ALU.is_ge, 0.0, base, [[HD, 2], [1, HD]], -1)
                    select(v, ALU.is_ge, 0.0, 0, [[-HD, 2], [0, HD]], 1)
                for m in (heads1, heads_mean):
                    v = m[:, :].rearrange("p (c t) -> p c t", c=2)
                    select(v, ALU.is_ge, 0.0, 0, [[-HD, 2], [0, HD]], 1)
                    select(v, ALU.is_ge, 0.0, HD - 1, [[HD, 2], [0, HD]], -1)
                for i, h_ in enumerate(halves):
                    b = 1 << i
                    n = P // (2 * b)
                    select(h_, ALU.is_ge, 0.0, 0, [[-2 * b, n], [0, b]], 1)
                    select(h_, ALU.is_ge, 0.0, b - 1, [[2 * b, n], [0, b]], -1)
                pool.sem_inc(pe_setup, 1)

            @block.scalar
            def _(act):
                act.wait_ge(c_in, 16)
                act.activation(crow[0:KC, 1, :], crow[0:KC, 0, :], ACT.Sigmoid).then_inc(act_setup, 1)

            @block.vector
            def _(dve):
                dve.wait_ge(act_setup, 1)
                dve.tensor_tensor(crow[0:KC, 2, :], crow[0:KC, 0, :], crow[0:KC, 1, :], ALU.mult)\
                   .then_inc(dve_setup, 1)
                dve.wait_ge(c_done, 1)
                dve.tensor_copy(cT[:, :], bank[0][:, 0:KC]).then_inc(dve_setup, 1)
                dve.wait_ge(dve_setup, 2)
                dve.wait_ge(x_in, 16)

            @block.tensor
            def _(pe):
                pe.wait_ge(pe_setup, 1)
                pe.wait_ge(dve_setup, 1)
                pe.transpose(bank[0][:, 0:KC], crow[0:KC, 2, :], ident[0:KC, 0:KC]).then_inc(c_done, 1)

        nc.all_engine_barrier()

        with nc.Fori(0, DEPTH) as l:
            with nc.Block() as block:
                L = bass.ds(l, 1)

                def vec(name, p=P):
                    return a[name][L].rearrange("l (r p) -> (l r) p", p=p)

                @block.sync
                def _(sp):
                    def param(to, of):
                        sp.dma_start(to, of).then_inc(params_in, 16)

                    param(brow, vec("ada_b", 512))
                    for name, row, n in (("rwkv_mu", ROW_MU, 8), ("rwkv_w0", ROW_W0, 2), ("rwkv_a0", ROW_A0, 2),
                                         ("rwkv_k_k", ROW_KK, 2), ("rwkv_k_a", ROW_KA, 2),
                                         ("rwkv_ln_g", ROW_LNG, 2), ("rwkv_ln_b", ROW_LNB, 2),
                                         ("conv_dw_b", ROW_CB, 2), ("conv_gn_g", ROW_CGG, 2),
                                         ("conv_gn_b", ROW_CGB, 2)):
                        param(rows_p[row:row + n, :], vec(name))
                    param(rows_p[ROW_RK:ROW_RK + 2, :],
                          a["rwkv_r_k"][L].rearrange("l (r h) d -> (l r) (h d)", r=2))
                    for i in range(2):
                        param(rows_p[ROW_TAP + i * TAPS:ROW_TAP + (i + 1) * TAPS, :],
                              a["conv_dw_w"][L, :, 0, i * P:(i + 1) * P].rearrange("l w c -> (l w) c"))
                    for name, row in (("nsa_ck_pos", ROW_KPOS), ("nsa_cv_pos", ROW_VPOS)):
                        param(rows_p[row:row + 16, :],
                              a[name][L].rearrange("l (n e) d -> (l n) (e d)", e=2))
                    param(lora_wa[0:HD, :], a["rwkv_w_up"][L].rearrange("l k n -> (l k) n"))
                    param(lora_wa[HD:P, :], a["rwkv_a_up"][L].rearrange("l k n -> (l k) n"))
                    param(lora_g[:, :], a["rwkv_g_up"][L].rearrange("l k n -> (l k) n"))
                    for i, name in enumerate(("nsa_ck_w2", "nsa_cv_w2")):
                        param(w2kv[:, i * HD:(i + 1) * HD], a[name][L].rearrange("l k n -> (l k) n"))
                    sp.dma_start(gain[:, :], a["norm1_g"][L].to_broadcast([P, D])).then_inc(gain_in, 16)

                    def load_chunk(i):
                        if i >= 2:
                            sp.wait_ge(streamed, BANKS_AFTER[i - 2])
                        for half in range(2):
                            ks = slice(half * KC // 2, (half + 1) * KC // 2)
                            if i < N_MOD:
                                cols, table = slice(i * 512, (i + 1) * 512), "ada_w"
                            elif i < N_MOD + 6:
                                c0 = W_IN_ORDER[i - N_MOD] * 512
                                cols, table = slice(c0, min(c0 + 512, N_IN)), "w_in"
                            elif i == N_MOD + 6:
                                of = a[("nsa_ck_w1", "nsa_cv_w1")[half]][L]\
                                    .rearrange("l (n p) j -> p (l n) j", p=P)
                                to = wslot[i % 2][:, ks, :].rearrange("p k (m j) -> p (k m) j", j=P)
                                sp.dma_start(to, of, max_dma_last_dim=4 * P).then_inc(w_landed[i % 2], 16)
                                continue
                            elif i < N_MOD + 9:
                                j = i - N_MOD - 7
                                cols, table = slice(j * 512, (j + 1) * 512), "w_out"
                            else:
                                j = i - N_MOD - 9
                                cols, table = slice(j * 512, (j + 1) * 512), "peer_wq"
                            of = a[table][L, :, cols].rearrange("l (k p) n -> p (l k) n", p=P)[:, ks, :]
                            to = wslot[i % 2][:, ks, 0:cols.stop - cols.start]
                            sp.dma_start(to, of).then_inc(w_landed[i % 2], 16)

                    for i in range(len(BANKS_AFTER)):
                        load_chunk(i)
                        if i == N_MOD + 6:
                            sp.wait_ge(gain_used, 1)
                            sp.dma_start(gain[:, :], a["norm2_g"][L].to_broadcast([P, D])).then_inc(gain_in, 16)
                        if i == N_MOD + 8:
                            sp.wait_ge(streamed, B_OUT + 1)
                            for j, name in enumerate(("peer_k1", "peer_k2")):
                                sp.dma_start(peer_k[:, j, :], a[name][L].rearrange("l n d -> (l n) d"))\
                                  .then_inc(peer_k_in, 16)

                @block.gpsimd
                def _(pool):
                    for v in (prw[:, :, 0:1], upad[:, :, 0:TAPS - 1], hidv, pc, zk[:, 2, :], zv[:, 2, :], ST):
                        pool.memset(v, 0.0).then_inc(zeros_set, 1)
                    s = Steps(pool, pool_steps)
                    pool.wait_ge(cols_ready, 1)
                    pool.wait_ge(zeros_set, 7)
                    pool.wait_ge(copied, B_CONV + 2)
                    s.then(pool.tensor_tensor(upad[:, :, TAPS - 1:UP], cval, csig, ALU.mult))
                    both = [P, 2, SEQ]
                    s.then(pool.tensor_copy(cval, cols_p[:, ROW_CB:ROW_CB + 2].unsqueeze(2).to_broadcast(both)))
                    for j in range(TAPS):
                        w = cols_p[:, ROW_TAP + j:ROW_TAP + TAPS + j + 1:TAPS].unsqueeze(2).to_broadcast(both)
                        s.then(pool.tensor_tensor(csig, upad[:, :, j:j + SEQ], w, ALU.mult))
                        s.then(pool.tensor_tensor(cval, cval, csig, ALU.add))
                    pool.sem_inc(conv_ready, 1)

                    def gather(table, ring, landed, used, b, k, n):
                        gate(pool, "pool", used, n + 1)
                        at = idx_cur[:, b * GROUP + k:b * GROUP + k + 1]
                        pool.indirect_dma_start(ring[:, k, :], None, table,
                                                bass.IndirectOffsetOnAxis(ap=at, axis=0)).then_inc(landed[k], 16)

                    def fetch_indices(b, g):
                        pool.tensor_copy(idx_cur[:, b * GROUP:(b + 1) * GROUP],
                                         idx_all[:, bass.ds(g * GROUP, GROUP)]).then_inc(idx_ready, 1)
                        gate(pool, "pool", idx_ready, g + 1)

                    pool.wait_ge(choice_ready, 1)
                    for g in range(2):
                        fetch_indices(g, g)
                        for k in range(GROUP):
                            gather(u_rows, u_ring, u_landed, u_used, g, k, g * GROUP + k)
                            if g:
                                gather(v_rows, v_ring, v_landed, v_used, 0, k, k)
                    with pool.Fori(0, (NG - 2) // NIDX) as i:
                        for m in range(NIDX):
                            g = NIDX * i + (2 + m)
                            b = (2 + m) % NIDX
                            gate(pool, "pool", v_used, GROUP * (g - NIDX + 1) + RING)
                            fetch_indices(b, g)
                            for k in range(GROUP):
                                gather(u_rows, u_ring, u_landed, u_used, b, k, GROUP * g + k)
                                gather(v_rows, v_ring, v_landed, v_used, (b + NIDX - 1) % NIDX, k,
                                       GROUP * (g - 1) + k)
                    for k in range(GROUP):
                        gather(v_rows, v_ring, v_landed, v_used, (NG - 1) % NIDX, k, GROUP * (NG - 1) + k)

                @block.scalar
                def _(act):
                    s = Steps(act, act_steps)

                    def squares(i):
                        for t in range(T):
                            act.activation(tok3[:, t, :], x3[:, t, :], ACT.Square,
                                           accum_out=stat[:, t:t + 1]).then_inc(ssq_ready, 1)

                    def root(i):
                        act.wait_ge(rms_ready, i + 1)
                        act.activation(stat[:, 6:6 + T], stat[:, 4:4 + T], ACT.Sqrt).then_inc(root_ready, 1)

                    def hT_copies(i):
                        for b in (0, 1):
                            act.wait_ge(hT_psum, 4 * i + b + 1)
                            act.activation(hT3[:, 2 * b:2 * b + 2, :],
                                           bank[4 + b][:, :].rearrange("p (k s) -> p k s", k=2), ACT.Copy)\
                               .then_inc(hT_act, 1)

                    def halves(n):
                        return bank[n % 4][:, :].rearrange("p (i s) -> p i s", i=2)

                    squares(0)
                    root(0)
                    for n in range(N_MOD):
                        act.wait_ge(streamed, n + 1)
                        act.activation(mod[:, n * 512:(n + 1) * 512], bank[n % 4][:, :], ACT.Copy)\
                           .then_inc(copied, 1)
                    hT_copies(0)
                    for n in range(B_RWKV, B_CMP):
                        act.wait_ge(streamed, n + 1)
                        h_ = halves(n)
                        if n == B_RWKV:
                            act.wait_ge(zeros_set, 7)
                        if n < B_CONV:
                            i = 2 * (n - B_RWKV)
                            last = act.activation(prw[:, i:i + 2, 1:SEQ + 1], h_, ACT.Copy)
                        elif n == B_CONV:
                            last = act.activation(cval, h_, ACT.Copy)
                        elif n == B_CONV + 1:
                            last = act.activation(csig, h_, ACT.Sigmoid)
                        elif n < B_KV:
                            i = 2 * (n - B_Q)
                            last = act.activation(qT[:, i:i + 2, :], h_, ACT.Copy, scale=float(HD) ** -0.5)
                        elif n == B_KV:
                            for z, i in ((zk, 0), (zv, 1)):
                                for g in range(2):
                                    for odd in range(2):
                                        of = h_[g * HD:(g + 1) * HD, i, :].rearrange("p (n e) -> p n e", e=2)
                                        last = act.activation(z[odd * HD:(odd + 1) * HD, g, :], of[:, :, odd],
                                                              ACT.Copy)
                                        if i * 4 + g * 2 + odd < 7:
                                            s.did(last)
                        elif n in (B_KV + 1, B_KV + 3):
                            keys = kselT if n == B_KV + 1 else kwinT
                            for g in range(2):
                                for half in range(2):
                                    last = act.activation(keys[half * HD:(half + 1) * HD, g, :],
                                                          h_[g * HD:(g + 1) * HD, 0, :], ACT.Copy)
                                    if g * 2 + half < 3:
                                        s.did(last)
                        elif n == B_KV + 2:
                            last = act.activation(vtok[:, :, 0:P], bank[n % 4][:, 0:T * P]
                                                  .rearrange("p (t c) -> p t c", t=T), ACT.Copy)
                        else:
                            v = bank[n % 4][:, 0:T * (P + 24)].rearrange("p (t c) -> p t c", t=T)
                            s.did(act.activation(vtok[:, :, P:2 * P], v[:, :, 0:P], ACT.Copy))
                            last = act.activation(gates, v[:, :, P:P + 24], ACT.Sigmoid)
                        last.then_inc(copied, 1)

                    act.wait_ge(lora_in, 2)
                    act.activation(rw[0:HD, 6, :], rw[0:HD, 6, :], ACT.Tanh).then_inc(lora_act, 1)
                    act.activation(rw[:, 7, :], rw[:, 7, :], ACT.Sigmoid).then_inc(lora_act, 1)
                    act.wait_ge(streamed, B_CMP + 1)
                    act.wait_ge(cmp_hid, 1)
                    act.activation(sigc, sigc, ACT.Sigmoid).then_inc(cmp_sig, 1)
                    act.wait_ge(lora_psum, 3)
                    for i in range(2):
                        act.activation(lw[:, i, :], bank[4][:, i * SEQ:(i + 1) * SEQ], ACT.Sigmoid,
                                       bias=cols_p[:, ROW_W0 + i:ROW_W0 + i + 1]).then_inc(lora_out, 1)
                    for i in range(2):
                        act.activation(aa[:, i, :], bank[5][:, i * SEQ:(i + 1) * SEQ], ACT.Sigmoid,
                                       bias=cols_p[:, ROW_A0 + i:ROW_A0 + i + 1]).then_inc(lora_out, 1)
                    act.activation(gg, bank[6][:, :].rearrange("p (i s) -> p i s", i=2), ACT.Copy)\
                       .then_inc(lora_out, 1)
                    act.wait_ge(cmp_psum2, 1)
                    s.did(act.activation(kcT, bank[0][:, 0:2 * N_C].rearrange("p (g n) -> p g n", g=2), ACT.Copy))
                    act.activation(vc, bank[1][:, 0:2 * HD].rearrange("p (g d) -> p g d", g=2), ACT.Copy)\
                       .then_inc(cmp_kv, 1)
                    act.wait_ge(kk_inv, 1)
                    act.activation(tmp, tmp, ACT.Sqrt).then_inc(kk_root, 1)
                    act.wait_ge(cum_ready, 1)
                    act.activation(pcum, cum, ACT.Exp).then_inc(decays, 1)
                    act.activation(pinv, cum, ACT.Exp, scale=-1.0).then_inc(decays, 1)
                    act.activation(lw, lw, ACT.Exp).then_inc(decays, 1)
                    for i, to in enumerate((BBt, KBt, Vt, QAt)):
                        act.wait_ge(tokm_psum, i + 1)
                        act.activation(to, bank[(5, 6, 7, 5)[i]][:, :].rearrange("p (t c) -> p t c", t=T), ACT.Copy)\
                           .then_inc(tokm_ready, 1)
                    act.wait_ge(cmp_sub, 1)
                    act.activation(pc[:, :, :, :, 0:16].rearrange("p t i j n -> p (t i j) n"),
                                   pc[:, :, :, :, 0:16].rearrange("p t i j n -> p (t i j) n"), ACT.Exp)\
                       .then_inc(cmp_exp, 1)
                    act.wait_ge(cmp_pT, 1)
                    act.activation(pcT, bank[2][:, :].rearrange("p (t i q) -> p t i q", t=T, i=2), ACT.Copy)\
                       .then_inc(cmp_pTr, 1)

                    def u_copy(lev):
                        for i in range(2):
                            act.wait_ge(u_psum, 2 * lev + i + 1)
                            act.activation(U[:, 4 * i:4 * i + 4, :],
                                           bank[4 + i][:, :].rearrange("p (u t) -> p u t", u=4), ACT.Copy)\
                               .then_inc(u_ready, 1)

                    def attend(k):
                        if k < UNITS:
                            t, h, n = k // NSA_HEADS, k % NSA_HEADS, (k // NSA_HEADS + 1) * P
                            act.wait_ge(maxed, k + 1)
                            if k >= 2:
                                act.wait_ge(turned, k - 1)
                            for b in range(2):
                                ins = act.activation(prob[k % 2][:, b * n:(b + 1) * n],
                                                     bank[k % 2][:, b * n:(b + 1) * n], ACT.Exp,
                                                     bias=stat[:, 48 + 2 * (k % 2) + b:49 + 2 * (k % 2) + b],
                                                     accum_out=stat[:, 52 + 2 * (k % 2) + b:53 + 2 * (k % 2) + b])
                                ins.then_inc(exped, 1)
                        if 1 <= k <= UNITS:
                            j = k - 1
                            n = 2 * (j // NSA_HEADS + 1) * P
                            act.wait_ge(turned, j + 1)
                            if j >= 2:
                                act.wait_ge(attended, j - 1)
                            act.activation(probT[j % 2][:, 0:n], bank[2][:, 0:n], ACT.Copy).then_inc(pT_ready, 1)
                        if k >= 2 and (k - 2) % NSA_HEADS == NSA_HEADS - 1:
                            t = (k - 2) // NSA_HEADS
                            act.wait_ge(attended, k - 1)
                            act.activation(mix3[:, 4:8, t * P:(t + 1) * P],
                                           bank[3][:, :].rearrange("p (j q) -> p j q", j=4), ACT.Copy)\
                               .then_inc(o_copied, 1)

                    for part, i in SCHEDULE:
                        if part == "level" and i:
                            u_copy(i)
                        elif part == "attend":
                            attend(i)
                        elif part == "solve":
                            act.wait_ge(mv_psum, 1)
                            act.activation(MV, bank[4][:, :].rearrange("p (u d) -> p u d", u=8), ACT.Copy)\
                               .then_inc(mv_ready, 1)
                            act.wait_ge(gt_psum, 1)
                            act.activation(GT, bank[5][:, :].rearrange("p (i s) -> p i s", i=2), ACT.Copy)\
                               .then_inc(gt_ready, 1)
                            act.wait_ge(z_psum, 1)
                            act.activation(Z, bank[6][:, :].rearrange("p (t c) -> p t c", t=T), ACT.Copy)\
                               .then_inc(z_ready, 1)
                    act.wait_ge(y_psum, 1)
                    act.activation(tmp, bank[7][:, :].rearrange("p (i s) -> p i s", i=2), ACT.Copy)\
                       .then_inc(y_copied, 1)
                    for i, v in ((0, csig), (1, keff)):
                        act.wait_ge(gn_inv, i + 1)
                        act.activation(v, v, ACT.Sqrt).then_inc(gn_root, 1)
                    act.wait_ge(gn_out, 1)
                    act.activation(csig, upad[:, :, 0:SEQ], ACT.Sigmoid).then_inc(gn_sig, 1)
                    act.wait_ge(x_added, 4)
                    squares(1)
                    root(1)
                    hT_copies(1)
                    act.wait_ge(kT_psum, 1)
                    act.activation(peer_kT, bank[3][:, 0:2 * P].rearrange("p (i n) -> p i n", i=2), ACT.Copy)\
                       .then_inc(kT_ready, 1)
                    for h in range(PEER_HEADS):
                        act.wait_ge(streamed, B_PEER + h + 1)
                        if h >= 2:
                            act.wait_ge(keys_scored, h - 1)
                        act.activation(peer_q[h % 2], bank[4 + h % 2][:, :].rearrange("p (i s) -> p i s", i=2),
                                       ACT.Copy).then_inc(q_ready, 1)
                    act.wait_ge(wexp_in, 1)
                    act.activation(wexp[:, :], wexp[:, :], ACT.Exp).then_inc(wexp_exp, 1)
                    with act.Fori(0, NG // 2) as i:
                        for b in range(2):
                            g = 2 * i + b
                            act.wait_ge(u_used, GROUP * (g + 1) + RING)
                            act.activation(gel[:, b * GROUP:(b + 1) * GROUP], hid[:, b * GROUP:(b + 1) * GROUP],
                                           ACT.Gelu).then_inc(gel_ready, 1)
                            act.wait_ge(act_ready, g + 1)
                            for k in range(GROUP):
                                act.wait_ge(v_used, GROUP * g + k + RING - 1)
                                act.activation(diag[k % 2], ident[:, :], ACT.Copy,
                                               scale=act_w[:, b * GROUP + k:b * GROUP + k + 1])\
                                   .then_inc(diag_ready, 1)

                @block.vector
                def _(dve):
                    s = Steps(dve, dve_steps)
                    tt, ts, stt = dve.tensor_tensor, dve.tensor_scalar, dve.scalar_tensor_tensor

                    def col(row):
                        return cols_p[:, row:row + 1]

                    def norm(i):
                        dve.wait_ge(ssq_ready, T * (i + 1))
                        s.then(ts(stat[:, 2:2 + T], stat[:, 0:T], 1.0 / D, RMS_EPS, ALU.mult, ALU.add))
                        dve.reciprocal(stat[:, 4:4 + T], stat[:, 2:2 + T]).then_inc(rms_ready, 1)
                        dve.wait_ge(gain_in, 16 * (i + 1))
                        dve.wait_ge(copied, 4 if i == 0 else N_MOD)
                        stt(out=mod6[:, 3 * i + 1, :], in0=mod6[:, 3 * i + 1, :], scalar=1.0, in1=gain[:, :],
                            op0=ALU.add, op1=ALU.mult).then_inc(gain_used, 1)
                        dve.wait_ge(gain_used, i + 1)
                        dve.wait_ge(root_ready, i + 1)
                        for t in range(T):
                            s.did(stt(out=tok3[:, t, :], in0=x3[:, t, :], scalar=stat[:, 6 + t:7 + t],
                                      in1=mod6[:, 3 * i + 1, :], op0=ALU.mult, op1=ALU.mult))
                        for t in range(T):
                            dve.wait_ge(dve_steps, s.n - T + t + 1)
                            tt(tok3[:, t, :], tok3[:, t, :], mod6[:, 3 * i, :], ALU.add).then_inc(h_ready, 1)
                        for b in (2, 3):
                            dve.wait_ge(hT_psum, 4 * i + b + 1)
                            dve.tensor_copy(hT3[:, 2 * b:2 * b + 2, :],
                                            bank[4 + b][:, :].rearrange("p (k s) -> p k s", k=2)).then_inc(hT_dve, 1)

                    norm(0)
                    dve.wait_ge(cols_psum, 1)
                    dve.tensor_copy(cols_p[:, 0:N_ROWS], bank[4][:, 0:N_ROWS]).then_inc(cols_ready, 1)
                    dve.wait_ge(cols_ready, 1)
                    s.did(ts(stat[:, 10:12], cols_p[:, ROW_KA:ROW_KA + 2], -1.0, 1.0, ALU.mult, ALU.add))
                    dve.wait_ge(zeros_set, 7)
                    s.did(dve.tensor_copy(zk[:, 2, 0:16], cols_p[:, ROW_KPOS:ROW_KPOS + 16]))
                    dve.tensor_copy(zv[:, 2, 0:16], cols_p[:, ROW_VPOS:ROW_VPOS + 16]).then_inc(cols_ready, 1)

                    dve.wait_ge(copied, B_RWKV + 4)
                    for part in (slice(6, 8), slice(0, 6)):
                        s.did(tt(rw[:, part, :], prw[:, part, 0:SEQ], prw[:, part, 1:SEQ + 1], ALU.subtract))
                    dve.wait_ge(dve_steps, s.n - 1)
                    for i in (6, 7):
                        stt(out=rw[:, i, :], in0=rw[:, i, :], scalar=col(ROW_MU + i), in1=prw[:, i, 1:SEQ + 1],
                            op0=ALU.mult, op1=ALU.add).then_inc(lora_in, 1)
                    s.wait()
                    for i in range(6):
                        s.did(stt(out=rw[:, i, :], in0=rw[:, i, :], scalar=col(ROW_MU + i),
                                  in1=prw[:, i, 1:SEQ + 1], op0=ALU.mult, op1=ALU.add))
                    s.wait()
                    for i in range(2):
                        s.did(ts(kk[:, i, :], k_[:, i, :], col(ROW_KK + i), None, ALU.mult))
                    s.wait()
                    tt(tmp, kk, kk, ALU.mult).then_inc(kk_sq, 1)
                    dve.wait_ge(streamed, B_CMP + 1)
                    hb = bank[B_CMP % 4]
                    s.then(dve.tensor_copy(stat[:, 12:14], hb[:, 0:90].rearrange("p (z g) -> p z g", z=2)[:, :, 30]))
                    for i, v in enumerate((hidk, hidv[:, :, 0:N_C])):
                        s.did(ts(v, hb[:, 45 * i:45 * i + 30].rearrange("p (g n) -> p g n", g=2),
                                 stat[:, 12 + i:13 + i], None, ALU.add))
                    s.wait()
                    sk = sigc.rearrange("p i (g n) -> p i g n", g=2)[:, :, :, 0:N_C]
                    s.did(dve.memset(sigc, 0.0))
                    s.wait()
                    s.did(dve.tensor_copy(sk[:, 0], hidk))
                    dve.tensor_copy(sk[:, 1], hidv[:, :, 0:N_C]).then_inc(cmp_hid, 1)
                    dve.wait_ge(cmp_sig, 1)
                    s.did(tt(hidk, hidk, sk[:, 0], ALU.mult))
                    tt(hidv[:, :, 0:N_C], hidv[:, :, 0:N_C], sk[:, 1], ALU.mult).then_inc(cmp_hid, 1)
                    dve.wait_ge(lora_out, 2)
                    s.then(ts(lw, lw, -DECAY_RATE, None, ALU.mult))
                    for i in range(2):
                        s.did(dve.tensor_tensor_scan(out=cum[:, i, :], data0=restart[:, :], data1=lw[:, i, :],
                                                     initial=0.0, op0=ALU.mult, op1=ALU.add))
                    s.wait()
                    tt(lw, cum, lw, ALU.subtract).then_inc(cum_ready, 1)
                    dve.wait_ge(kk_sum, 1)
                    s.then(ts(tmp, bank[7][:, :].rearrange("p (i s) -> p i s", i=2), 1e-24, None, ALU.max))
                    dve.reciprocal(tmp, tmp).then_inc(kk_inv, 1)
                    dve.wait_ge(lora_out, 5)
                    for i in range(2):
                        s.did(ts(keff[:, i, :], aa[:, i, :], col(ROW_KA + i), stat[:, 10 + i:11 + i],
                                 ALU.mult, ALU.add))
                    s.wait()
                    s.then(tt(keff, keff, k_, ALU.mult))
                    dve.wait_ge(kk_root, 1)
                    s.then(tt(kk, kk, tmp, ALU.mult))
                    s.did(tt(bb, aa, kk, ALU.mult))
                    dve.wait_ge(decays, 3)
                    for i in range(2):
                        stt(out=bonus[:, i, :], in0=r_[:, i, :], scalar=col(ROW_RK + i), in1=keff[:, i, :],
                            op0=ALU.mult, op1=ALU.mult).then_inc(bonus_in, 1)
                    s.did(dve.tensor_copy(pend, pcum.rearrange("p i (c t) -> p i c t", t=HD)[:, :, :, HD - 1]))
                    s.wait()
                    tt(bb, bb, pinv, ALU.mult).then_inc(chan_ready, 1)
                    dve.wait_ge(chan_ready, 1)
                    tt(kb, keff, pinv, ALU.mult).then_inc(chan_ready, 1)
                    stt(out=qa, in0=lw, scalar=-1.0, in1=kk, op0=ALU.mult, op1=ALU.mult).then_inc(chan_ready, 1)
                    tt(qr, pcum, r_, ALU.mult).then_inc(chan_ready, 1)
                    dve.wait_ge(bonus_psum, 1)
                    tt(bonus, bank[4][:, :].rearrange("p (i s) -> p i s", i=2), v_, ALU.mult).then_inc(bonus_out, 1)

                    dve.wait_ge(cmp_scores, 2)
                    cs = [bank[2 + i][:, 0:T * 64].rearrange("p (t j n) -> p t j n", t=T, j=4) for i in range(2)]
                    mx = cut(stat, 16, 2, T, 4)
                    for i in range(2):
                        s.did(dve.tensor_reduce(mx[:, i], cs[i], AXX, ALU.max))
                    s.wait()
                    for i in range(2):
                        ins = tt(pc[:, :, i, :, 0:16], cs[i], mx[:, i].unsqueeze(3).to_broadcast([P, T, 4, 16]),
                                 ALU.subtract)
                        if i == 0:
                            s.did(ins)
                        else:
                            ins.then_inc(cmp_sub, 1)
                    dve.wait_ge(cmp_exp, 1)
                    sm = cut(stat, 56, T, 2, 4)
                    pce = pc[:, :, :, :, 0:16]
                    for t in range(T):
                        s.did(dve.tensor_reduce(sm[:, t], pce[:, t], AXX, ALU.add))
                    s.wait()
                    s.then(dve.reciprocal(sm, sm))
                    s.then(tt(sm, sm, gates[:, :, 0:8].rearrange("p t (j i) -> p t i j", i=2), ALU.mult))
                    for t in range(T):
                        s.did(ts(sm[:, t], sm[:, t], any_cmp[:, t:t + 1], None, ALU.mult))
                    s.wait()
                    for t in range(T):
                        tt(pce[:, t], pce[:, t], sm[:, t].unsqueeze(3).to_broadcast([P, 2, 4, 16]),
                           ALU.mult).then_inc(cmp_prob, 1)

                    for m, (to, mask) in enumerate(((LT, strict), (N1T, incl), (MT, strict), (N2T, incl))):
                        for i in range(2):
                            dve.wait_ge(pair_psum, 2 * m + i + 1)
                            tt(to[:, 4 * i:4 * i + 4, :],
                               bank[4 + 2 * (m % 2) + i][:, :].rearrange("p (u t) -> p u t", u=4),
                               mask[:, :].unsqueeze(1).to_broadcast([P, 4, P]), ALU.mult).then_inc(pair_masked, 1)

                    eye8 = ident[:, :].unsqueeze(1).to_broadcast([P, 8, P])
                    lv = levels[:, :].rearrange("p (l t) -> p l t", l=6)

                    def level(i):
                        dve.wait_ge(pair_masked, 2) if i == 0 else dve.wait_ge(inv_ready, 2 * i)
                        tt(LTm, LT, lv[:, i, :].unsqueeze(1).to_broadcast([P, 8, P]), ALU.mult).then_inc(lt_level, 1)
                        dve.wait_ge(lt_level, i + 1)
                        if i == 0:
                            tt(TT, LTm, eye8, ALU.add).then_inc(inv_ready, 1)
                            for j in range(2):
                                dve.wait_ge(u_psum, j + 1)
                                ins = tt(TM[:, 4 * j:4 * j + 4, :],
                                         bank[4 + j][:, :].rearrange("p (u t) -> p u t", u=4),
                                         eye8[:, 0:4, :], ALU.add)
                                s.did(ins) if j == 0 else ins.then_inc(inv_ready, 1)
                            return
                        for j in range(2):
                            rows = slice(4 * j, 4 * j + 4)
                            if i < 5:
                                dve.wait_ge(inv_psum, 4 * (i - 1) + j + 1)
                                s.did(tt(TM[:, rows, :], bank[6 + j][:, :].rearrange("p (u t) -> p u t", u=4),
                                         TM[:, rows, :], ALU.add))
                        for j in range(2):
                            rows = slice(4 * j, 4 * j + 4)
                            dve.wait_ge(inv_psum, 4 * (i - 1) + (2 if i < 5 else 0) + j + 1)
                            tt(TT[:, rows, :], bank[4 + j][:, :].rearrange("p (u t) -> p u t", u=4),
                               TT[:, rows, :], ALU.add).then_inc(inv_ready, 1)

                    def chunk(c):
                        t, rows = c // 2, slice(HD * (c % 2), HD * (c % 2) + HD)
                        if c == 0:
                            dve.wait_ge(z_ready, 1)
                        dve.wait_ge(sa_psum, c + 1)
                        tt(SA[rows, t, :], bank[4][rows, 0:256], Z[rows, t, :], ALU.add).then_inc(sa_ready, 1)
                        if c == NCH - 1:
                            return
                        dve.wait_ge(st_psum, c + 1)
                        for i in range(2):
                            hs = slice(HD * i, HD * (i + 1))
                            ps = bank[5][hs, 0:256].rearrange("p (j v) -> p j v", j=2)[:, :, hs]
                            s.did(tt(ST[hs, :, hs], ps, ST[hs, :, hs], ALU.add))
                        for i in range(2):
                            hs = slice(HD * i, HD * (i + 1))
                            dve.wait_ge(dve_steps, s.n - 1 + i)
                            tt(ST[hs, :, hs], ST[hs, :, hs],
                               pend[hs, :, c:c + 1].to_broadcast([HD, 2, HD]), ALU.mult).then_inc(st_ready, 1)

                    def attend(k):
                        if k < UNITS:
                            n = (k // NSA_HEADS + 1) * P
                            dve.wait_ge(scored, k + 1)
                            m = 48 + 2 * (k % 2)
                            dve.tensor_reduce(stat[:, m:m + 2],
                                              bank[k % 2][:, 0:2 * n].rearrange("p (b n) -> p b n", b=2),
                                              AXX, ALU.max, negate=True).then_inc(maxed, 1)
                        if 1 <= k <= UNITS:
                            j = k - 1
                            t, h, n = j // NSA_HEADS, j % NSA_HEADS, (j // NSA_HEADS + 1) * P
                            m = 52 + 2 * (j % 2)
                            dve.wait_ge(exped, 2 * j + 2)
                            s.then(dve.reciprocal(stat[:, m + 20:m + 22], stat[:, m:m + 2]))
                            s.then(tt(stat[:, m + 20:m + 22], stat[:, m + 20:m + 22],
                                      gates[:, t, 8:24].rearrange("p (b h) -> p b h", b=2)[:, :, h], ALU.mult))
                            for b in range(2):
                                ts(prob[j % 2][:, b * n:(b + 1) * n], prob[j % 2][:, b * n:(b + 1) * n],
                                   stat[:, m + 20 + b:m + 21 + b], None, ALU.mult).then_inc(scaled, 1)

                    def group_norm(i, y, psum, d, inv, eps, g_row, b_row, last):
                        dve.wait_ge(gn_psum, 2 * i + 1)
                        s.then(tt(d, y, psum, ALU.subtract))
                        tt(inv, d, d, ALU.mult).then_inc(gn_in, 1)
                        dve.wait_ge(gn_psum, 2 * i + 2)
                        s.then(ts(inv, psum, eps, None, ALU.add))
                        dve.reciprocal(inv, inv).then_inc(gn_inv, 1)
                        dve.wait_ge(gn_root, i + 1)
                        s.then(tt(d, d, inv, ALU.mult))
                        for j in range(2):
                            ins = ts(d[:, j, :], d[:, j, :], col(g_row + j), col(b_row + j), ALU.mult, ALU.add)
                            if last and j:
                                ins.then_inc(gn_out, 1)
                            else:
                                s.did(ins)

                    for part, i in SCHEDULE:
                        if part == "level":
                            level(i)
                        elif part == "attend":
                            attend(i)
                        elif part == "chunk":
                            chunk(i)
                    b45 = [bank[4 + i][:, :].rearrange("p (i s) -> p i s", i=2) for i in range(2)]
                    dve.wait_ge(conv_ready, 1)
                    group_norm(0, cval, b45[0], upad[:, :, 0:SEQ], csig, CONV_EPS, ROW_CGG, ROW_CGB, True)
                    dve.wait_ge(y_copied, 1)
                    group_norm(1, tmp, b45[1], dev, keff, RWKV_EPS, ROW_LNG, ROW_LNB, False)
                    s.wait()
                    s.then(tt(dev, dev, bonus, ALU.add))
                    tt(mix3[:, 2:4, :], dev, gg, ALU.mult).then_inc(mix_ready, 1)
                    dve.wait_ge(gn_sig, 1)
                    tt(mix3[:, 0:2, :], upad[:, :, 0:SEQ], csig, ALU.mult).then_inc(mix_ready, 1)

                    for n in range(B_OUT, B_PEER):
                        i, t = (n - B_OUT) // 2, (n - B_OUT) % 2
                        cols = slice(i * 512, (i + 1) * 512)
                        dve.wait_ge(streamed, n + 1)
                        part = work[:, (n % 2) * 512:(n % 2 + 1) * 512]
                        s.then(tt(part, bank[n % 4][:, :], mod6[:, 2, cols], ALU.mult))
                        tt(x3[:, t, cols], x3[:, t, cols], part, ALU.add).then_inc(x_added, 1)
                    norm(1)

                    def pick(v_out, i_out, scores, rest):
                        s.then(dve.max(v_out[:, 0:8], scores))
                        s.did(dve.max_index(i_out[:, 0:8], v_out[:, 0:8], scores))
                        s.then(dve.match_replace(rest, v_out[:, 0:8], scores, LOWEST))
                        s.then(dve.max(v_out[:, 8:16], rest))
                        return dve.max_index(i_out[:, 8:16], v_out[:, 8:16], rest)

                    for h in range(PEER_HEADS):
                        dve.wait_ge(keys_scored, h + 1)
                        for t in range(T):
                            for half in range(2):
                                q = 2 * t + half
                                ins = pick(topv[:, t, half, h, :], topi[:, t, half, h, :],
                                           bank[6 + h % 2][:, q * P:(q + 1) * P], left[:, q, :])
                                if q == 3:
                                    ins.then_inc(picked, 1)
                                else:
                                    s.did(ins)
                    dve.wait_ge(picked, PEER_HEADS)
                    s.then(dve.tensor_copy(topf, topi))
                    full = [P, PEER_HEADS, TOPK, TOPK]
                    for t in range(T):
                        s.then(tt(cand, topv[:, t, 0].unsqueeze(3).to_broadcast(full),
                                  topv[:, t, 1].unsqueeze(2).to_broadcast(full), ALU.add))
                        for h in range(PEER_HEADS):
                            s.did(pick(best[:, t, h, :], besti[:, t, h, :],
                                       cand[:, h].rearrange("p i j -> p (i j)"), left2[:, h % 2, :]))
                        s.wait()
                    w3 = cut(wexp, 0, T * PEER_HEADS, TOPK)
                    b3 = cut(work, 1536, T * PEER_HEADS, TOPK)
                    tt(w3, b3, b3[:, :, 0:1].to_broadcast([P, T * PEER_HEADS, TOPK]), ALU.subtract)\
                        .then_inc(wexp_in, 1)
                    s.did(ts(quot_i, besti.bitcast(I32), 4, None, ALU.arith_shift_right))
                    s.did(ts(rem_i, besti.bitcast(I32), TOPK - 1, None, ALU.bitwise_and))
                    s.wait()
                    s.did(dve.tensor_copy(quot, quot_i))
                    s.did(dve.tensor_copy(rem, rem_i))
                    s.wait()
                    for t in range(T):
                        for half, (pos, to) in enumerate(((quot, e1), (rem, e2))):
                            s.then(tt(onehot, pos[:, t].unsqueeze(3).to_broadcast(full),
                                      iota_j[:, :].unsqueeze(1).unsqueeze(1).to_broadcast(full), ALU.is_equal))
                            s.then(tt(onehot, onehot, topf[:, t, half].unsqueeze(2).to_broadcast(full), ALU.mult))
                            s.then(dve.tensor_reduce(to[:, t], onehot, AXX, ALU.add))
                    s.then(stt(out=e1, in0=e1, scalar=float(PEER_KEYS), in1=e2, op0=ALU.mult, op1=ALU.add))
                    s.did(ts(cut(idx_all, 0, T, PEER_HEADS, TOPK), e1, layer_base[:, 0:1], None, ALU.add))
                    dve.wait_ge(wexp_exp, 1)
                    sums = stat[:, 72:72 + T * PEER_HEADS]
                    s.then(dve.tensor_reduce(sums, w3, AXX, ALU.add))
                    s.then(dve.reciprocal(sums, sums))
                    s.then(tt(w3, w3, sums.unsqueeze(2).to_broadcast([P, T * PEER_HEADS, TOPK]), ALU.mult))
                    dve.sem_inc(u_used, RING)
                    s.then(ts(layer_base[:, :], layer_base[:, :], float(N_EXPERTS), None, ALU.add))
                    dve.sem_inc(choice_ready, 1)

                    with dve.Fori(0, T) as t:
                        dve.tensor_copy(gain[:, :], tok3[:, bass.ds(t, 1), :].rearrange("p t d -> p (t d)"))\
                           .then_inc(h2cur_ready, 1)
                        gate(dve, "dve", h2cur_ready, t + 1)
                        with dve.Fori(0, TG // 2) as i:
                            for b in range(2):
                                g = TG * t + 2 * i + b
                                for k in range(GROUP):
                                    dve.wait_ge(u_landed[k], 16 * (NG * l + g + 1))
                                    row = u_ring[:, k, :]
                                    dve.tensor_tensor_reduce(out=row, in0=row, in1=gain[:, :], scale=1.0, scalar=0.0,
                                                             op0=ALU.mult, op1=ALU.add,
                                                             accum_out=hid[:, b * GROUP + k:b * GROUP + k + 1])\
                                       .then_inc(u_used, 1)
                                gate(dve, "dve", v_used, GROUP * g + 1)
                                gate(dve, "dve", gel_ready, g + 1)
                                tt(act_w[:, b * GROUP:(b + 1) * GROUP], gel[:, b * GROUP:(b + 1) * GROUP],
                                   wexp[:, bass.ds(GROUP * g, GROUP)], ALU.mult).then_inc(act_ready, 1)
                        gate(dve, "dve", y_ready, t + 1)
                        for i in range(2):
                            tt(yg[:, i * 512:(i + 1) * 512], bank[i][:, :], mod6[:, 5, i * 512:(i + 1) * 512],
                               ALU.mult).then_inc(y_used, 1)
                        gate(dve, "dve", y_used, 3 * t + 2)
                        xt = x3[:, bass.ds(t, 1), :].rearrange("p t d -> p (t d)")
                        tt(xt, xt, yg, ALU.add).then_inc(y_used, 1)

                @block.tensor
                def _(pe):
                    mm = pe.matmul

                    def transposes_h(i):
                        pe.wait_ge(h_ready, T * (i + 1))
                        for b in range(4):
                            for kc in (2 * b, 2 * b + 1):
                                for t in range(T):
                                    at = (kc % 2) * SEQ + t * P
                                    ins = pe.transpose(bank[4 + b][:, at:at + P], tok3[:, t, kc * P:(kc + 1) * P],
                                                       ident[:, :])
                            ins.then_inc(hT_psum, 1)

                    pe.wait_ge(params_in, 16 * N_PARAMS)
                    for n in range(N_MOD):
                        if n >= 4:
                            pe.wait_ge(copied, n - 3)
                        mm(bank[n % 4][:, :], ident[0:N_MOD, n:n + 1].to_broadcast([N_MOD, P]), brow,
                           start=True, stop=False)
                        chunk_wait(pe, n)
                        for k in range(KC):
                            ins = mm(bank[n % 4][:, :], cT[:, k:k + 1].to_broadcast([P, P]), wslot[n % 2][:, k, :],
                                     start=False, stop=(k == KC - 1))
                        ins.then_inc(streamed, 1)
                    transposes_h(0)
                    pe.wait_ge(hT_act, 1)
                    pe.transpose(bank[4][:, 0:N_ROWS], rows_p[0:N_ROWS, :], ident[0:N_ROWS, 0:N_ROWS])\
                      .then_inc(cols_psum, 1)
                    pe.wait_ge(hT_act, 2)
                    pe.wait_ge(hT_dve, 2)

                    def channels(n, tiles, slot):
                        pe.wait_ge(copied, n - 3)
                        for i, cols in enumerate(tiles):
                            for k in range(KC):
                                ins = mm(bank[n % 4][:, i * SEQ:(i + 1) * SEQ], wslot[slot][:, k, cols], hT3[:, k, :],
                                         start=(k == 0), stop=(k == KC - 1))
                        ins.then_inc(streamed, 1)

                    def tokens(n, cols, slot):
                        w_ = cols.stop - cols.start
                        pe.wait_ge(copied, n - 3)
                        for t in range(T):
                            for k in range(KC):
                                ins = mm(bank[n % 4][:, t * w_:(t + 1) * w_], hT3[:, k, t * P:(t + 1) * P],
                                         wslot[slot][:, k, cols], start=(k == 0), stop=(k == KC - 1))
                        ins.then_inc(streamed, 1)

                    def two(c0):
                        return [slice(c0, c0 + P), slice(c0 + P, c0 + 2 * P)]

                    n = B_RWKV
                    for i in range(4):
                        chunk_wait(pe, N_MOD + i)
                        for c0 in (0, 256):
                            channels(n, two(c0), (N_MOD + i) % 2)
                            n += 1
                    chunk_wait(pe, N_MOD + 4)
                    channels(B_KV, two(0), (N_MOD + 4) % 2)
                    channels(B_KV + 1, [slice(2 * P, 3 * P)], (N_MOD + 4) % 2)
                    tokens(B_KV + 2, slice(3 * P, 4 * P), (N_MOD + 4) % 2)
                    chunk_wait(pe, N_MOD + 5)
                    channels(B_KV + 3, [slice(0, P)], (N_MOD + 5) % 2)
                    tokens(B_KV + 4, slice(P, N_IN - 5 * 512), (N_MOD + 5) % 2)

                    chunk_wait(pe, N_MOD + 6)
                    pe.wait_ge(copied, B_CMP - 3)
                    pe.wait_ge(cols_ready, 2)
                    w1 = wslot[(N_MOD + 6) % 2].rearrange("p k (m j) -> p (k m) j", j=P)
                    for i, z in enumerate((zk, zv)):
                        for j in range(16):
                            ins = mm(bank[B_CMP % 4][:, 45 * i:45 * i + 45], w1[:, 16 * i + j, :],
                                     z[:, :, j:j + 8 * N_C - 7:8], start=(j == 0), stop=(j == 15))
                    ins.then_inc(streamed, 1)

                    pe.wait_ge(lora_act, 2)
                    for b, w, of in ((4, lora_wa[0:HD, :], rw[0:HD, 6, :]), (5, lora_wa[HD:P, :], rw[HD:P, 6, :]),
                                     (6, lora_g[:, :], rw[:, 7, :])):
                        for i in range(2):
                            ins = mm(bank[b][:, i * SEQ:(i + 1) * SEQ], w[:, i * P:(i + 1) * P], of,
                                     start=True, stop=True)
                        ins.then_inc(lora_psum, 1)
                    pe.wait_ge(kk_sq, 1)
                    mm(bank[7][:, :], heads1[:, :], tmp.rearrange("p i s -> p (i s)"), start=True, stop=True)\
                        .then_inc(kk_sum, 1)

                    pe.wait_ge(cmp_hid, 2)
                    pe.wait_ge(copied, B_CMP)
                    for i in range(2):
                        mm(bank[0][HD * i:HD * (i + 1), 0:2 * N_C], w2kv[:, 0:HD],
                           hidk, start=True, stop=True)
                    for g in range(2):
                        for i in range(4):
                            ins = mm(bank[1][32 * i:32 * (i + 1), g * HD:(g + 1) * HD], hidv[:, g, :],
                                     w2kv[:, HD:2 * HD], start=True, stop=True)
                    ins.then_inc(cmp_psum2, 1)
                    pe.wait_ge(cmp_kv, 1)
                    for i in range(2):
                        mask = cmask_b[:, :].rearrange("p (t n) -> p t n", t=T)
                        mm(bank[2 + i][:, 0:T * 64].rearrange("p (t j n) -> p t j n", t=T, j=4), ident_b[:, :],
                           mask.unsqueeze(2).to_broadcast([P, T, 4, 16]), start=True, stop=False,
                           skip_group_check=True)
                        rows = slice(HD * i, HD * (i + 1))
                        for t in range(T):
                            for j in range(4):
                                at = t * 64 + j * 16
                                ins = mm(bank[2 + i][:, at:at + N_C], qT[rows, j, t * P:(t + 1) * P],
                                         kcT[rows, j // 2, :], start=False, stop=(t == T - 1 and j == 3),
                                         skip_group_check=True)
                        ins.then_inc(cmp_scores, 1)

                    pe.wait_ge(bonus_in, 2)
                    pe.wait_ge(lora_out, 5)
                    mm(bank[4][:, :], heads1[:, :], bonus.rearrange("p i s -> p (i s)"), start=True, stop=True)\
                        .then_inc(bonus_psum, 1)
                    pe.wait_ge(kk_inv, 1)
                    for i, (of, need) in enumerate(((bb, 1), (kb, 2), (v_, 2), (qa, 3))):
                        pe.wait_ge(chan_ready, need)
                        if i == 3:
                            pe.wait_ge(tokm_ready, 1)
                        for t in range(T):
                            for j in range(2):
                                at = t * 256 + j * P
                                ins = pe.transpose(bank[(5, 6, 7, 5)[i]][:, at:at + P],
                                                   of[:, j, t * P:(t + 1) * P], ident[:, :])
                        ins.then_inc(tokm_psum, 1)
                    pe.wait_ge(cmp_prob, T)
                    for t in range(T):
                        for i in range(2):
                            ins = pe.transpose(bank[2][:, (2 * t + i) * P:(2 * t + i + 1) * P],
                                               pc[:, t, i].rearrange("p j n -> p (j n)"), ident[:, :])
                    ins.then_inc(cmp_pT, 1)
                    pe.wait_ge(chan_ready, 4)
                    pe.wait_ge(tokm_ready, 4)
                    pe.wait_ge(bonus_out, 1)
                    for m, (of, by) in enumerate(((bb, qa), (bb, qr), (kb, qa), (kb, qr))):
                        for i in range(2):
                            if m >= 2:
                                pe.wait_ge(pair_masked, 2 * (m - 2) + i + 1)
                            rows = slice(HD * i, HD * (i + 1))
                            for j in range(2):
                                for t in range(T):
                                    at = (2 * j + t) * P
                                    ins = mm(bank[4 + 2 * (m % 2) + i][:, at:at + P],
                                             of[rows, j, t * P:(t + 1) * P], by[rows, j, t * P:(t + 1) * P],
                                             start=True, stop=True)
                            ins.then_inc(pair_psum, 1)

                    def products(lhs, rhs, b, done):
                        for j in range(2):
                            for u in range(4 * j, 4 * j + 4):
                                ins = mm(bank[b + j][:, (u % 4) * P:(u % 4 + 1) * P], lhs[:, u, :],
                                         rhs[:, u, :] if rhs is not None else ident[:, :], start=True, stop=True)
                            ins.then_inc(done, 1)

                    def level(i):
                        if i == 0:
                            pe.wait_ge(pair_masked, 8)
                        pe.wait_ge(lt_level, i + 1)
                        if i == 0:
                            products(LTm, None, 4, u_psum)
                            return
                        pe.wait_ge(inv_ready, 2 * i)
                        products(LTm, TM, 4, u_psum)
                        pe.wait_ge(u_ready, 2 * i)
                        if i < 5:
                            products(TT, U, 6, inv_psum)
                        products(U, TT, 4, inv_psum)

                    def unit_of(h, t):
                        return 4 * (h % 2) + 2 * (h // 2) + t

                    def solve():
                        pe.wait_ge(inv_ready, 12)
                        for u in range(8):
                            h = 2 * (u % 4 // 2) + u // 4
                            ins = mm(bank[4][:, u * HD:(u + 1) * HD], MT[:, u, :],
                                     Vt[:, u % 2, h * HD:(h + 1) * HD], start=True, stop=True)
                        ins.then_inc(mv_psum, 1)
                        for h in range(4):
                            for t in range(T):
                                at = (h // 2) * SEQ + t * P
                                ins = mm(bank[5][HD * (h % 2):HD * (h % 2) + HD, at:at + P],
                                         QAt[:, t, h * HD:(h + 1) * HD], TT[:, unit_of(h, t), :],
                                         start=True, stop=True)
                        ins.then_inc(gt_psum, 1)
                        pe.wait_ge(mv_ready, 1)
                        for h in range(4):
                            for t in range(T):
                                at = t * 256 + h * HD
                                ins = mm(bank[6][:, at:at + HD], TT[:, unit_of(h, t), :], MV[:, unit_of(h, t), :],
                                         start=True, stop=True)
                        ins.then_inc(z_psum, 1)
                        mm(bank[7][:, :], zero_b[:, :], zero_b[:, 0:1].to_broadcast([P, 512]), start=True,
                           stop=False, skip_group_check=True)

                    def chunk(c):
                        t, rows = c // 2, slice(HD * (c % 2), HD * (c % 2) + HD)
                        toks = slice(c * HD, (c + 1) * HD)
                        if c == 0:
                            pe.wait_ge(gt_ready, 1)
                            pe.wait_ge(zeros_set, 7)
                        else:
                            pe.wait_ge(st_ready, 2 * c)
                        for j in range(2):
                            ins = mm(bank[4][rows, j * P:(j + 1) * P], GT[:, j, toks], ST[:, j, :],
                                     start=True, stop=True)
                        ins.then_inc(sa_psum, 1)
                        for j in range(2):
                            mm(bank[7][:, j * SEQ + c * HD:j * SEQ + (c + 1) * HD], ST[:, j, :], qr[:, j, toks],
                               start=False, stop=False, skip_group_check=True)
                        pe.wait_ge(sa_ready, c + 1)
                        if c < NCH - 1:
                            for h in range(4):
                                hs = slice(h * HD, (h + 1) * HD)
                                half = slice(HD * (h % 2), HD * (h % 2) + HD)
                                to = bank[5][half, (h // 2) * P + HD * (h % 2):(h // 2) * P + HD * (h % 2) + HD]
                                mm(to, BBt[rows, t, hs], SA[rows, t, hs], start=True, stop=False)
                                ins = mm(to, KBt[rows, t, hs], Vt[rows, t, hs], start=False, stop=True)
                            ins.then_inc(st_psum, 1)
                        if c % 2:
                            for h in range(4):
                                hs = slice(h * HD, (h + 1) * HD)
                                half = slice(HD * (h % 2), HD * (h % 2) + HD)
                                to = bank[7][half, (h // 2) * SEQ + t * P:(h // 2) * SEQ + (t + 1) * P]
                                mm(to, SA[:, t, hs], N1T[:, unit_of(h, t), :], start=False, stop=False,
                                   skip_group_check=True)
                                ins = mm(to, Vt[:, t, hs], N2T[:, unit_of(h, t), :], start=False,
                                         stop=(c == NCH - 1), skip_group_check=True)
                            if c == NCH - 1:
                                ins.then_inc(y_psum, 1)

                    def attend(k):
                        if k < UNITS:
                            t, h, n = k // NSA_HEADS, k % NSA_HEADS, (k // NSA_HEADS + 1) * P
                            rows = slice(HD * (h % 2), HD * (h % 2) + HD)
                            if k >= 2:
                                pe.wait_ge(exped, 2 * (k - 1))
                            for b, keys in enumerate((kselT, kwinT)):
                                mm(bank[k % 2][:, b * n:(b + 1) * n], qT[rows, h // 2, t * P:(t + 1) * P],
                                   keys[rows, h // 4, 0:n], start=True, stop=False, skip_group_check=True)
                                ins = mm(bank[k % 2][:, (b + 1) * n - P:(b + 1) * n], ident_b[:, :], causal_b[:, :],
                                         start=False, stop=True, skip_group_check=True)
                            ins.then_inc(scored, 1)
                        if 2 <= k:
                            j = k - 2
                            t, h = j // NSA_HEADS, j % NSA_HEADS
                            pe.wait_ge(pT_ready, j + 1)
                            if h == 0 and t:
                                pe.wait_ge(o_copied, t)
                            to = bank[3][HD * (h % 2):HD * (h % 2) + HD, (h // 2) * P:(h // 2 + 1) * P]
                            quarter = slice(32 * (h // 2), 32 * (h // 2) + 32)
                            mm(to, vc[quarter, h // 4, :], pcT[quarter, t, h % 2, :], start=True, stop=False,
                               skip_group_check=True)
                            for i in range(2 * (t + 1)):
                                b, kt = i // (t + 1), i % (t + 1)
                                vcols = slice(b * P + (h // 4) * HD, b * P + (h // 4) * HD + HD)
                                ins = mm(to, vtok[:, kt, vcols], probT[j % 2][:, i * P:(i + 1) * P],
                                         start=False, stop=(i == 2 * t + 1), skip_group_check=True)
                            ins.then_inc(attended, 1)
                        if 1 <= k <= UNITS:
                            j = k - 1
                            pe.wait_ge(scaled, 2 * (j + 1))
                            if j == 0:
                                pe.wait_ge(cmp_pTr, 1)
                            else:
                                pe.wait_ge(pT_ready, j)
                            for i in range(2 * (j // NSA_HEADS + 1)):
                                ins = pe.transpose(bank[2][:, i * P:(i + 1) * P],
                                                   prob[j % 2][:, i * P:(i + 1) * P], ident[:, :])
                            ins.then_inc(turned, 1)

                    for part, i in SCHEDULE:
                        if part == "level":
                            level(i)
                        elif part == "attend":
                            attend(i)
                        elif part == "solve":
                            solve()
                        elif part == "chunk":
                            chunk(i)

                    def flat(v):
                        return v.rearrange("p i s -> p (i s)")

                    pe.wait_ge(conv_ready, 1)
                    pe.wait_ge(sa_ready, NCH)
                    mm(bank[4][:, :], heads_mean[:, :], flat(cval), start=True, stop=True).then_inc(gn_psum, 1)
                    pe.wait_ge(gn_in, 1)
                    mm(bank[4][:, :], heads_mean[:, :], flat(csig), start=True, stop=True).then_inc(gn_psum, 1)
                    pe.wait_ge(y_copied, 1)
                    mm(bank[5][:, :], heads_mean[:, :], flat(tmp), start=True, stop=True).then_inc(gn_psum, 1)
                    pe.wait_ge(gn_in, 2)
                    mm(bank[5][:, :], heads_mean[:, :], flat(keff), start=True, stop=True).then_inc(gn_psum, 1)

                    pe.wait_ge(mix_ready, 2)
                    pe.wait_ge(o_copied, T)
                    for n in range(B_OUT, B_PEER):
                        i, t = (n - B_OUT) // 2, (n - B_OUT) % 2
                        if t == 0:
                            chunk_wait(pe, N_MOD + 7 + i)
                        for k in range(KC):
                            ins = mm(bank[n % 4][:, :], mix3[:, k, t * P:(t + 1) * P],
                                     wslot[(N_MOD + 7 + i) % 2][:, k, :], start=(k == 0), stop=(k == KC - 1))
                        ins.then_inc(streamed, 1)
                    transposes_h(1)

                    pe.wait_ge(peer_k_in, 32)
                    for i in range(2):
                        ins = pe.transpose(bank[3][:, i * P:(i + 1) * P], peer_k[:, i, :], ident[:, :])
                    ins.then_inc(kT_psum, 1)
                    pe.wait_ge(hT_act, 4)
                    pe.wait_ge(hT_dve, 4)

                    def queries(h):
                        if h % 2 == 0:
                            chunk_wait(pe, N_MOD + 9 + h // 2)
                        if h >= 2:
                            pe.wait_ge(q_ready, h - 1)
                        w = wslot[(N_MOD + 9 + h // 2) % 2]
                        for i in range(2):
                            c0 = (h % 2) * 256 + i * P
                            for k in range(KC):
                                ins = mm(bank[4 + h % 2][:, i * SEQ:(i + 1) * SEQ], w[:, k, c0:c0 + P],
                                         hT3[:, k, :], start=(k == 0), stop=(k == KC - 1))
                        ins.then_inc(streamed, 1)

                    def key_scores(h):
                        pe.wait_ge(q_ready, h + 1)
                        if h >= 2:
                            pe.wait_ge(picked, h - 1)
                        for t in range(T):
                            for i in range(2):
                                at = (2 * t + i) * P
                                ins = mm(bank[6 + h % 2][:, at:at + P], peer_q[h % 2][:, i, t * P:(t + 1) * P],
                                         peer_kT[:, i, :], start=True, stop=True)
                        ins.then_inc(keys_scored, 1)

                    queries(0)
                    pe.wait_ge(kT_ready, 1)
                    for h in range(1, PEER_HEADS):
                        queries(h)
                        key_scores(h - 1)
                    key_scores(PEER_HEADS - 1)

                    pe.sem_inc(v_used, RING)
                    with pe.Fori(0, T) as t:
                        for i in range(2):
                            mm(bank[i][:, :], zero_b[:, :], zero_b[:, 0:1].to_broadcast([P, 512]), start=True,
                               stop=False, skip_group_check=True)
                        with pe.Fori(0, TG) as i:
                            g = TG * t + i
                            for k in range(GROUP):
                                pe.wait_ge(diag_ready, GROUP * g + k + 1)
                                pe.wait_ge(v_landed[k], 16 * (NG * l + g + 1))
                                for c in range(2):
                                    ins = mm(bank[c][:, :], diag[k % 2], v_ring[:, k, c * 512:(c + 1) * 512],
                                             start=False, stop=False, skip_group_check=True)
                                ins.then_inc(v_used, 1)
                        mm(bank[1][:, 511:512], zero_b[:, :], zero_b[:, 0:1], start=False, stop=True,
                           skip_group_check=True).then_inc(y_ready, 1)
                        pe.wait_ge(y_used, 3 * t + 2)

            lo, hi = layer_sems[0].num, layer_sems[-1].num
            assert [q.num for q in layer_sems] == list(range(lo, hi + 1))
            nc.all_engine_barrier(sems_to_clear=range(lo, hi + 1))

        with nc.Block() as block:
            @block.sync
            def _(sp):
                sp.dma_start(gain[:, :], a["final_g"].rearrange("(a d) -> a d", a=1).to_broadcast([P, D]))\
                  .then_inc(final_in, 16)
                for t in range(T):
                    sp.wait_ge(out_ready, t + 1)
                    sp.dma_start(out[0, t * P:(t + 1) * P, :], tok3[:, t, :]).then_inc(out_done, 16)
                sp.wait_ge(out_done, 16 * T)

            @block.scalar
            def _(act):
                for t in range(T):
                    act.activation(tok3[:, t, :], x3[:, t, :], ACT.Square,
                                   accum_out=stat[:, t:t + 1]).then_inc(final_ssq, 1)
                act.wait_ge(dve_final, 2)
                act.activation(stat[:, 6:6 + T], stat[:, 4:4 + T], ACT.Sqrt).then_inc(final_root, 1)

            @block.vector
            def _(dve):
                dve.wait_ge(final_ssq, T)
                s = Steps(dve, dve_final)
                s.then(dve.tensor_scalar(stat[:, 2:2 + T], stat[:, 0:T], 1.0 / D, RMS_EPS, ALU.mult, ALU.add))
                s.did(dve.reciprocal(stat[:, 4:4 + T], stat[:, 2:2 + T]))
                dve.wait_ge(final_root, 1)
                dve.wait_ge(final_in, 16)
                for t in range(T):
                    dve.scalar_tensor_tensor(out=tok3[:, t, :], in0=x3[:, t, :], scalar=stat[:, 6 + t:7 + t],
                                             in1=gain[:, :], op0=ALU.mult, op1=ALU.mult).then_inc(out_ready, 1)


SCHEDULE = ([("level", i) for i in range(6)] + [("solve", 0)] + [("chunk", i) for i in range(4)]
            + [("attend", k) for k in range(18)])
N_PARAMS = 21

_INS = ['x', 'c', 'ada_w', 'ada_b', 'norm1_g', 'norm2_g', 'w_in', 'conv_dw_w', 'conv_dw_b', 'conv_gn_g', 'conv_gn_b',
        'rwkv_mu', 'rwkv_w0', 'rwkv_w_up', 'rwkv_a0', 'rwkv_a_up', 'rwkv_g_up', 'rwkv_k_k', 'rwkv_k_a', 'rwkv_r_k',
        'rwkv_ln_g', 'rwkv_ln_b', 'nsa_ck_pos', 'nsa_ck_w1', 'nsa_ck_w2', 'nsa_cv_pos', 'nsa_cv_w1', 'nsa_cv_w2',
        'w_out', 'peer_wq', 'peer_k1', 'peer_k2', 'peer_u', 'peer_v', 'final_g']


def kernel(**inputs):
    import numpy as _np
    import concourse.bacc as _bacc
    from concourse.bass_utils import run_bass_kernel_spmd as _run

    nc = _bacc.Bacc("TRN2", target_bir_lowering=False, num_devices=1)
    arrays, args = {}, {}
    for name in _INS:
        v = _np.ascontiguousarray(inputs[name])
        arrays[f"in_{name}_dram"] = v
        args[name] = nc.dram_tensor(f"in_{name}_dram", v.shape, mybir.dt.from_np(v.dtype), kind="ExternalInput").ap()
    out = nc.dram_tensor("out_0_dram", inputs["x"].shape, F32, kind="ExternalOutput").ap()
    build_trunk(nc, args, out)
    r = _run(nc, [arrays], core_ids=[0])
    return r.results[0]["out_0_dram"]
```

```python
from contextlib import ExitStack

import concourse.bass as bass
from concourse import mybir

ALU = mybir.AluOpType
ACT = mybir.ActivationFunctionType
AXX = mybir.AxisListType.X
F32 = mybir.dt.float32
BF16 = mybir.dt.bfloat16
I32 = mybir.dt.int32
U32 = mybir.dt.uint32

P = 128
HD = 64
NEG = -1e30
LOWEST = -3.0e38
RMS_EPS, CONV_EPS, RWKV_EPS = 1e-6, 1e-5, 64e-5
DECAY_RATE = 0.6065306597126334
TAPS = 31
CMP_BLOCK, CMP_STRIDE = 32, 16
TOPK, PEER_HEADS, PEER_KEYS = 16, 8, 128
GROUP = 8
RING = GROUP
NIDX = 3
NSA_HEADS = 8

ROW_MU, ROW_W0, ROW_A0, ROW_KK, ROW_KA, ROW_RK = 0, 8, 10, 12, 14, 16
ROW_LNG, ROW_LNB, ROW_CB, ROW_CGG, ROW_CGB, ROW_TAP = 18, 20, 22, 24, 26, 28
ROW_KPOS, ROW_VPOS, N_ROWS = 90, 106, 122

W_IN_ORDER = [1, 2, 0, 3, 4, 5]
CHUNKS = ([("ada_w", i, 1) for i in range(4)]
          + [("w_in", i, 3 if i == 4 else 2) for i in W_IN_ORDER]
          + [("compression", 0, 1)]
          + [("ada_w", i, 1) for i in range(4, 10)]
          + [("w_out", i, 2) for i in range(2)]
          + [("peer_wq", i, 2) for i in range(4)]
          + [("ada_w", i, 1) for i in range(10, 12)])
BANKS_AFTER = [sum(c[2] for c in CHUNKS[:i + 1]) for i in range(len(CHUNKS))]
CH_IN, CH_CMP, CH_MOD, CH_OUT, CH_PEER = 4, 10, 11, 17, 19
B_RWKV, B_CMP, B_MOD, B_OUT, B_PEER = (BANKS_AFTER[i - 1] for i in (CH_IN, CH_CMP, CH_MOD, CH_OUT, CH_PEER))
B_CONV, B_Q, B_KV = B_RWKV + 4, B_RWKV + 6, B_RWKV + 8
N_COPIED = B_CMP + 8
N_QUERIES = PEER_HEADS + 2


def chosen_at(t, h):
    if t == 0:
        return max(1, 2 * h)
    return min(2 * h + 3, 2 * PEER_HEADS)


class Steps:

    def __init__(self, eng, sem):
        self.eng, self.sem, self.n = eng, sem, 0

    def did(self, ins):
        ins.then_inc(self.sem, 1)
        self.n += 1

    def wait(self):
        self.eng.wait_ge(self.sem, self.n)

    def then(self, ins):
        self.did(ins)
        self.wait()


def build_trunk(nc, a, out):
    DEPTH, D, MODS = a["ada_w"].shape
    SEQ = a["x"].shape[1]
    N_IN = a["w_in"].shape[2]
    N_EXPERTS = a["peer_u"].shape[1]
    T = SEQ // P
    KC = D // P
    N_MOD = MODS // 512
    N_C = (SEQ - CMP_BLOCK) // CMP_STRIDE + 1
    NCH = SEQ // HD
    TG = PEER_HEADS * TOPK // GROUP
    NG = T * TG

    u_rows = a["peer_u"].rearrange("l e d -> (l e) d")
    v_rows = a["peer_v"].rearrange("l e d -> (l e) d")

    with ExitStack() as ctx:
        def sb(name, cols, dt=F32):
            return ctx.enter_context(nc.sbuf_tensor(name, [P, cols], dt))

        def cut(t, at, *shape):
            n = 1
            for s in shape:
                n *= s
            v = t[:, at:at + n]
            if len(shape) == 1:
                return v
            names = "abcd"[:len(shape)]
            return v.rearrange(f"p ({' '.join(names)}) -> p {' '.join(names)}", **dict(zip(names, shape)))

        x_sb = sb("x_sb", T * D)
        mod = sb("mod", MODS)
        gain = sb("gain", D)
        tok = sb("tok", T * D)
        hT = sb("hT", KC * SEQ)
        mixT = sb("mixT", KC * SEQ)
        wring = sb("wring", 2 * KC * 512)
        scratch = sb("scratch", 16384)
        work = sb("work", 9 * 512)
        nsa = sb("nsa", 3960)
        conv = sb("conv", 2 * (SEQ + TAPS - 1) + 1024)
        ident = sb("ident", P)
        ident_b = sb("ident_b", P, BF16)
        causal_b = sb("causal_b", P, BF16)
        cmask_b = sb("cmask_b", T * 16, BF16)
        zero_b = sb("zero_b", P, BF16)
        strict = sb("strict", P, BF16)
        incl = sb("incl", P, BF16)
        levels = sb("levels", 6 * P, BF16)
        heads1 = sb("heads1", P)
        heads_mean = sb("heads_mean", P)
        restart = sb("restart", SEQ)
        iota_j = sb("iota_j", TOPK)
        any_cmp = sb("any_cmp", T)
        rows_p = sb("rows_p", P)
        cols_p = sb("cols_p", P)
        brow = sb("brow", P)
        lora_wa = sb("lora_wa", 256)
        lora_g = sb("lora_g", 256)
        w2kv = sb("w2kv", 2 * HD)
        cT = sb("cT", KC)
        stat = sb("stat", 96)
        layer_base = sb("layer_base", 1)
        idx_all = sb("idx_all", NG * GROUP, I32)
        idx_cur = sb("idx_cur", NIDX * GROUP, I32)
        wexp = sb("wexp", NG * GROUP)
        hid = sb("hid", 2 * GROUP)
        gel = sb("gel", 2 * GROUP)
        act_w = sb("act_w", 2 * GROUP)
        bank = [ctx.enter_context(nc.psum_tensor(f"bank{i}", [P, 512], F32)) for i in range(8)]

        x3 = cut(x_sb, 0, T, D)
        mod6 = cut(mod, 0, 6, D)
        tok3 = cut(tok, 0, T, D)
        hT3 = cut(hT, 0, KC, SEQ)
        mix3 = cut(mixT, 0, KC, SEQ)
        wslot = [cut(wring, i * KC * 512, KC, 512) for i in range(2)]
        crow = cut(work, 512, 3, P)
        prw = cut(scratch, 0, 8, SEQ + 1)
        rw = cut(scratch, 2056, 8, SEQ)
        LT, LTm, U, TM, TT, MT, N1T, N2T = (cut(scratch, 4104 + i * 1024, 8, P) for i in range(8))
        MV = cut(scratch, 4104 + 1024, 8, HD)
        Z = cut(scratch, 12296, T, 4 * HD)
        GT = cut(scratch, 12808, 2, SEQ)
        SA = cut(scratch, 13320, T, 4 * HD)
        BBt, KBt, Vt, QAt = (cut(scratch, 13832 + i * 512, T, 4 * HD) for i in range(4))
        ST = cut(scratch, 15880, 2, P)
        u_ring = cut(scratch, 0, RING, D)
        v_ring = cut(scratch, RING * D, RING, D)
        lw, cum, pcum, pinv, aa, gg, kk, tmp, keff = (cut(work, i * 512, 2, SEQ) for i in range(9))
        qa, qr, kb, bb, bonus, dev = lw, pcum, pinv, aa, cum, kk
        r_, k_, v_ = rw[:, 0:2, :], rw[:, 2:4, :], rw[:, 4:6, :]
        pend = cut(stat, 32, 2, NCH)
        UP = SEQ + TAPS - 1
        upad = cut(conv, 0, 2, UP)
        cval = cut(conv, 2 * UP, 2, SEQ)
        csig = cut(conv, 2 * UP + 512, 2, SEQ)
        qT = cut(nsa, 0, 4, SEQ)
        kselT = cut(nsa, 1024, 2, SEQ)
        kwinT = cut(nsa, 1536, 2, SEQ)
        vtok = cut(nsa, 2048, T, 2 * P)
        kcT = cut(nsa, 2560, 2, N_C)
        vc = cut(nsa, 2592, 2, HD)
        gates = cut(nsa, 2720, T, 24)
        hidk = cut(nsa, 2768, 2, 16)[:, :, 0:N_C]
        hidv = cut(nsa, 2800, 2, 32)
        sigc = cut(nsa, 2864, 2, 32)
        pc = cut(nsa, 2928, T, 2, 4, 32)
        pcT = cut(nsa, 3440, T, 2, P)
        zk = cut(mixT, 4 * SEQ, 3, P)
        zv = cut(mixT, 4 * SEQ + 3 * P, 3, P)
        prob = [cut(tok, i * 512, 512) for i in range(2)]
        probT = [cut(tok, 1024 + i * 512, 512) for i in range(2)]
        topv = cut(work, 0, T, 2, PEER_HEADS, TOPK)
        topi = cut(work, 512, T, 2, PEER_HEADS, TOPK).bitcast(U32)
        topf = cut(work, 1024, T, 2, PEER_HEADS, TOPK)
        best = cut(work, 1536, T, PEER_HEADS, TOPK)
        besti = cut(work, 1792, T, PEER_HEADS, TOPK).bitcast(U32)
        pos_f = cut(work, 2048, 2, TOPK)
        pos_i = cut(work, 2080, 2, TOPK).bitcast(I32)
        chosen = cut(work, 2112, 2, TOPK)
        left = cut(work, 3072, 2, P)
        left2 = work[:, 3584:3840]
        cand = cut(mixT, 0, TOPK, TOPK)
        onehot = cut(mixT, 256, 2, TOPK, TOPK)
        peer_k = cut(conv, 0, 2, P)
        peer_kT = cut(conv, 256, 2, P)
        peer_q = [cut(nsa, i * 512, 2, SEQ) for i in range(2)]
        diag = [cut(nsa, 1024 + i * P, P) for i in range(2)]
        yg = cut(conv, 512, D)

        def sem(name):
            return ctx.enter_context(nc.semaphore(name))

        u_landed = [sem(f"u_landed{i}") for i in range(RING)]
        v_landed = [sem(f"v_landed{i}") for i in range(RING)]
        x_in, c_in, consts, c_done, pe_setup, act_setup, dve_setup = map(sem, (
            "x_in", "c_in", "consts", "c_done", "pe_setup", "act_setup", "dve_setup"))
        final_in, final_ssq, final_root, out_ready, out_done, dve_final = map(sem, (
            "final_in", "final_ssq", "final_root", "out_ready", "out_done", "dve_final"))
        layer_sems = []

        def lsem(name):
            layer_sems.append(sem(name))
            return layer_sems[-1]

        params_in, gain_in, peer_k_in = lsem("params_in"), lsem("gain_in"), lsem("peer_k_in")
        w_landed = [lsem(f"w_landed{i}") for i in range(2)]
        streamed, copied = lsem("streamed"), lsem("copied")
        dve_steps, act_steps, pool_steps = lsem("dve_steps"), lsem("act_steps"), lsem("pool_steps")
        zeros_set, cols_psum, cols_ready, gain_used = map(lsem, ("zeros_set", "cols_psum", "cols_ready", "gain_used"))
        ssq_ready, rms_ready, root_ready, h_ready = map(lsem, ("ssq_ready", "rms_ready", "root_ready", "h_ready"))
        hT_psum, hT_act, hT_dve = map(lsem, ("hT_psum", "hT_act", "hT_dve"))
        lora_in, lora_act, lora_psum, lora_out = map(lsem, ("lora_in", "lora_act", "lora_psum", "lora_out"))
        kk_sq, kk_sum, kk_inv, kk_root = map(lsem, ("kk_sq", "kk_sum", "kk_inv", "kk_root"))
        cum_ready, decays, bonus_in, bonus_psum, bonus_out = map(lsem, (
            "cum_ready", "decays", "bonus_in", "bonus_psum", "bonus_out"))
        chan_ready, tokm_psum, tokm_ready = map(lsem, ("chan_ready", "tokm_psum", "tokm_ready"))
        pair_psum, pair_masked = map(lsem, ("pair_psum", "pair_masked"))
        lt_level, u_psum, u_ready, inv_psum, inv_ready = map(lsem, (
            "lt_level", "u_psum", "u_ready", "inv_psum", "inv_ready"))
        mv_psum, mv_ready, gt_psum, gt_ready, z_psum, z_ready = map(lsem, (
            "mv_psum", "mv_ready", "gt_psum", "gt_ready", "z_psum", "z_ready"))
        sa_psum, sa_ready, st_psum, st_ready, y_psum, y_copied = map(lsem, (
            "sa_psum", "sa_ready", "st_psum", "st_ready", "y_psum", "y_copied"))
        conv_ready, gn_in, gn_psum, gn_inv, gn_root, gn_out, gn_sig = map(lsem, (
            "conv_ready", "gn_in", "gn_psum", "gn_inv", "gn_root", "gn_out", "gn_sig"))
        cmp_sig, cmp_hid, cmp_psum2, cmp_kv = map(lsem, ("cmp_sig", "cmp_hid", "cmp_psum2", "cmp_kv"))
        cmp_scores, cmp_sub, cmp_exp, cmp_prob, cmp_pT, cmp_pTr = map(lsem, (
            "cmp_scores", "cmp_sub", "cmp_exp", "cmp_prob", "cmp_pT", "cmp_pTr"))
        scored, maxed, exped, scaled, turned, pT_ready, attended, o_copied = map(lsem, (
            "scored", "maxed", "exped", "scaled", "turned", "pT_ready", "attended", "o_copied"))
        mix_ready, x_added = lsem("mix_ready"), lsem("x_added")
        kT_psum, kT_ready, q_ready, keys_scored, picked = map(lsem, (
            "kT_psum", "kT_ready", "q_ready", "keys_scored", "picked"))
        wexp_in, wexp_exp, choice_ready = map(lsem, ("wexp_in", "wexp_exp", "choice_ready"))
        idx_ready, u_used, v_used, gel_ready, act_ready, diag_ready, y_ready, y_used = map(lsem, (
            "idx_ready", "u_used", "v_used", "gel_ready", "act_ready", "diag_ready", "y_ready", "y_used"))
        turns = {e: lsem(f"turns_{e}") for e in ("pool", "dve")}

        def chunk_wait(eng, i):
            eng.wait_ge(w_landed[i % 2], 32 * (i // 2 + 1))

        def gate(eng, name, s, value):
            eng.wait_ge(s, value)
            eng.sem_inc(turns[name], 1)

        UNITS = T * NSA_HEADS

        with nc.Block() as block:
            @block.sync
            def _(sp):
                sp.dma_start(crow[0:KC, 0, :], a["c"].rearrange("a (k p) -> (a k) p", p=P)).then_inc(c_in, 16)
                sp.dma_start(x3, a["x"].rearrange("a (t p) d -> p (a t) d", p=P)).then_inc(x_in, 16)

            @block.gpsimd
            def _(pool):
                s = Steps(pool, consts)

                def select(view, op, fill, base, pattern, cm):
                    s.then(pool.affine_select(out=view, in_=view, compare_op=op, fill=fill, base=base,
                                              pattern=pattern, channel_multiplier=cm))

                for t_, v in ((ident, 0.0), (ident_b, 0.0), (causal_b, 0.0), (cmask_b, 0.0), (zero_b, 0.0),
                              (strict, 1.0), (incl, 1.0), (levels, 0.0), (heads1, 1.0), (heads_mean, 1.0 / HD),
                              (restart, 1.0), (any_cmp, 1.0), (layer_base, 0.0)):
                    s.did(pool.memset(t_[:, :], v))
                lv = levels[:, :].rearrange("p (l t) -> p l t", l=6)
                halves = []
                for i in range(6):
                    b = 1 << i
                    halves.append(lv[:, i, :].rearrange("p (n h b) -> p n h b", h=2, b=b)[:, :, 1, :])
                s.wait()
                s.did(pool.memset(restart[:, :].rearrange("p (c t) -> p c t", t=HD)[:, :, 0:1], 0.0))
                for h_ in halves:
                    s.did(pool.memset(h_, 1.0))
                s.then(pool.iota(iota_j[:, :], pattern=[[1, TOPK]], base=0, channel_multiplier=0,
                                 allow_small_or_imprecise_dtypes=True))
                for m in (ident, ident_b):
                    select(m[:, :], ALU.not_equal, 1.0, 0, [[-1, P]], 1)
                select(causal_b[:, :], ALU.is_ge, NEG, 0, [[-1, P]], 1)
                cm3 = cmask_b[:, :].rearrange("p (t n) -> p t n", t=T)
                select(cm3, ALU.is_ge, NEG, -(CMP_BLOCK - 1), [[P, T], [-CMP_STRIDE, 16]], 1)
                s.then(pool.memset(cm3[:, :, N_C:16], NEG))
                select(any_cmp[:, :], ALU.is_ge, 0.0, -(CMP_BLOCK - 1), [[P, T]], 1)
                for m, base in ((strict, -1), (incl, 0)):
                    v = m[:, :].rearrange("p (c t) -> p c t", c=2)
                    select(v, ALU.is_ge, 0.0, base, [[HD, 2], [1, HD]], -1)
                    select(v, ALU.is_ge, 0.0, 0, [[-HD, 2], [0, HD]], 1)
                for m in (heads1, heads_mean):
                    v = m[:, :].rearrange("p (c t) -> p c t", c=2)
                    select(v, ALU.is_ge, 0.0, 0, [[-HD, 2], [0, HD]], 1)
                    select(v, ALU.is_ge, 0.0, HD - 1, [[HD, 2], [0, HD]], -1)
                for i, h_ in enumerate(halves):
                    b = 1 << i
                    n = P // (2 * b)
                    select(h_, ALU.is_ge, 0.0, 0, [[-2 * b, n], [0, b]], 1)
                    select(h_, ALU.is_ge, 0.0, b - 1, [[2 * b, n], [0, b]], -1)
                pool.sem_inc(pe_setup, 1)

            @block.scalar
            def _(act):
                act.wait_ge(c_in, 16)
                act.activation(crow[0:KC, 1, :], crow[0:KC, 0, :], ACT.Sigmoid).then_inc(act_setup, 1)

            @block.vector
            def _(dve):
                dve.wait_ge(act_setup, 1)
                dve.tensor_tensor(crow[0:KC, 2, :], crow[0:KC, 0, :], crow[0:KC, 1, :], ALU.mult)\
                   .then_inc(dve_setup, 1)
                dve.wait_ge(c_done, 1)
                dve.tensor_copy(cT[:, :], bank[0][:, 0:KC]).then_inc(dve_setup, 1)
                dve.wait_ge(dve_setup, 2)
                dve.wait_ge(x_in, 16)

            @block.tensor
            def _(pe):
                pe.wait_ge(pe_setup, 1)
                pe.wait_ge(dve_setup, 1)
                pe.transpose(bank[0][:, 0:KC], crow[0:KC, 2, :], ident[0:KC, 0:KC]).then_inc(c_done, 1)

        nc.all_engine_barrier()

        with nc.Fori(0, DEPTH) as l:
            with nc.Block() as block:
                L = bass.ds(l, 1)

                def vec(name, p=P):
                    return a[name][L].rearrange("l (r p) -> (l r) p", p=p)

                @block.sync
                def _(sp):
                    def param(to, of):
                        sp.dma_start(to, of).then_inc(params_in, 16)

                    param(brow[0:MODS // P, :], vec("ada_b"))
                    for name, row, n in (("rwkv_mu", ROW_MU, 8), ("rwkv_w0", ROW_W0, 2), ("rwkv_a0", ROW_A0, 2),
                                         ("rwkv_k_k", ROW_KK, 2), ("rwkv_k_a", ROW_KA, 2),
                                         ("rwkv_ln_g", ROW_LNG, 2), ("rwkv_ln_b", ROW_LNB, 2),
                                         ("conv_dw_b", ROW_CB, 2), ("conv_gn_g", ROW_CGG, 2),
                                         ("conv_gn_b", ROW_CGB, 2)):
                        param(rows_p[row:row + n, :], vec(name))
                    param(rows_p[ROW_RK:ROW_RK + 2, :],
                          a["rwkv_r_k"][L].rearrange("l (r h) d -> (l r) (h d)", r=2))
                    for i in range(2):
                        param(rows_p[ROW_TAP + i * TAPS:ROW_TAP + (i + 1) * TAPS, :],
                              a["conv_dw_w"][L, :, 0, i * P:(i + 1) * P].rearrange("l w c -> (l w) c"))
                    for name, row in (("nsa_ck_pos", ROW_KPOS), ("nsa_cv_pos", ROW_VPOS)):
                        param(rows_p[row:row + 16, :],
                              a[name][L].rearrange("l (n e) d -> (l n) (e d)", e=2))
                    param(lora_wa[0:HD, :], a["rwkv_w_up"][L].rearrange("l k n -> (l k) n"))
                    param(lora_wa[HD:P, :], a["rwkv_a_up"][L].rearrange("l k n -> (l k) n"))
                    param(lora_g[:, :], a["rwkv_g_up"][L].rearrange("l k n -> (l k) n"))
                    for i, name in enumerate(("nsa_ck_w2", "nsa_cv_w2")):
                        param(w2kv[:, i * HD:(i + 1) * HD], a[name][L].rearrange("l k n -> (l k) n"))
                    sp.dma_start(gain[:, :], a["norm1_g"][L].to_broadcast([P, D])).then_inc(gain_in, 16)

                    def load_chunk(i):
                        if i >= 2:
                            sp.wait_ge(streamed, BANKS_AFTER[i - 2])
                        for half in range(2):
                            ks = slice(half * KC // 2, (half + 1) * KC // 2)
                            table, j, _ = CHUNKS[i]
                            if table == "compression":
                                of = a[("nsa_ck_w1", "nsa_cv_w1")[half]][L]\
                                    .rearrange("l (n p) j -> p (l n) j", p=P)
                                to = wslot[i % 2][:, ks, :].rearrange("p k (m j) -> p (k m) j", j=P)
                                sp.dma_start(to, of, max_dma_last_dim=4 * P).then_inc(w_landed[i % 2], 16)
                                continue
                            cols = slice(j * 512, min((j + 1) * 512, a[table].shape[2]))
                            of = a[table][L, :, cols].rearrange("l (k p) n -> p (l k) n", p=P)[:, ks, :]
                            to = wslot[i % 2][:, ks, 0:cols.stop - cols.start]
                            sp.dma_start(to, of).then_inc(w_landed[i % 2], 16)

                    for i in range(len(CHUNKS)):
                        load_chunk(i)
                        if i == CH_CMP:
                            sp.wait_ge(gain_used, 1)
                            sp.dma_start(gain[:, :], a["norm2_g"][L].to_broadcast([P, D])).then_inc(gain_in, 16)
                        if i == CH_PEER - 1:
                            sp.wait_ge(streamed, B_OUT + 1)
                            for j, name in enumerate(("peer_k1", "peer_k2")):
                                sp.dma_start(peer_k[:, j, :], a[name][L].rearrange("l n d -> (l n) d"))\
                                  .then_inc(peer_k_in, 16)

                @block.gpsimd
                def _(pool):
                    for v in (prw[:, :, 0:1], upad[:, :, 0:TAPS - 1], hidv, pc, zk[:, 2, :], zv[:, 2, :], ST):
                        pool.memset(v, 0.0).then_inc(zeros_set, 1)
                    s = Steps(pool, pool_steps)
                    pool.wait_ge(cols_ready, 1)
                    pool.wait_ge(zeros_set, 7)
                    pool.wait_ge(copied, B_CONV + 2)
                    s.then(pool.tensor_tensor(upad[:, :, TAPS - 1:UP], cval, csig, ALU.mult))
                    both = [P, 2, SEQ]
                    s.then(pool.tensor_copy(cval, cols_p[:, ROW_CB:ROW_CB + 2].unsqueeze(2).to_broadcast(both)))
                    for j in range(TAPS):
                        w = cols_p[:, ROW_TAP + j:ROW_TAP + TAPS + j + 1:TAPS].unsqueeze(2).to_broadcast(both)
                        s.then(pool.tensor_tensor(csig, upad[:, :, j:j + SEQ], w, ALU.mult))
                        s.then(pool.tensor_tensor(cval, cval, csig, ALU.add))
                    pool.sem_inc(conv_ready, 1)

                    def gather(table, ring, landed, used, b, k, n):
                        gate(pool, "pool", used, n + 1)
                        at = idx_cur[:, b * GROUP + k:b * GROUP + k + 1]
                        pool.indirect_dma_start(ring[:, k, :], None, table,
                                                bass.IndirectOffsetOnAxis(ap=at, axis=0)).then_inc(landed[k], 16)

                    def fetch_indices(b, g):
                        gate(pool, "pool", choice_ready, g + 1)
                        pool.tensor_copy(idx_cur[:, b * GROUP:(b + 1) * GROUP],
                                         idx_all[:, bass.ds(g * GROUP, GROUP)]).then_inc(idx_ready, 1)
                        gate(pool, "pool", idx_ready, g + 1)

                    for g in range(2):
                        fetch_indices(g, g)
                        for k in range(GROUP):
                            gather(u_rows, u_ring, u_landed, u_used, g, k, g * GROUP + k)
                            if g:
                                gather(v_rows, v_ring, v_landed, v_used, 0, k, k)
                    with pool.Fori(0, (NG - 2) // NIDX) as i:
                        for m in range(NIDX):
                            g = NIDX * i + (2 + m)
                            b = (2 + m) % NIDX
                            gate(pool, "pool", v_used, GROUP * (g - NIDX + 1) + RING)
                            fetch_indices(b, g)
                            for k in range(GROUP):
                                gather(u_rows, u_ring, u_landed, u_used, b, k, GROUP * g + k)
                                gather(v_rows, v_ring, v_landed, v_used, (b + NIDX - 1) % NIDX, k,
                                       GROUP * (g - 1) + k)
                    for k in range(GROUP):
                        gather(v_rows, v_ring, v_landed, v_used, (NG - 1) % NIDX, k, GROUP * (NG - 1) + k)

                @block.scalar
                def _(act):
                    s = Steps(act, act_steps)

                    def squares(i):
                        for t in range(T):
                            act.activation(tok3[:, t, :], x3[:, t, :], ACT.Square,
                                           accum_out=stat[:, t:t + 1]).then_inc(ssq_ready, 1)

                    def root(i):
                        act.wait_ge(rms_ready, i + 1)
                        act.activation(stat[:, 6:6 + T], stat[:, 4:4 + T], ACT.Sqrt).then_inc(root_ready, 1)

                    def hT_copies(i):
                        for b in (0, 1):
                            act.wait_ge(hT_psum, 4 * i + b + 1)
                            act.activation(hT3[:, 2 * b:2 * b + 2, :],
                                           bank[4 + b][:, :].rearrange("p (k s) -> p k s", k=2), ACT.Copy)\
                               .then_inc(hT_act, 1)

                    def halves(n):
                        return bank[n % 4][:, :].rearrange("p (i s) -> p i s", i=2)

                    squares(0)
                    root(0)
                    for n in range(4):
                        act.wait_ge(streamed, n + 1)
                        act.activation(mod[:, n * 512:(n + 1) * 512], bank[n % 4][:, :], ACT.Copy)\
                           .then_inc(copied, 1)
                    hT_copies(0)
                    for n in range(B_RWKV, B_CMP):
                        act.wait_ge(streamed, n + 1)
                        h_ = halves(n)
                        if n == B_RWKV:
                            act.wait_ge(zeros_set, 7)
                        if n < B_CONV:
                            i = 2 * (n - B_RWKV)
                            last = act.activation(prw[:, i:i + 2, 1:SEQ + 1], h_, ACT.Copy)
                        elif n == B_CONV:
                            last = act.activation(cval, h_, ACT.Copy)
                        elif n == B_CONV + 1:
                            last = act.activation(csig, h_, ACT.Sigmoid)
                        elif n < B_KV:
                            i = 2 * (n - B_Q)
                            last = act.activation(qT[:, i:i + 2, :], h_, ACT.Copy, scale=float(HD) ** -0.5)
                        elif n == B_KV:
                            for z, i in ((zk, 0), (zv, 1)):
                                for g in range(2):
                                    for odd in range(2):
                                        of = h_[g * HD:(g + 1) * HD, i, :].rearrange("p (n e) -> p n e", e=2)
                                        last = act.activation(z[odd * HD:(odd + 1) * HD, g, :], of[:, :, odd],
                                                              ACT.Copy)
                                        if i * 4 + g * 2 + odd < 7:
                                            s.did(last)
                        elif n in (B_KV + 1, B_KV + 3):
                            keys = kselT if n == B_KV + 1 else kwinT
                            for g in range(2):
                                for half in range(2):
                                    last = act.activation(keys[half * HD:(half + 1) * HD, g, :],
                                                          h_[g * HD:(g + 1) * HD, 0, :], ACT.Copy)
                                    if g * 2 + half < 3:
                                        s.did(last)
                        elif n == B_KV + 2:
                            last = act.activation(vtok[:, :, 0:P], bank[n % 4][:, 0:T * P]
                                                  .rearrange("p (t c) -> p t c", t=T), ACT.Copy)
                        else:
                            v = bank[n % 4][:, 0:T * (P + 24)].rearrange("p (t c) -> p t c", t=T)
                            s.did(act.activation(vtok[:, :, P:2 * P], v[:, :, 0:P], ACT.Copy))
                            last = act.activation(gates, v[:, :, P:P + 24], ACT.Sigmoid)
                        last.then_inc(copied, 1)

                    act.wait_ge(lora_in, 2)
                    act.activation(rw[0:HD, 6, :], rw[0:HD, 6, :], ACT.Tanh).then_inc(lora_act, 1)
                    act.activation(rw[:, 7, :], rw[:, 7, :], ACT.Sigmoid).then_inc(lora_act, 1)
                    act.wait_ge(streamed, B_CMP + 1)
                    act.wait_ge(cmp_hid, 1)
                    act.activation(sigc, sigc, ACT.Sigmoid).then_inc(cmp_sig, 1)
                    act.wait_ge(lora_psum, 3)
                    for i in range(2):
                        act.activation(lw[:, i, :], bank[4][:, i * SEQ:(i + 1) * SEQ], ACT.Sigmoid,
                                       bias=cols_p[:, ROW_W0 + i:ROW_W0 + i + 1]).then_inc(lora_out, 1)
                    for i in range(2):
                        act.activation(aa[:, i, :], bank[5][:, i * SEQ:(i + 1) * SEQ], ACT.Sigmoid,
                                       bias=cols_p[:, ROW_A0 + i:ROW_A0 + i + 1]).then_inc(lora_out, 1)
                    act.activation(gg, bank[6][:, :].rearrange("p (i s) -> p i s", i=2), ACT.Copy)\
                       .then_inc(lora_out, 1)
                    act.wait_ge(cmp_psum2, 1)
                    s.did(act.activation(kcT, bank[0][:, 0:2 * N_C].rearrange("p (g n) -> p g n", g=2), ACT.Copy))
                    act.activation(vc, bank[1][:, 0:2 * HD].rearrange("p (g d) -> p g d", g=2), ACT.Copy)\
                       .then_inc(cmp_kv, 1)
                    act.wait_ge(kk_inv, 1)
                    act.activation(tmp, tmp, ACT.Sqrt).then_inc(kk_root, 1)
                    act.wait_ge(cum_ready, 1)
                    act.activation(pcum, cum, ACT.Exp).then_inc(decays, 1)
                    act.activation(pinv, cum, ACT.Exp, scale=-1.0).then_inc(decays, 1)
                    act.activation(lw, lw, ACT.Exp).then_inc(decays, 1)
                    for i, to in enumerate((BBt, KBt, Vt, QAt)):
                        act.wait_ge(tokm_psum, i + 1)
                        act.activation(to, bank[(5, 6, 7, 5)[i]][:, :].rearrange("p (t c) -> p t c", t=T), ACT.Copy)\
                           .then_inc(tokm_ready, 1)
                    act.wait_ge(cmp_sub, 1)
                    act.activation(pc[:, :, :, :, 0:16].rearrange("p t i j n -> p (t i j) n"),
                                   pc[:, :, :, :, 0:16].rearrange("p t i j n -> p (t i j) n"), ACT.Exp)\
                       .then_inc(cmp_exp, 1)
                    act.wait_ge(cmp_pT, 1)
                    act.activation(pcT, bank[2][:, :].rearrange("p (t i q) -> p t i q", t=T, i=2), ACT.Copy)\
                       .then_inc(cmp_pTr, 1)

                    def modulation(j):
                        act.wait_ge(streamed, B_MOD + j - 4 + 1)
                        act.activation(mod[:, j * 512:(j + 1) * 512], bank[6][:, :], ACT.Copy).then_inc(copied, 1)

                    def u_copy(lev):
                        for i in range(2):
                            act.wait_ge(u_psum, 2 * lev + i + 1)
                            act.activation(U[:, 4 * i:4 * i + 4, :],
                                           bank[4 + i][:, :].rearrange("p (u t) -> p u t", u=4), ACT.Copy)\
                               .then_inc(u_ready, 1)

                    def attend(k):
                        if k < UNITS:
                            t, h, n = k // NSA_HEADS, k % NSA_HEADS, (k // NSA_HEADS + 1) * P
                            act.wait_ge(maxed, k + 1)
                            if k >= 2:
                                act.wait_ge(turned, k - 1)
                            for b in range(2):
                                ins = act.activation(prob[k % 2][:, b * n:(b + 1) * n],
                                                     bank[k % 2][:, b * n:(b + 1) * n], ACT.Exp,
                                                     bias=stat[:, 48 + 2 * (k % 2) + b:49 + 2 * (k % 2) + b],
                                                     accum_out=stat[:, 52 + 2 * (k % 2) + b:53 + 2 * (k % 2) + b])
                                ins.then_inc(exped, 1)
                        if 1 <= k <= UNITS:
                            j = k - 1
                            n = 2 * (j // NSA_HEADS + 1) * P
                            act.wait_ge(turned, j + 1)
                            if j >= 2:
                                act.wait_ge(attended, j - 1)
                            act.activation(probT[j % 2][:, 0:n], bank[2][:, 0:n], ACT.Copy).then_inc(pT_ready, 1)
                        if k >= 2 and (k - 2) % NSA_HEADS == NSA_HEADS - 1:
                            t = (k - 2) // NSA_HEADS
                            act.wait_ge(attended, k - 1)
                            act.activation(mix3[:, 4:8, t * P:(t + 1) * P],
                                           bank[3][:, :].rearrange("p (j q) -> p j q", j=4), ACT.Copy)\
                               .then_inc(o_copied, 1)

                    for part, i in SCHEDULE:
                        if part == "level" and i:
                            u_copy(i)
                        elif part == "attend":
                            attend(i)
                        elif part == "mod":
                            modulation(i)
                        elif part == "solve":
                            act.wait_ge(mv_psum, 1)
                            act.activation(MV, bank[4][:, :].rearrange("p (u d) -> p u d", u=8), ACT.Copy)\
                               .then_inc(mv_ready, 1)
                            act.wait_ge(gt_psum, 1)
                            act.activation(GT, bank[5][:, :].rearrange("p (i s) -> p i s", i=2), ACT.Copy)\
                               .then_inc(gt_ready, 1)
                            act.wait_ge(z_psum, 1)
                            act.activation(Z, bank[6][:, :].rearrange("p (t c) -> p t c", t=T), ACT.Copy)\
                               .then_inc(z_ready, 1)
                    act.wait_ge(y_psum, 1)
                    act.activation(tmp, bank[7][:, :].rearrange("p (i s) -> p i s", i=2), ACT.Copy)\
                       .then_inc(y_copied, 1)
                    for i, v in ((0, csig), (1, keff)):
                        act.wait_ge(gn_inv, i + 1)
                        act.activation(v, v, ACT.Sqrt).then_inc(gn_root, 1)
                    act.wait_ge(gn_out, 1)
                    act.activation(csig, upad[:, :, 0:SEQ], ACT.Sigmoid).then_inc(gn_sig, 1)
                    act.wait_ge(x_added, 4)
                    squares(1)
                    root(1)
                    hT_copies(1)
                    act.wait_ge(kT_psum, 1)
                    act.activation(peer_kT, bank[3][:, 0:2 * P].rearrange("p (i n) -> p i n", i=2), ACT.Copy)\
                       .then_inc(kT_ready, 1)
                    def query_copy(h):
                        act.wait_ge(streamed, B_PEER + h + 1)
                        if h >= PEER_HEADS:
                            j = N_MOD - 2 + h - PEER_HEADS
                            act.activation(mod[:, j * 512:(j + 1) * 512], bank[2 + h % 2][:, :], ACT.Copy)\
                               .then_inc(copied, 1)
                            return
                        if h >= 2:
                            act.wait_ge(keys_scored, h - 1)
                        act.activation(peer_q[h % 2], bank[2 + h % 2][:, :].rearrange("p (i s) -> p i s", i=2),
                                       ACT.Copy).then_inc(q_ready, 1)

                    def exponentials(nth, cols):
                        act.wait_ge(wexp_in, nth)
                        act.activation(wexp[:, cols], wexp[:, cols], ACT.Exp).then_inc(wexp_exp, 1)

                    def experts(g, b):
                        act.wait_ge(u_used, GROUP * (g + 1) + RING)
                        act.activation(gel[:, b * GROUP:(b + 1) * GROUP], hid[:, b * GROUP:(b + 1) * GROUP],
                                       ACT.Gelu).then_inc(gel_ready, 1)
                        act.wait_ge(act_ready, g + 1)
                        for k in range(GROUP):
                            act.wait_ge(v_used, GROUP * g + k + RING - 1)
                            act.activation(diag[k % 2], ident[:, :], ACT.Copy,
                                           scale=act_w[:, b * GROUP + k:b * GROUP + k + 1])\
                               .then_inc(diag_ready, 1)

                    for h in range(3):
                        query_copy(h)
                    exponentials(1, slice(0, TOPK))
                    for h in range(PEER_HEADS):
                        experts(2 * h, 0)
                        if h < PEER_HEADS - 1:
                            exponentials(chosen_at(0, h + 1), slice((h + 1) * TOPK, (h + 2) * TOPK))
                        else:
                            exponentials(T * PEER_HEADS, slice(PEER_HEADS * TOPK, T * PEER_HEADS * TOPK))
                        experts(2 * h + 1, 1)
                        if h < N_QUERIES - 3:
                            query_copy(h + 3)
                    with act.Fori(TG // 2, NG // 2) as i:
                        for b in range(2):
                            experts(2 * i + b, b)

                @block.vector
                def _(dve):
                    s = Steps(dve, dve_steps)
                    tt, ts, stt = dve.tensor_tensor, dve.tensor_scalar, dve.scalar_tensor_tensor

                    def col(row):
                        return cols_p[:, row:row + 1]

                    def norm(i):
                        dve.wait_ge(ssq_ready, T * (i + 1))
                        s.then(ts(stat[:, 2:2 + T], stat[:, 0:T], 1.0 / D, RMS_EPS, ALU.mult, ALU.add))
                        dve.reciprocal(stat[:, 4:4 + T], stat[:, 2:2 + T]).then_inc(rms_ready, 1)
                        dve.wait_ge(gain_in, 16 * (i + 1))
                        dve.wait_ge(copied, 4 if i == 0 else N_COPIED - 2)
                        stt(out=mod6[:, 3 * i + 1, :], in0=mod6[:, 3 * i + 1, :], scalar=1.0, in1=gain[:, :],
                            op0=ALU.add, op1=ALU.mult).then_inc(gain_used, 1)
                        dve.wait_ge(gain_used, i + 1)
                        dve.wait_ge(root_ready, i + 1)
                        for t in range(T):
                            s.did(stt(out=tok3[:, t, :], in0=x3[:, t, :], scalar=stat[:, 6 + t:7 + t],
                                      in1=mod6[:, 3 * i + 1, :], op0=ALU.mult, op1=ALU.mult))
                        for t in range(T):
                            dve.wait_ge(dve_steps, s.n - T + t + 1)
                            tt(tok3[:, t, :], tok3[:, t, :], mod6[:, 3 * i, :], ALU.add).then_inc(h_ready, 1)
                        for b in (2, 3):
                            dve.wait_ge(hT_psum, 4 * i + b + 1)
                            dve.tensor_copy(hT3[:, 2 * b:2 * b + 2, :],
                                            bank[4 + b][:, :].rearrange("p (k s) -> p k s", k=2)).then_inc(hT_dve, 1)

                    norm(0)
                    dve.wait_ge(cols_psum, 1)
                    dve.tensor_copy(cols_p[:, 0:N_ROWS], bank[4][:, 0:N_ROWS]).then_inc(cols_ready, 1)
                    dve.wait_ge(cols_ready, 1)
                    s.did(ts(stat[:, 10:12], cols_p[:, ROW_KA:ROW_KA + 2], -1.0, 1.0, ALU.mult, ALU.add))
                    dve.wait_ge(zeros_set, 7)
                    s.did(dve.tensor_copy(zk[:, 2, 0:16], cols_p[:, ROW_KPOS:ROW_KPOS + 16]))
                    dve.tensor_copy(zv[:, 2, 0:16], cols_p[:, ROW_VPOS:ROW_VPOS + 16]).then_inc(cols_ready, 1)

                    dve.wait_ge(copied, B_RWKV + 4)
                    for part in (slice(6, 8), slice(0, 6)):
                        s.did(tt(rw[:, part, :], prw[:, part, 0:SEQ], prw[:, part, 1:SEQ + 1], ALU.subtract))
                    dve.wait_ge(dve_steps, s.n - 1)
                    for i in (6, 7):
                        stt(out=rw[:, i, :], in0=rw[:, i, :], scalar=col(ROW_MU + i), in1=prw[:, i, 1:SEQ + 1],
                            op0=ALU.mult, op1=ALU.add).then_inc(lora_in, 1)
                    s.wait()
                    for i in range(6):
                        s.did(stt(out=rw[:, i, :], in0=rw[:, i, :], scalar=col(ROW_MU + i),
                                  in1=prw[:, i, 1:SEQ + 1], op0=ALU.mult, op1=ALU.add))
                    s.wait()
                    for i in range(2):
                        s.did(ts(kk[:, i, :], k_[:, i, :], col(ROW_KK + i), None, ALU.mult))
                    s.wait()
                    tt(tmp, kk, kk, ALU.mult).then_inc(kk_sq, 1)
                    dve.wait_ge(streamed, B_CMP + 1)
                    hb = bank[B_CMP % 4]
                    s.then(dve.tensor_copy(stat[:, 12:14], hb[:, 0:90].rearrange("p (z g) -> p z g", z=2)[:, :, 30]))
                    for i, v in enumerate((hidk, hidv[:, :, 0:N_C])):
                        s.did(ts(v, hb[:, 45 * i:45 * i + 30].rearrange("p (g n) -> p g n", g=2),
                                 stat[:, 12 + i:13 + i], None, ALU.add))
                    s.wait()
                    sk = sigc.rearrange("p i (g n) -> p i g n", g=2)[:, :, :, 0:N_C]
                    s.did(dve.memset(sigc, 0.0))
                    s.wait()
                    s.did(dve.tensor_copy(sk[:, 0], hidk))
                    dve.tensor_copy(sk[:, 1], hidv[:, :, 0:N_C]).then_inc(cmp_hid, 1)
                    dve.wait_ge(cmp_sig, 1)
                    s.did(tt(hidk, hidk, sk[:, 0], ALU.mult))
                    tt(hidv[:, :, 0:N_C], hidv[:, :, 0:N_C], sk[:, 1], ALU.mult).then_inc(cmp_hid, 1)
                    dve.wait_ge(lora_out, 2)
                    s.then(ts(lw, lw, -DECAY_RATE, None, ALU.mult))
                    for i in range(2):
                        s.did(dve.tensor_tensor_scan(out=cum[:, i, :], data0=restart[:, :], data1=lw[:, i, :],
                                                     initial=0.0, op0=ALU.mult, op1=ALU.add))
                    s.wait()
                    tt(lw, cum, lw, ALU.subtract).then_inc(cum_ready, 1)
                    dve.wait_ge(kk_sum, 1)
                    s.then(ts(tmp, bank[7][:, :].rearrange("p (i s) -> p i s", i=2), 1e-24, None, ALU.max))
                    dve.reciprocal(tmp, tmp).then_inc(kk_inv, 1)
                    dve.wait_ge(lora_out, 5)
                    for i in range(2):
                        s.did(ts(keff[:, i, :], aa[:, i, :], col(ROW_KA + i), stat[:, 10 + i:11 + i],
                                 ALU.mult, ALU.add))
                    s.wait()
                    s.then(tt(keff, keff, k_, ALU.mult))
                    dve.wait_ge(kk_root, 1)
                    s.then(tt(kk, kk, tmp, ALU.mult))
                    s.did(tt(bb, aa, kk, ALU.mult))
                    dve.wait_ge(decays, 3)
                    for i in range(2):
                        stt(out=bonus[:, i, :], in0=r_[:, i, :], scalar=col(ROW_RK + i), in1=keff[:, i, :],
                            op0=ALU.mult, op1=ALU.mult).then_inc(bonus_in, 1)
                    s.did(dve.tensor_copy(pend, pcum.rearrange("p i (c t) -> p i c t", t=HD)[:, :, :, HD - 1]))
                    s.wait()
                    tt(bb, bb, pinv, ALU.mult).then_inc(chan_ready, 1)
                    dve.wait_ge(chan_ready, 1)
                    tt(kb, keff, pinv, ALU.mult).then_inc(chan_ready, 1)
                    stt(out=qa, in0=lw, scalar=-1.0, in1=kk, op0=ALU.mult, op1=ALU.mult).then_inc(chan_ready, 1)
                    tt(qr, pcum, r_, ALU.mult).then_inc(chan_ready, 1)
                    dve.wait_ge(bonus_psum, 1)
                    tt(bonus, bank[4][:, :].rearrange("p (i s) -> p i s", i=2), v_, ALU.mult).then_inc(bonus_out, 1)

                    dve.wait_ge(cmp_scores, 2)
                    cs = [bank[2 + i][:, 0:T * 64].rearrange("p (t j n) -> p t j n", t=T, j=4) for i in range(2)]
                    mx = cut(stat, 16, 2, T, 4)
                    for i in range(2):
                        s.did(dve.tensor_reduce(mx[:, i], cs[i], AXX, ALU.max))
                    s.wait()
                    for i in range(2):
                        ins = tt(pc[:, :, i, :, 0:16], cs[i], mx[:, i].unsqueeze(3).to_broadcast([P, T, 4, 16]),
                                 ALU.subtract)
                        if i == 0:
                            s.did(ins)
                        else:
                            ins.then_inc(cmp_sub, 1)
                    dve.wait_ge(cmp_exp, 1)
                    sm = cut(stat, 56, T, 2, 4)
                    pce = pc[:, :, :, :, 0:16]
                    for t in range(T):
                        s.did(dve.tensor_reduce(sm[:, t], pce[:, t], AXX, ALU.add))
                    s.wait()
                    s.then(dve.reciprocal(sm, sm))
                    s.then(tt(sm, sm, gates[:, :, 0:8].rearrange("p t (j i) -> p t i j", i=2), ALU.mult))
                    for t in range(T):
                        s.did(ts(sm[:, t], sm[:, t], any_cmp[:, t:t + 1], None, ALU.mult))
                    s.wait()
                    for t in range(T):
                        tt(pce[:, t], pce[:, t], sm[:, t].unsqueeze(3).to_broadcast([P, 2, 4, 16]),
                           ALU.mult).then_inc(cmp_prob, 1)

                    for m, (to, mask) in enumerate(((LT, strict), (N1T, incl), (MT, strict), (N2T, incl))):
                        for i in range(2):
                            dve.wait_ge(pair_psum, 2 * m + i + 1)
                            tt(to[:, 4 * i:4 * i + 4, :],
                               bank[4 + 2 * (m % 2) + i][:, :].rearrange("p (u t) -> p u t", u=4),
                               mask[:, :].unsqueeze(1).to_broadcast([P, 4, P]), ALU.mult).then_inc(pair_masked, 1)

                    eye8 = ident[:, :].unsqueeze(1).to_broadcast([P, 8, P])
                    lv = levels[:, :].rearrange("p (l t) -> p l t", l=6)

                    def level(i):
                        dve.wait_ge(pair_masked, 2) if i == 0 else dve.wait_ge(inv_ready, 2 * i)
                        tt(LTm, LT, lv[:, i, :].unsqueeze(1).to_broadcast([P, 8, P]), ALU.mult).then_inc(lt_level, 1)
                        dve.wait_ge(lt_level, i + 1)
                        if i == 0:
                            tt(TT, LTm, eye8, ALU.add).then_inc(inv_ready, 1)
                            for j in range(2):
                                dve.wait_ge(u_psum, j + 1)
                                ins = tt(TM[:, 4 * j:4 * j + 4, :],
                                         bank[4 + j][:, :].rearrange("p (u t) -> p u t", u=4),
                                         eye8[:, 0:4, :], ALU.add)
                                s.did(ins) if j == 0 else ins.then_inc(inv_ready, 1)
                            return
                        for j in range(2):
                            rows = slice(4 * j, 4 * j + 4)
                            if i < 5:
                                dve.wait_ge(inv_psum, 4 * (i - 1) + j + 1)
                                s.did(tt(TM[:, rows, :], bank[6 + j][:, :].rearrange("p (u t) -> p u t", u=4),
                                         TM[:, rows, :], ALU.add))
                        for j in range(2):
                            rows = slice(4 * j, 4 * j + 4)
                            dve.wait_ge(inv_psum, 4 * (i - 1) + (2 if i < 5 else 0) + j + 1)
                            tt(TT[:, rows, :], bank[4 + j][:, :].rearrange("p (u t) -> p u t", u=4),
                               TT[:, rows, :], ALU.add).then_inc(inv_ready, 1)

                    def chunk(c):
                        t, rows = c // 2, slice(HD * (c % 2), HD * (c % 2) + HD)
                        if c == 0:
                            dve.wait_ge(z_ready, 1)
                        dve.wait_ge(sa_psum, c + 1)
                        tt(SA[rows, t, :], bank[4][rows, 0:256], Z[rows, t, :], ALU.add).then_inc(sa_ready, 1)
                        if c == NCH - 1:
                            return
                        dve.wait_ge(st_psum, c + 1)
                        for i in range(2):
                            hs = slice(HD * i, HD * (i + 1))
                            ps = bank[5][hs, 0:256].rearrange("p (j v) -> p j v", j=2)[:, :, hs]
                            s.did(tt(ST[hs, :, hs], ps, ST[hs, :, hs], ALU.add))
                        for i in range(2):
                            hs = slice(HD * i, HD * (i + 1))
                            dve.wait_ge(dve_steps, s.n - 1 + i)
                            tt(ST[hs, :, hs], ST[hs, :, hs],
                               pend[hs, :, c:c + 1].to_broadcast([HD, 2, HD]), ALU.mult).then_inc(st_ready, 1)

                    def attend(k):
                        if k < UNITS:
                            n = (k // NSA_HEADS + 1) * P
                            dve.wait_ge(scored, k + 1)
                            m = 48 + 2 * (k % 2)
                            dve.tensor_reduce(stat[:, m:m + 2],
                                              bank[k % 2][:, 0:2 * n].rearrange("p (b n) -> p b n", b=2),
                                              AXX, ALU.max, negate=True).then_inc(maxed, 1)
                        if 1 <= k <= UNITS:
                            j = k - 1
                            t, h, n = j // NSA_HEADS, j % NSA_HEADS, (j // NSA_HEADS + 1) * P
                            m = 52 + 2 * (j % 2)
                            dve.wait_ge(exped, 2 * j + 2)
                            s.then(dve.reciprocal(stat[:, m + 20:m + 22], stat[:, m:m + 2]))
                            s.then(tt(stat[:, m + 20:m + 22], stat[:, m + 20:m + 22],
                                      gates[:, t, 8:24].rearrange("p (b h) -> p b h", b=2)[:, :, h], ALU.mult))
                            for b in range(2):
                                ts(prob[j % 2][:, b * n:(b + 1) * n], prob[j % 2][:, b * n:(b + 1) * n],
                                   stat[:, m + 20 + b:m + 21 + b], None, ALU.mult).then_inc(scaled, 1)

                    def group_norm(i, y, psum, d, inv, eps, g_row, b_row, last):
                        dve.wait_ge(gn_psum, 2 * i + 1)
                        s.then(tt(d, y, psum, ALU.subtract))
                        tt(inv, d, d, ALU.mult).then_inc(gn_in, 1)
                        dve.wait_ge(gn_psum, 2 * i + 2)
                        s.then(ts(inv, psum, eps, None, ALU.add))
                        dve.reciprocal(inv, inv).then_inc(gn_inv, 1)
                        dve.wait_ge(gn_root, i + 1)
                        s.then(tt(d, d, inv, ALU.mult))
                        for j in range(2):
                            ins = ts(d[:, j, :], d[:, j, :], col(g_row + j), col(b_row + j), ALU.mult, ALU.add)
                            if last and j:
                                ins.then_inc(gn_out, 1)
                            else:
                                s.did(ins)

                    for part, i in SCHEDULE:
                        if part == "level":
                            level(i)
                        elif part == "attend":
                            attend(i)
                        elif part == "chunk":
                            chunk(i)
                    b45 = [bank[4 + i][:, :].rearrange("p (i s) -> p i s", i=2) for i in range(2)]
                    dve.wait_ge(conv_ready, 1)
                    group_norm(0, cval, b45[0], upad[:, :, 0:SEQ], csig, CONV_EPS, ROW_CGG, ROW_CGB, True)
                    dve.wait_ge(y_copied, 1)
                    group_norm(1, tmp, b45[1], dev, keff, RWKV_EPS, ROW_LNG, ROW_LNB, False)
                    s.wait()
                    s.then(tt(dev, dev, bonus, ALU.add))
                    tt(mix3[:, 2:4, :], dev, gg, ALU.mult).then_inc(mix_ready, 1)
                    dve.wait_ge(gn_sig, 1)
                    tt(mix3[:, 0:2, :], upad[:, :, 0:SEQ], csig, ALU.mult).then_inc(mix_ready, 1)

                    for n in range(B_OUT, B_PEER):
                        i, t = (n - B_OUT) // 2, (n - B_OUT) % 2
                        cols = slice(i * 512, (i + 1) * 512)
                        dve.wait_ge(streamed, n + 1)
                        part = work[:, (n % 2) * 512:(n % 2 + 1) * 512]
                        if n == B_OUT:
                            dve.wait_ge(copied, B_CMP + 2)
                        s.then(tt(part, bank[n % 4][:, :], mod6[:, 2, cols], ALU.mult))
                        tt(x3[:, t, cols], x3[:, t, cols], part, ALU.add).then_inc(x_added, 1)
                    norm(1)

                    def pick(v_out, i_out, scores, rest):
                        s.then(dve.max(v_out[:, 0:8], scores))
                        s.did(dve.max_index(i_out[:, 0:8], v_out[:, 0:8], scores))
                        s.then(dve.match_replace(rest, v_out[:, 0:8], scores, LOWEST))
                        s.then(dve.max(v_out[:, 8:16], rest))
                        return dve.max_index(i_out[:, 8:16], v_out[:, 8:16], rest)

                    def choose(t, h):
                        dve.wait_ge(keys_scored, h + 1)
                        for half in range(2):
                            at = (2 * t + half) * P
                            ins = pick(topv[:, t, half, h, :], topi[:, t, half, h, :],
                                       bank[4 + h % 4][:, at:at + P], left[:, half, :])
                            if half:
                                ins.then_inc(picked, 1)
                            else:
                                s.did(ins)
                        dve.wait_ge(picked, chosen_at(t, h))
                        s.did(dve.tensor_copy(topf[:, t, :, h, :], topi[:, t, :, h, :]))
                        s.wait()
                        square = [P, TOPK, TOPK]
                        s.then(tt(cand, topv[:, t, 0, h].unsqueeze(2).to_broadcast(square),
                                  topv[:, t, 1, h].unsqueeze(1).to_broadcast(square), ALU.add))
                        s.then(pick(best[:, t, h, :], besti[:, t, h, :], cand.rearrange("p i j -> p (i j)"), left2))
                        at = (t * PEER_HEADS + h) * TOPK
                        tt(wexp[:, at:at + TOPK], best[:, t, h, :], best[:, t, h, 0:1].to_broadcast([P, TOPK]),
                           ALU.subtract).then_inc(wexp_in, 1)
                        s.did(ts(pos_i[:, 0], besti[:, t, h].bitcast(I32), 4, None, ALU.arith_shift_right))
                        s.then(ts(pos_i[:, 1], besti[:, t, h].bitcast(I32), TOPK - 1, None, ALU.bitwise_and))
                        s.then(dve.tensor_copy(pos_f, pos_i))
                        full = [P, 2, TOPK, TOPK]
                        s.then(tt(onehot, pos_f.unsqueeze(3).to_broadcast(full),
                                  iota_j[:, :].unsqueeze(1).unsqueeze(1).to_broadcast(full), ALU.is_equal))
                        s.then(tt(onehot, onehot, topf[:, t, :, h].unsqueeze(2).to_broadcast(full), ALU.mult))
                        s.then(dve.tensor_reduce(chosen, onehot, AXX, ALU.add))
                        s.then(stt(out=chosen[:, 0], in0=chosen[:, 0], scalar=float(PEER_KEYS), in1=chosen[:, 1],
                                   op0=ALU.mult, op1=ALU.add))
                        s.then(ts(idx_all[:, at:at + TOPK], chosen[:, 0], layer_base[:, 0:1], None, ALU.add))
                        if t == 0:
                            dve.sem_inc(choice_ready, TOPK // GROUP)

                    def normalise(nth, heads):
                        n = heads.stop - heads.start
                        w = wexp[:, heads.start * TOPK:heads.stop * TOPK].rearrange("p (h k) -> p h k", h=n)
                        sums = stat[:, 72:72 + n]
                        dve.wait_ge(wexp_exp, nth)
                        s.then(dve.tensor_reduce(sums, w, AXX, ALU.add))
                        s.then(dve.reciprocal(sums, sums))
                        s.then(tt(w, w, sums.unsqueeze(2).to_broadcast([P, n, TOPK]), ALU.mult))

                    def experts(g, b, t):
                        for k in range(GROUP):
                            dve.wait_ge(u_landed[k], 16 * (NG * l + g + 1))
                            row = u_ring[:, k, :]
                            dve.tensor_tensor_reduce(out=row, in0=row, in1=tok3[:, t, :], scale=1.0, scalar=0.0,
                                                     op0=ALU.mult, op1=ALU.add,
                                                     accum_out=hid[:, b * GROUP + k:b * GROUP + k + 1])\
                               .then_inc(u_used, 1)
                        gate(dve, "dve", v_used, GROUP * g + 1)
                        gate(dve, "dve", gel_ready, g + 1)
                        w = wexp[:, g * GROUP:(g + 1) * GROUP] if isinstance(g, int) else \
                            wexp[:, bass.ds(GROUP * g, GROUP)]
                        tt(act_w[:, b * GROUP:(b + 1) * GROUP], gel[:, b * GROUP:(b + 1) * GROUP], w, ALU.mult)\
                            .then_inc(act_ready, 1)

                    def finish(t):
                        dve.wait_ge(y_ready, t + 1)
                        dve.wait_ge(copied, N_COPIED)
                        for i in range(2):
                            s.did(tt(yg[:, i * 512:(i + 1) * 512], bank[2 * t + i][:, :],
                                     mod6[:, 5, i * 512:(i + 1) * 512], ALU.mult))
                        s.wait()
                        s.then(tt(x3[:, t, :], x3[:, t, :], yg, ALU.add))

                    dve.sem_inc(u_used, RING)
                    choose(0, 0)
                    normalise(1, slice(0, 1))
                    for h in range(PEER_HEADS):
                        if h < PEER_HEADS - 1:
                            choose(0, h + 1)
                        experts(2 * h, 0, 0)
                        choose(1, h)
                        if h == PEER_HEADS - 1:
                            dve.sem_inc(choice_ready, TG)
                        experts(2 * h + 1, 1, 0)
                        if h < PEER_HEADS - 1:
                            normalise(h + 2, slice(h + 1, h + 2))
                        else:
                            normalise(h + 2, slice(PEER_HEADS, 2 * PEER_HEADS))
                    s.then(ts(layer_base[:, :], layer_base[:, :], float(N_EXPERTS), None, ALU.add))
                    experts(TG, 0, 1)
                    finish(0)
                    experts(TG + 1, 1, 1)
                    with dve.Fori(TG // 2 + 1, NG // 2) as i:
                        for b in range(2):
                            experts(2 * i + b, b, 1)
                    finish(1)

                @block.tensor
                def _(pe):
                    mm = pe.matmul

                    def transposes_h(i):
                        pe.wait_ge(h_ready, T * (i + 1))
                        for b in range(4):
                            for kc in (2 * b, 2 * b + 1):
                                for t in range(T):
                                    at = (kc % 2) * SEQ + t * P
                                    ins = pe.transpose(bank[4 + b][:, at:at + P], tok3[:, t, kc * P:(kc + 1) * P],
                                                       ident[:, :])
                            ins.then_inc(hT_psum, 1)

                    def modulation(j, i, to):
                        chunk_wait(pe, i)
                        for k in range(KC):
                            ins = mm(to[:, :], cT[:, k:k + 1].to_broadcast([P, P]), wslot[i % 2][:, k, :],
                                     start=(k == 0), stop=False)
                        for r in range(4):
                            row = ident[0:MODS // P, 4 * j + r:4 * j + r + 1].to_broadcast([MODS // P, P])
                            ins = mm(to[:, r * P:(r + 1) * P], row, brow[0:MODS // P, :], start=False,
                                     stop=(r == 3))
                        ins.then_inc(streamed, 1)

                    pe.wait_ge(params_in, 16 * N_PARAMS)
                    for j in range(4):
                        modulation(j, j, bank[j])
                    transposes_h(0)
                    pe.wait_ge(hT_act, 1)
                    pe.transpose(bank[4][:, 0:N_ROWS], rows_p[0:N_ROWS, :], ident[0:N_ROWS, 0:N_ROWS])\
                      .then_inc(cols_psum, 1)
                    pe.wait_ge(hT_act, 2)
                    pe.wait_ge(hT_dve, 2)

                    def channels(n, tiles, slot):
                        pe.wait_ge(copied, n - 3)
                        for i, cols in enumerate(tiles):
                            for k in range(KC):
                                ins = mm(bank[n % 4][:, i * SEQ:(i + 1) * SEQ], wslot[slot][:, k, cols], hT3[:, k, :],
                                         start=(k == 0), stop=(k == KC - 1))
                        ins.then_inc(streamed, 1)

                    def tokens(n, cols, slot):
                        w_ = cols.stop - cols.start
                        pe.wait_ge(copied, n - 3)
                        for t in range(T):
                            for k in range(KC):
                                ins = mm(bank[n % 4][:, t * w_:(t + 1) * w_], hT3[:, k, t * P:(t + 1) * P],
                                         wslot[slot][:, k, cols], start=(k == 0), stop=(k == KC - 1))
                        ins.then_inc(streamed, 1)

                    def two(c0):
                        return [slice(c0, c0 + P), slice(c0 + P, c0 + 2 * P)]

                    n = B_RWKV
                    for i in range(4):
                        chunk_wait(pe, CH_IN + i)
                        for c0 in (0, 256):
                            channels(n, two(c0), (CH_IN + i) % 2)
                            n += 1
                    chunk_wait(pe, CH_IN + 4)
                    channels(B_KV, two(0), (CH_IN + 4) % 2)
                    channels(B_KV + 1, [slice(2 * P, 3 * P)], (CH_IN + 4) % 2)
                    tokens(B_KV + 2, slice(3 * P, 4 * P), (CH_IN + 4) % 2)
                    chunk_wait(pe, CH_IN + 5)
                    channels(B_KV + 3, [slice(0, P)], (CH_IN + 5) % 2)
                    tokens(B_KV + 4, slice(P, N_IN - 5 * 512), (CH_IN + 5) % 2)

                    chunk_wait(pe, CH_CMP)
                    pe.wait_ge(copied, B_CMP - 3)
                    pe.wait_ge(cols_ready, 2)
                    w1 = wslot[CH_CMP % 2].rearrange("p k (m j) -> p (k m) j", j=P)
                    for i, z in enumerate((zk, zv)):
                        for j in range(16):
                            ins = mm(bank[B_CMP % 4][:, 45 * i:45 * i + 45], w1[:, 16 * i + j, :],
                                     z[:, :, j:j + 8 * N_C - 7:8], start=(j == 0), stop=(j == 15))
                    ins.then_inc(streamed, 1)

                    pe.wait_ge(lora_act, 2)
                    for b, w, of in ((4, lora_wa[0:HD, :], rw[0:HD, 6, :]), (5, lora_wa[HD:P, :], rw[HD:P, 6, :]),
                                     (6, lora_g[:, :], rw[:, 7, :])):
                        for i in range(2):
                            ins = mm(bank[b][:, i * SEQ:(i + 1) * SEQ], w[:, i * P:(i + 1) * P], of,
                                     start=True, stop=True)
                        ins.then_inc(lora_psum, 1)
                    pe.wait_ge(kk_sq, 1)
                    mm(bank[7][:, :], heads1[:, :], tmp.rearrange("p i s -> p (i s)"), start=True, stop=True)\
                        .then_inc(kk_sum, 1)

                    pe.wait_ge(cmp_hid, 2)
                    pe.wait_ge(copied, B_CMP)
                    for i in range(2):
                        mm(bank[0][HD * i:HD * (i + 1), 0:2 * N_C], w2kv[:, 0:HD],
                           hidk, start=True, stop=True)
                    for g in range(2):
                        for i in range(4):
                            ins = mm(bank[1][32 * i:32 * (i + 1), g * HD:(g + 1) * HD], hidv[:, g, :],
                                     w2kv[:, HD:2 * HD], start=True, stop=True)
                    ins.then_inc(cmp_psum2, 1)
                    pe.wait_ge(cmp_kv, 1)
                    for i in range(2):
                        mask = cmask_b[:, :].rearrange("p (t n) -> p t n", t=T)
                        mm(bank[2 + i][:, 0:T * 64].rearrange("p (t j n) -> p t j n", t=T, j=4), ident_b[:, :],
                           mask.unsqueeze(2).to_broadcast([P, T, 4, 16]), start=True, stop=False,
                           skip_group_check=True)
                        rows = slice(HD * i, HD * (i + 1))
                        for t in range(T):
                            for j in range(4):
                                at = t * 64 + j * 16
                                ins = mm(bank[2 + i][:, at:at + N_C], qT[rows, j, t * P:(t + 1) * P],
                                         kcT[rows, j // 2, :], start=False, stop=(t == T - 1 and j == 3),
                                         skip_group_check=True)
                        ins.then_inc(cmp_scores, 1)

                    pe.wait_ge(bonus_in, 2)
                    pe.wait_ge(lora_out, 5)
                    mm(bank[4][:, :], heads1[:, :], bonus.rearrange("p i s -> p (i s)"), start=True, stop=True)\
                        .then_inc(bonus_psum, 1)
                    pe.wait_ge(kk_inv, 1)
                    for i, (of, need) in enumerate(((bb, 1), (kb, 2), (v_, 2), (qa, 3))):
                        pe.wait_ge(chan_ready, need)
                        if i == 3:
                            pe.wait_ge(tokm_ready, 1)
                        for t in range(T):
                            for j in range(2):
                                at = t * 256 + j * P
                                ins = pe.transpose(bank[(5, 6, 7, 5)[i]][:, at:at + P],
                                                   of[:, j, t * P:(t + 1) * P], ident[:, :])
                        ins.then_inc(tokm_psum, 1)
                    pe.wait_ge(cmp_prob, T)
                    for t in range(T):
                        for i in range(2):
                            ins = pe.transpose(bank[2][:, (2 * t + i) * P:(2 * t + i + 1) * P],
                                               pc[:, t, i].rearrange("p j n -> p (j n)"), ident[:, :])
                    ins.then_inc(cmp_pT, 1)
                    pe.wait_ge(chan_ready, 4)
                    pe.wait_ge(tokm_ready, 4)
                    pe.wait_ge(bonus_out, 1)
                    for m, (of, by) in enumerate(((bb, qa), (bb, qr), (kb, qa), (kb, qr))):
                        for i in range(2):
                            if m >= 2:
                                pe.wait_ge(pair_masked, 2 * (m - 2) + i + 1)
                            rows = slice(HD * i, HD * (i + 1))
                            for j in range(2):
                                for t in range(T):
                                    at = (2 * j + t) * P
                                    ins = mm(bank[4 + 2 * (m % 2) + i][:, at:at + P],
                                             of[rows, j, t * P:(t + 1) * P], by[rows, j, t * P:(t + 1) * P],
                                             start=True, stop=True)
                            ins.then_inc(pair_psum, 1)

                    def products(lhs, rhs, b, done):
                        for j in range(2):
                            for u in range(4 * j, 4 * j + 4):
                                ins = mm(bank[b + j][:, (u % 4) * P:(u % 4 + 1) * P], lhs[:, u, :],
                                         rhs[:, u, :] if rhs is not None else ident[:, :], start=True, stop=True)
                            ins.then_inc(done, 1)

                    def level(i):
                        if i == 0:
                            pe.wait_ge(pair_masked, 8)
                        pe.wait_ge(lt_level, i + 1)
                        if i == 0:
                            products(LTm, None, 4, u_psum)
                            return
                        pe.wait_ge(inv_ready, 2 * i)
                        products(LTm, TM, 4, u_psum)
                        pe.wait_ge(u_ready, 2 * i)
                        if i < 5:
                            products(TT, U, 6, inv_psum)
                        products(U, TT, 4, inv_psum)

                    def unit_of(h, t):
                        return 4 * (h % 2) + 2 * (h // 2) + t

                    def solve():
                        pe.wait_ge(inv_ready, 12)
                        for u in range(8):
                            h = 2 * (u % 4 // 2) + u // 4
                            ins = mm(bank[4][:, u * HD:(u + 1) * HD], MT[:, u, :],
                                     Vt[:, u % 2, h * HD:(h + 1) * HD], start=True, stop=True)
                        ins.then_inc(mv_psum, 1)
                        for h in range(4):
                            for t in range(T):
                                at = (h // 2) * SEQ + t * P
                                ins = mm(bank[5][HD * (h % 2):HD * (h % 2) + HD, at:at + P],
                                         QAt[:, t, h * HD:(h + 1) * HD], TT[:, unit_of(h, t), :],
                                         start=True, stop=True)
                        ins.then_inc(gt_psum, 1)
                        pe.wait_ge(mv_ready, 1)
                        for h in range(4):
                            for t in range(T):
                                at = t * 256 + h * HD
                                ins = mm(bank[6][:, at:at + HD], TT[:, unit_of(h, t), :], MV[:, unit_of(h, t), :],
                                         start=True, stop=True)
                        ins.then_inc(z_psum, 1)
                        mm(bank[7][:, :], zero_b[:, :], zero_b[:, 0:1].to_broadcast([P, 512]), start=True,
                           stop=False, skip_group_check=True)

                    def chunk(c):
                        t, rows = c // 2, slice(HD * (c % 2), HD * (c % 2) + HD)
                        toks = slice(c * HD, (c + 1) * HD)
                        if c == 0:
                            pe.wait_ge(gt_ready, 1)
                            pe.wait_ge(zeros_set, 7)
                        else:
                            pe.wait_ge(st_ready, 2 * c)
                        for j in range(2):
                            ins = mm(bank[4][rows, j * P:(j + 1) * P], GT[:, j, toks], ST[:, j, :],
                                     start=True, stop=True)
                        ins.then_inc(sa_psum, 1)
                        for j in range(2):
                            mm(bank[7][:, j * SEQ + c * HD:j * SEQ + (c + 1) * HD], ST[:, j, :], qr[:, j, toks],
                               start=False, stop=False, skip_group_check=True)
                        pe.wait_ge(sa_ready, c + 1)
                        if c < NCH - 1:
                            for h in range(4):
                                hs = slice(h * HD, (h + 1) * HD)
                                half = slice(HD * (h % 2), HD * (h % 2) + HD)
                                to = bank[5][half, (h // 2) * P + HD * (h % 2):(h // 2) * P + HD * (h % 2) + HD]
                                mm(to, BBt[rows, t, hs], SA[rows, t, hs], start=True, stop=False)
                                ins = mm(to, KBt[rows, t, hs], Vt[rows, t, hs], start=False, stop=True)
                            ins.then_inc(st_psum, 1)
                        if c % 2:
                            for h in range(4):
                                hs = slice(h * HD, (h + 1) * HD)
                                half = slice(HD * (h % 2), HD * (h % 2) + HD)
                                to = bank[7][half, (h // 2) * SEQ + t * P:(h // 2) * SEQ + (t + 1) * P]
                                mm(to, SA[:, t, hs], N1T[:, unit_of(h, t), :], start=False, stop=False,
                                   skip_group_check=True)
                                ins = mm(to, Vt[:, t, hs], N2T[:, unit_of(h, t), :], start=False,
                                         stop=(c == NCH - 1), skip_group_check=True)
                            if c == NCH - 1:
                                ins.then_inc(y_psum, 1)

                    def attend(k):
                        if k < UNITS:
                            t, h, n = k // NSA_HEADS, k % NSA_HEADS, (k // NSA_HEADS + 1) * P
                            rows = slice(HD * (h % 2), HD * (h % 2) + HD)
                            if k >= 2:
                                pe.wait_ge(exped, 2 * (k - 1))
                            for b, keys in enumerate((kselT, kwinT)):
                                mm(bank[k % 2][:, b * n:(b + 1) * n], qT[rows, h // 2, t * P:(t + 1) * P],
                                   keys[rows, h // 4, 0:n], start=True, stop=False, skip_group_check=True)
                                ins = mm(bank[k % 2][:, (b + 1) * n - P:(b + 1) * n], ident_b[:, :], causal_b[:, :],
                                         start=False, stop=True, skip_group_check=True)
                            ins.then_inc(scored, 1)
                        if 2 <= k:
                            j = k - 2
                            t, h = j // NSA_HEADS, j % NSA_HEADS
                            pe.wait_ge(pT_ready, j + 1)
                            if h == 0 and t:
                                pe.wait_ge(o_copied, t)
                            to = bank[3][HD * (h % 2):HD * (h % 2) + HD, (h // 2) * P:(h // 2 + 1) * P]
                            quarter = slice(32 * (h // 2), 32 * (h // 2) + 32)
                            mm(to, vc[quarter, h // 4, :], pcT[quarter, t, h % 2, :], start=True, stop=False,
                               skip_group_check=True)
                            for i in range(2 * (t + 1)):
                                b, kt = i // (t + 1), i % (t + 1)
                                vcols = slice(b * P + (h // 4) * HD, b * P + (h // 4) * HD + HD)
                                ins = mm(to, vtok[:, kt, vcols], probT[j % 2][:, i * P:(i + 1) * P],
                                         start=False, stop=(i == 2 * t + 1), skip_group_check=True)
                            ins.then_inc(attended, 1)
                        if 1 <= k <= UNITS:
                            j = k - 1
                            pe.wait_ge(scaled, 2 * (j + 1))
                            if j == 0:
                                pe.wait_ge(cmp_pTr, 1)
                            else:
                                pe.wait_ge(pT_ready, j)
                            for i in range(2 * (j // NSA_HEADS + 1)):
                                ins = pe.transpose(bank[2][:, i * P:(i + 1) * P],
                                                   prob[j % 2][:, i * P:(i + 1) * P], ident[:, :])
                            ins.then_inc(turned, 1)

                    for part, i in SCHEDULE:
                        if part == "level":
                            level(i)
                        elif part == "attend":
                            attend(i)
                        elif part == "mod":
                            if i == 4:
                                pe.wait_ge(z_ready, 1)
                            else:
                                pe.wait_ge(copied, B_CMP + i - 4)
                            modulation(i, CH_MOD + i - 4, bank[6])
                        elif part == "solve":
                            solve()
                        elif part == "chunk":
                            chunk(i)

                    def flat(v):
                        return v.rearrange("p i s -> p (i s)")

                    pe.wait_ge(conv_ready, 1)
                    pe.wait_ge(sa_ready, NCH)
                    mm(bank[4][:, :], heads_mean[:, :], flat(cval), start=True, stop=True).then_inc(gn_psum, 1)
                    pe.wait_ge(gn_in, 1)
                    mm(bank[4][:, :], heads_mean[:, :], flat(csig), start=True, stop=True).then_inc(gn_psum, 1)
                    pe.wait_ge(y_copied, 1)
                    mm(bank[5][:, :], heads_mean[:, :], flat(tmp), start=True, stop=True).then_inc(gn_psum, 1)
                    pe.wait_ge(gn_in, 2)
                    mm(bank[5][:, :], heads_mean[:, :], flat(keff), start=True, stop=True).then_inc(gn_psum, 1)

                    pe.wait_ge(mix_ready, 2)
                    pe.wait_ge(o_copied, T)
                    for n in range(B_OUT, B_PEER):
                        i, t = (n - B_OUT) // 2, (n - B_OUT) % 2
                        if t == 0:
                            chunk_wait(pe, CH_OUT + i)
                        for k in range(KC):
                            ins = mm(bank[n % 4][:, :], mix3[:, k, t * P:(t + 1) * P],
                                     wslot[(CH_OUT + i) % 2][:, k, :], start=(k == 0), stop=(k == KC - 1))
                        ins.then_inc(streamed, 1)
                    transposes_h(1)

                    pe.wait_ge(peer_k_in, 32)
                    for i in range(2):
                        ins = pe.transpose(bank[3][:, i * P:(i + 1) * P], peer_k[:, i, :], ident[:, :])
                    ins.then_inc(kT_psum, 1)
                    pe.wait_ge(hT_act, 4)
                    pe.wait_ge(hT_dve, 4)

                    def queries(h):
                        if h >= 2:
                            pe.wait_ge(q_ready, min(h - 1, PEER_HEADS))
                        if h >= PEER_HEADS:
                            modulation(N_MOD - 2 + h - PEER_HEADS, CH_PEER + 4 + h - PEER_HEADS, bank[2 + h % 2])
                            return
                        i = CH_PEER + h // 2
                        if h % 2 == 0:
                            chunk_wait(pe, i)
                        for j in range(2):
                            c0 = (h % 2) * 256 + j * P
                            for k in range(KC):
                                ins = mm(bank[2 + h % 2][:, j * SEQ:(j + 1) * SEQ], wslot[i % 2][:, k, c0:c0 + P],
                                         hT3[:, k, :], start=(k == 0), stop=(k == KC - 1))
                        ins.then_inc(streamed, 1)

                    def key_scores(h):
                        pe.wait_ge(q_ready, h + 1)
                        if h >= 4:
                            pe.wait_ge(picked, chosen_at(1, h - 4))
                        for t in range(T):
                            for i in range(2):
                                at = (2 * t + i) * P
                                ins = mm(bank[4 + h % 4][:, at:at + P], peer_q[h % 2][:, i, t * P:(t + 1) * P],
                                         peer_kT[:, i, :], start=True, stop=True)
                        ins.then_inc(keys_scored, 1)

                    def experts(g, t):
                        for k in range(GROUP):
                            pe.wait_ge(diag_ready, GROUP * g + k + 1)
                            pe.wait_ge(v_landed[k], 16 * (NG * l + g + 1))
                            for c in range(2):
                                ins = mm(bank[2 * t + c][:, :], diag[k % 2], v_ring[:, k, c * 512:(c + 1) * 512],
                                         start=False, stop=False, skip_group_check=True)
                            ins.then_inc(v_used, 1)

                    def sum_from_zero(t):
                        for i in range(2):
                            mm(bank[2 * t + i][:, :], zero_b[:, :], zero_b[:, 0:1].to_broadcast([P, 512]), start=True,
                               stop=False, skip_group_check=True)

                    def sum_done(t):
                        mm(bank[2 * t + 1][:, 511:512], zero_b[:, :], zero_b[:, 0:1], start=False, stop=True,
                           skip_group_check=True).then_inc(y_ready, 1)

                    pe.sem_inc(v_used, RING)
                    sum_from_zero(0)
                    queries(0)
                    pe.wait_ge(kT_ready, 1)
                    key_scores(0)
                    queries(1)
                    key_scores(1)
                    queries(2)
                    for h in range(PEER_HEADS):
                        experts(2 * h, 0)
                        if h + 2 < PEER_HEADS:
                            key_scores(h + 2)
                        if h + 3 < N_QUERIES:
                            queries(h + 3)
                        experts(2 * h + 1, 0)
                    sum_done(0)
                    pe.wait_ge(copied, N_COPIED)
                    sum_from_zero(1)
                    with pe.Fori(TG, NG) as g:
                        experts(g, 1)
                    sum_done(1)

            lo, hi = layer_sems[0].num, layer_sems[-1].num
            assert [q.num for q in layer_sems] == list(range(lo, hi + 1))
            nc.all_engine_barrier(sems_to_clear=range(lo, hi + 1))

        with nc.Block() as block:
            @block.sync
            def _(sp):
                sp.dma_start(gain[:, :], a["final_g"].rearrange("(a d) -> a d", a=1).to_broadcast([P, D]))\
                  .then_inc(final_in, 16)
                for t in range(T):
                    sp.wait_ge(out_ready, t + 1)
                    sp.dma_start(out[0, t * P:(t + 1) * P, :], tok3[:, t, :]).then_inc(out_done, 16)
                sp.wait_ge(out_done, 16 * T)

            @block.scalar
            def _(act):
                for t in range(T):
                    act.activation(tok3[:, t, :], x3[:, t, :], ACT.Square,
                                   accum_out=stat[:, t:t + 1]).then_inc(final_ssq, 1)
                act.wait_ge(dve_final, 2)
                act.activation(stat[:, 6:6 + T], stat[:, 4:4 + T], ACT.Sqrt).then_inc(final_root, 1)

            @block.vector
            def _(dve):
                dve.wait_ge(final_ssq, T)
                s = Steps(dve, dve_final)
                s.then(dve.tensor_scalar(stat[:, 2:2 + T], stat[:, 0:T], 1.0 / D, RMS_EPS, ALU.mult, ALU.add))
                s.did(dve.reciprocal(stat[:, 4:4 + T], stat[:, 2:2 + T]))
                dve.wait_ge(final_root, 1)
                dve.wait_ge(final_in, 16)
                for t in range(T):
                    dve.scalar_tensor_tensor(out=tok3[:, t, :], in0=x3[:, t, :], scalar=stat[:, 6 + t:7 + t],
                                             in1=gain[:, :], op0=ALU.mult, op1=ALU.mult).then_inc(out_ready, 1)


SCHEDULE = []
for _i in range(6):
    SCHEDULE += [("level", _i), ("attend", 2 * _i), ("attend", 2 * _i + 1)]
SCHEDULE += [("solve", 0)]
for _i in range(4):
    SCHEDULE += [("chunk", _i), ("mod", 4 + _i), ("attend", 12 + _i)]
SCHEDULE += [("mod", 8), ("attend", 16), ("mod", 9), ("attend", 17)]
N_PARAMS = 21

_INS = ['x', 'c', 'ada_w', 'ada_b', 'norm1_g', 'norm2_g', 'w_in', 'conv_dw_w', 'conv_dw_b', 'conv_gn_g', 'conv_gn_b',
        'rwkv_mu', 'rwkv_w0', 'rwkv_w_up', 'rwkv_a0', 'rwkv_a_up', 'rwkv_g_up', 'rwkv_k_k', 'rwkv_k_a', 'rwkv_r_k',
        'rwkv_ln_g', 'rwkv_ln_b', 'nsa_ck_pos', 'nsa_ck_w1', 'nsa_ck_w2', 'nsa_cv_pos', 'nsa_cv_w1', 'nsa_cv_w2',
        'w_out', 'peer_wq', 'peer_k1', 'peer_k2', 'peer_u', 'peer_v', 'final_g']


def kernel(**inputs):
    import numpy as _np
    import concourse.bacc as _bacc
    from concourse.bass_utils import run_bass_kernel_spmd as _run

    nc = _bacc.Bacc("TRN2", target_bir_lowering=False, num_devices=1)
    arrays, args = {}, {}
    for name in _INS:
        v = _np.ascontiguousarray(inputs[name])
        arrays[f"in_{name}_dram"] = v
        args[name] = nc.dram_tensor(f"in_{name}_dram", v.shape, mybir.dt.from_np(v.dtype), kind="ExternalInput").ap()
    out = nc.dram_tensor("out_0_dram", inputs["x"].shape, F32, kind="ExternalOutput").ap()
    build_trunk(nc, args, out)
    r = _run(nc, [arrays], core_ids=[0])
    return r.results[0]["out_0_dram"]
```

```python
from contextlib import ExitStack

import concourse.bass as bass
from concourse import mybir

ALU = mybir.AluOpType
ACT = mybir.ActivationFunctionType
AXX = mybir.AxisListType.X
F32 = mybir.dt.float32
BF16 = mybir.dt.bfloat16
I32 = mybir.dt.int32
U32 = mybir.dt.uint32

P = 128
HD = 64
NEG = -1e30
LOWEST = -3.0e38
RMS_EPS, CONV_EPS, RWKV_EPS = 1e-6, 1e-5, 64e-5
DECAY_RATE = 0.6065306597126334
TAPS = 31
CMP_BLOCK, CMP_STRIDE = 32, 16
TOPK, PEER_HEADS, PEER_KEYS = 16, 8, 128
GROUP = 8
RING = GROUP
NIDX = 3
NSA_HEADS = 8

ROW_MU, ROW_W0, ROW_A0, ROW_KK, ROW_KA, ROW_RK = 0, 8, 10, 12, 14, 16
ROW_LNG, ROW_LNB, ROW_CB, ROW_CGG, ROW_CGB, ROW_TAP = 18, 20, 22, 24, 26, 28
ROW_KPOS, ROW_VPOS, N_ROWS = 90, 106, 122

W_IN_ORDER = [1, 2, 0, 3, 4, 5]
CHUNKS = ([("ada_w", i, 1) for i in (2, 3, 0, 1)]
          + [("w_in", i, 3 if i == 4 else 2) for i in W_IN_ORDER]
          + [("compression", 0, 1)]
          + [("ada_w", i, 1) for i in range(4, 12)]
          + [("w_out", 0, 3), ("w_out", 1, 1)]
          + [("peer_wq", i, 2) for i in range(4)])
BANKS_AFTER = [sum(c[2] for c in CHUNKS[:i + 1]) for i in range(len(CHUNKS))]
CH_IN, CH_CMP, CH_MOD, CH_OUT, CH_PEER = 4, 10, 11, 19, 21
B_RWKV, B_CMP, B_MOD, B_OUT, B_PEER = (BANKS_AFTER[i - 1] for i in (CH_IN, CH_CMP, CH_MOD, CH_OUT, CH_PEER))
SPARE = CH_PEER + 3
EARLY = range(CH_MOD, CH_MOD + 6)
EARLY_PLACES = [*EARLY, CH_PEER]
RING_CHUNKS = [i for i in range(len(CHUNKS)) if i != SPARE and i not in EARLY_PLACES]
B_CONV, B_Q, B_KV = B_RWKV + 4, B_RWKV + 6, B_RWKV + 8
K_PE = 3
N_COPIED = B_CMP + 8


def nth_reduced(i):
    return i + 1 if i < CH_IN else CH_IN + i - CH_MOD + 1


def chosen_at(t, h):
    if t == 0:
        return max(1, 2 * h)
    return min(2 * h + 3, 2 * PEER_HEADS)


class Steps:

    def __init__(self, eng, sem):
        self.eng, self.sem, self.n = eng, sem, 0

    def did(self, ins):
        ins.then_inc(self.sem, 1)
        self.n += 1

    def wait(self):
        self.eng.wait_ge(self.sem, self.n)

    def then(self, ins):
        self.did(ins)
        self.wait()


def build_trunk(nc, a, out):
    DEPTH, D, MODS = a["ada_w"].shape
    SEQ = a["x"].shape[1]
    N_IN = a["w_in"].shape[2]
    N_EXPERTS = a["peer_u"].shape[1]
    T = SEQ // P
    KC = D // P
    N_C = (SEQ - CMP_BLOCK) // CMP_STRIDE + 1
    NCH = SEQ // HD
    TG = PEER_HEADS * TOPK // GROUP
    NG = T * TG

    u_rows = a["peer_u"].rearrange("l e d -> (l e) d")
    v_rows = a["peer_v"].rearrange("l e d -> (l e) d")

    with ExitStack() as ctx:
        def sb(name, cols, dt=F32):
            return ctx.enter_context(nc.sbuf_tensor(name, [P, cols], dt))

        def cut(t, at, *shape):
            n = 1
            for s in shape:
                n *= s
            v = t[:, at:at + n]
            if len(shape) == 1:
                return v
            names = "abcd"[:len(shape)]
            return v.rearrange(f"p ({' '.join(names)}) -> p {' '.join(names)}", **dict(zip(names, shape)))

        x_sb = sb("x_sb", T * D)
        mod = sb("mod", MODS)
        gain = sb("gain", D)
        tok = sb("tok", T * D)
        hT = sb("hT", KC * SEQ)
        mixT = sb("mixT", KC * SEQ)
        wring = sb("wring", 2 * KC * 512)
        scratch = sb("scratch", 16384)
        work = sb("work", 9 * 512)
        nsa = sb("nsa", 3960)
        conv = sb("conv", 2 * (SEQ + TAPS - 1) + 1024)
        ident = sb("ident", P)
        ident_b = sb("ident_b", P, BF16)
        causal_b = sb("causal_b", P, BF16)
        cmask_b = sb("cmask_b", T * 16, BF16)
        zero_b = sb("zero_b", P, BF16)
        strict = sb("strict", P, BF16)
        incl = sb("incl", P, BF16)
        levels = sb("levels", 6 * P, BF16)
        heads1 = sb("heads1", P)
        heads_mean = sb("heads_mean", P)
        restart = sb("restart", SEQ)
        iota_j = sb("iota_j", TOPK)
        any_cmp = sb("any_cmp", T)
        rows_p = sb("rows_p", P)
        cols_p = sb("cols_p", P)
        brow = sb("brow", P)
        lora_wa = sb("lora_wa", 256)
        lora_g = sb("lora_g", 256)
        w2kv = sb("w2kv", 2 * HD)
        cT = sb("cT", KC)
        stat = sb("stat", 96)
        layer_base = sb("layer_base", 1)
        idx_all = sb("idx_all", NG * GROUP, I32)
        idx_cur = sb("idx_cur", NIDX * GROUP, I32)
        wexp = sb("wexp", NG * GROUP)
        hid = sb("hid", 2 * GROUP)
        gel = sb("gel", 2 * GROUP)
        act_w = sb("act_w", 2 * GROUP)
        bank = [ctx.enter_context(nc.psum_tensor(f"bank{i}", [P, 512], F32)) for i in range(8)]

        x3 = cut(x_sb, 0, T, D)
        mod6 = cut(mod, 0, 6, D)
        ones = stat[:, 95:96]
        tok3 = cut(tok, 0, T, D)
        hT3 = cut(hT, 0, KC, SEQ)
        mix3 = cut(mixT, 0, KC, SEQ)
        wslot = [cut(wring, i * KC * 512, KC, 512) for i in range(2)]
        wearly = [cut(scratch, 4104 + i * KC * 512, KC, 512) for i in range(2)]
        early_total = [cut(tok, i * 512, 512) for i in range(4)] + [cut(mixT, i * 512, 512) for i in range(2)]
        wspare = [cut(nsa, 1280, KC // 2, 512), cut(mixT, 0, KC // 2, 512)]
        crow = cut(work, 512, 3, P)
        prw = cut(scratch, 0, 8, SEQ + 1)
        rw = cut(scratch, 2056, 8, SEQ)
        LT, LTm, U, TM, TT, MT, N1T, N2T = (cut(scratch, 4104 + i * 1024, 8, P) for i in range(8))
        MV = cut(scratch, 4104 + 1024, 8, HD)
        Z = cut(scratch, 12296, T, 4 * HD)
        GT = cut(scratch, 12808, 2, SEQ)
        SA = cut(scratch, 13320, T, 4 * HD)
        BBt, KBt, Vt, QAt = (cut(scratch, 13832 + i * 512, T, 4 * HD) for i in range(4))
        ST = cut(scratch, 15880, 2, P)
        u_ring = cut(scratch, 0, RING, D)
        v_ring = cut(scratch, RING * D, RING, D)
        lw, cum, pcum, pinv, aa, gg, kk, tmp, keff = (cut(work, i * 512, 2, SEQ) for i in range(9))
        qa, qr, kb, bb, bonus, dev = lw, pcum, pinv, aa, cum, kk
        r_, k_, v_ = rw[:, 0:2, :], rw[:, 2:4, :], rw[:, 4:6, :]
        pend = cut(stat, 32, 2, NCH)
        UP = SEQ + TAPS - 1
        upad = cut(conv, 0, 2, UP)
        cval = cut(conv, 2 * UP, 2, SEQ)
        csig = cut(conv, 2 * UP + 512, 2, SEQ)
        qT = cut(nsa, 0, 4, SEQ)
        kselT = cut(nsa, 1024, 2, SEQ)
        kwinT = cut(nsa, 1536, 2, SEQ)
        vtok = cut(nsa, 2048, T, 2 * P)
        kcT = cut(nsa, 2560, 2, N_C)
        vc = cut(nsa, 2592, 2, HD)
        gates = cut(nsa, 2720, T, 24)
        hidk = cut(nsa, 2768, 2, 16)[:, :, 0:N_C]
        hidv = cut(nsa, 2800, 2, 32)
        sigc = cut(nsa, 2864, 2, 32)
        pc = cut(nsa, 2928, T, 2, 4, 32)
        pcT = cut(nsa, 3440, T, 2, P)
        zk = cut(mixT, 4 * SEQ, 3, P)
        zv = cut(mixT, 4 * SEQ + 3 * P, 3, P)
        prob = [cut(tok, i * 512, 512) for i in range(2)]
        probT = [cut(tok, 1024 + i * 512, 512) for i in range(2)]
        topv = cut(work, 0, T, 2, PEER_HEADS, TOPK)
        topi = cut(work, 512, T, 2, PEER_HEADS, TOPK).bitcast(U32)
        topf = cut(work, 1024, T, 2, PEER_HEADS, TOPK)
        best = cut(work, 1536, T, PEER_HEADS, TOPK)
        besti = cut(work, 1792, T, PEER_HEADS, TOPK).bitcast(U32)
        pos_f = cut(work, 2048, 2, TOPK)
        pos_i = cut(work, 2080, 2, TOPK).bitcast(I32)
        chosen = cut(work, 2112, 2, TOPK)
        left = cut(work, 3072, 2, P)
        left2 = work[:, 3584:3840]
        cand = cut(work, 2176, TOPK, TOPK)
        onehot = cut(work, 2432, 2, TOPK, TOPK)
        peer_k = cut(conv, 0, 2, P)
        peer_kT = cut(conv, 256, 2, P)
        peer_q = [cut(nsa, i * 512, 2, SEQ) for i in range(2)]
        diag = [cut(nsa, 1024 + i * P, P) for i in range(2)]
        yg = cut(conv, 512, D)

        def sem(name):
            return ctx.enter_context(nc.semaphore(name))

        u_landed = [sem(f"u_landed{i}") for i in range(RING)]
        v_landed = [sem(f"v_landed{i}") for i in range(RING)]
        x_in, c_in, consts, c_done, pe_setup, act_setup, dve_setup = map(sem, (
            "x_in", "c_in", "consts", "c_done", "pe_setup", "act_setup", "dve_setup"))
        final_in, final_ssq, final_root, out_ready, out_done, dve_final = map(sem, (
            "final_in", "final_ssq", "final_root", "out_ready", "out_done", "dve_final"))
        layer_sems = []

        def lsem(name):
            layer_sems.append(sem(name))
            return layer_sems[-1]

        brow_in, params_in, gain_in, peer_k_in = map(lsem, ("brow_in", "params_in", "gain_in", "peer_k_in"))
        w_landed = [lsem(f"w_landed{i}") for i in range(2)]
        spare_landed = lsem("spare_landed")
        early_landed = [lsem(f"early_landed{i}") for i in range(2)]
        streamed, copied = lsem("streamed"), lsem("copied")
        dve_steps, act_steps, pool_steps = lsem("dve_steps"), lsem("act_steps"), lsem("pool_steps")
        masks_set = lsem("masks_set")
        zeros_set, cols_psum, cols_ready, gain_used = map(lsem, ("zeros_set", "cols_psum", "cols_ready", "gain_used"))
        ssq_ready, rms_ready, root_ready, h_ready = map(lsem, ("ssq_ready", "rms_ready", "root_ready", "h_ready"))
        w_reduced, hT_psum, hT_ready = map(lsem, ("w_reduced", "hT_psum", "hT_ready"))
        q0_psum, q0_ready, keys0_scored = map(lsem, ("q0_psum", "q0_ready", "keys0_scored"))
        lora_in, lora_act, lora_psum, lora_out = map(lsem, ("lora_in", "lora_act", "lora_psum", "lora_out"))
        kk_sq, kk_sum, kk_inv, kk_root = map(lsem, ("kk_sq", "kk_sum", "kk_inv", "kk_root"))
        cum_ready, decays, bonus_in, bonus_psum, bonus_out = map(lsem, (
            "cum_ready", "decays", "bonus_in", "bonus_psum", "bonus_out"))
        chan_ready, tokm_psum, tokm_ready = map(lsem, ("chan_ready", "tokm_psum", "tokm_ready"))
        pair_psum, pair_masked = map(lsem, ("pair_psum", "pair_masked"))
        lt_level, u_psum, u_ready, inv_psum, inv_ready = map(lsem, (
            "lt_level", "u_psum", "u_ready", "inv_psum", "inv_ready"))
        mv_psum, mv_ready, gt_psum, gt_ready, z_psum, z_ready = map(lsem, (
            "mv_psum", "mv_ready", "gt_psum", "gt_ready", "z_psum", "z_ready"))
        sa_psum, sa_ready, st_psum, st_ready, y_psum, y_copied = map(lsem, (
            "sa_psum", "sa_ready", "st_psum", "st_ready", "y_psum", "y_copied"))
        conv_ready, gn_in, gn_mean, gn_var, gn_inv, gn_root, gn_out, gn_sig = map(lsem, (
            "conv_ready", "gn_in", "gn_mean", "gn_var", "gn_inv", "gn_root", "gn_out", "gn_sig"))
        cmp_sig, cmp_hid, cmp_psum2, cmp_kv = map(lsem, ("cmp_sig", "cmp_hid", "cmp_psum2", "cmp_kv"))
        cmp_scores, cmp_sub, cmp_exp, cmp_prob, cmp_pT, cmp_pTr = map(lsem, (
            "cmp_scores", "cmp_sub", "cmp_exp", "cmp_prob", "cmp_pT", "cmp_pTr"))
        scored, maxed, exped, scaled, turned, pT_ready, attended, o_copied = map(lsem, (
            "scored", "maxed", "exped", "scaled", "turned", "pT_ready", "attended", "o_copied"))
        mix_ready, x_added = lsem("mix_ready"), lsem("x_added")
        kT_psum, kT_ready, q_ready, keys_scored, picked = map(lsem, (
            "kT_psum", "kT_ready", "q_ready", "keys_scored", "picked"))
        wexp_in, wexp_exp, choice_ready = map(lsem, ("wexp_in", "wexp_exp", "choice_ready"))
        idx_ready, u_used, v_used, gel_ready, act_ready, diag_ready, y_ready = map(lsem, (
            "idx_ready", "u_used", "v_used", "gel_ready", "act_ready", "diag_ready", "y_ready"))
        turns = {e: lsem(f"turns_{e}") for e in ("pool", "dve")}

        def chunk_wait(eng, i):
            if i == SPARE:
                eng.wait_ge(spare_landed, 32)
            elif i in EARLY_PLACES:
                n = EARLY_PLACES.index(i)
                eng.wait_ge(early_landed[n % 2], 32 * (n // 2 + 1))
            else:
                n = RING_CHUNKS.index(i)
                eng.wait_ge(w_landed[n % 2], 32 * (n // 2 + 1))

        def half_slot(i, half):
            if i == SPARE:
                return wspare[half]
            if i in EARLY_PLACES:
                return wearly[EARLY_PLACES.index(i) % 2][:, half * KC // 2:(half + 1) * KC // 2, :]
            return wslot[RING_CHUNKS.index(i) % 2][:, half * KC // 2:(half + 1) * KC // 2, :]

        def chunk_total(i):
            return early_total[EARLY.index(i)] if i in EARLY else weights(i, KC - 1)

        def weights(i, k):
            return half_slot(i, k // (KC // 2))[:, k % (KC // 2), :]

        def gate(eng, name, s, value):
            eng.wait_ge(s, value)
            eng.sem_inc(turns[name], 1)

        UNITS = T * NSA_HEADS

        with nc.Block() as block:
            @block.sync
            def _(sp):
                sp.dma_start(crow[0:KC, 0, :], a["c"].rearrange("a (k p) -> (a k) p", p=P)).then_inc(c_in, 16)
                sp.dma_start(x3, a["x"].rearrange("a (t p) d -> p (a t) d", p=P)).then_inc(x_in, 16)

            @block.gpsimd
            def _(pool):
                s = Steps(pool, consts)

                def select(view, op, fill, base, pattern, cm):
                    s.then(pool.affine_select(out=view, in_=view, compare_op=op, fill=fill, base=base,
                                              pattern=pattern, channel_multiplier=cm))

                for t_, v in ((ident, 0.0), (ident_b, 0.0), (zero_b, 0.0), (brow, 0.0), (ones, 1.0), (layer_base, 0.0)):
                    s.did(pool.memset(t_[:, :], v))
                s.wait()
                for m in (ident, ident_b):
                    select(m[:, :], ALU.not_equal, 1.0, 0, [[-1, P]], 1)
                pool.sem_inc(pe_setup, 1)

            @block.scalar
            def _(act):
                act.wait_ge(c_in, 16)
                act.activation(crow[0:KC, 1, :], crow[0:KC, 0, :], ACT.Sigmoid).then_inc(act_setup, 1)

            @block.vector
            def _(dve):
                dve.wait_ge(act_setup, 1)
                dve.tensor_tensor(crow[0:KC, 2, :], crow[0:KC, 0, :], crow[0:KC, 1, :], ALU.mult)\
                   .then_inc(dve_setup, 1)
                dve.wait_ge(c_done, 1)
                dve.tensor_copy(cT[:, :], bank[0][:, 0:KC]).then_inc(dve_setup, 1)
                dve.wait_ge(dve_setup, 2)
                dve.wait_ge(x_in, 16)

            @block.tensor
            def _(pe):
                pe.wait_ge(pe_setup, 1)
                pe.wait_ge(dve_setup, 1)
                pe.transpose(bank[0][:, 0:KC], crow[0:KC, 2, :], ident[0:KC, 0:KC]).then_inc(c_done, 1)

        nc.all_engine_barrier()

        with nc.Fori(0, DEPTH) as l:
            with nc.Block() as block:
                L = bass.ds(l, 1)

                def vec(name, p=P):
                    return a[name][L].rearrange("l (r p) -> (l r) p", p=p)

                @block.sync
                def _(sp):
                    def param(to, of):
                        sp.dma_start(to, of).then_inc(params_in, 16)

                    def load_chunk(i):
                        if i == SPARE:
                            sp.wait_ge(streamed, B_PEER)
                            landed = spare_landed
                        elif i in EARLY_PLACES:
                            n = EARLY_PLACES.index(i)
                            if i == CH_PEER:
                                sp.wait_ge(z_ready, 1)
                            elif n >= 2:
                                sp.wait_ge(w_reduced, nth_reduced(i - 2))
                            landed = early_landed[n % 2]
                        else:
                            n = RING_CHUNKS.index(i)
                            if n >= 2:
                                sp.wait_ge(streamed, BANKS_AFTER[RING_CHUNKS[n - 2]])
                            landed = w_landed[n % 2]
                        for half in range(2):
                            ks = slice(half * KC // 2, (half + 1) * KC // 2)
                            table, j, _ = CHUNKS[i]
                            if table == "compression":
                                of = a[("nsa_ck_w1", "nsa_cv_w1")[half]][L]\
                                    .rearrange("l (n p) j -> p (l n) j", p=P)
                                to = half_slot(i, half).rearrange("p k (m j) -> p (k m) j", j=P)
                                sp.dma_start(to, of, max_dma_last_dim=4 * P).then_inc(landed, 16)
                                continue
                            cols = slice(j * 512, min((j + 1) * 512, a[table].shape[2]))
                            of = a[table][L, :, cols].rearrange("l (k p) n -> p (l k) n", p=P)[:, ks, :]
                            to = half_slot(i, half)[:, :, 0:cols.stop - cols.start]
                            sp.dma_start(to, of).then_inc(landed, 16)

                    sp.dma_start(brow[0:MODS // P, :], vec("ada_b")).then_inc(brow_in, 16)
                    load_chunk(0)
                    sp.dma_start(gain[:, :], a["norm1_g"][L].to_broadcast([P, D])).then_inc(gain_in, 16)
                    load_chunk(1)
                    for name, row, n in (("rwkv_mu", ROW_MU, 8), ("rwkv_w0", ROW_W0, 2), ("rwkv_a0", ROW_A0, 2),
                                         ("rwkv_k_k", ROW_KK, 2), ("rwkv_k_a", ROW_KA, 2),
                                         ("rwkv_ln_g", ROW_LNG, 2), ("rwkv_ln_b", ROW_LNB, 2),
                                         ("conv_dw_b", ROW_CB, 2), ("conv_gn_g", ROW_CGG, 2),
                                         ("conv_gn_b", ROW_CGB, 2)):
                        param(rows_p[row:row + n, :], vec(name))
                    param(rows_p[ROW_RK:ROW_RK + 2, :],
                          a["rwkv_r_k"][L].rearrange("l (r h) d -> (l r) (h d)", r=2))
                    for i in range(2):
                        param(rows_p[ROW_TAP + i * TAPS:ROW_TAP + (i + 1) * TAPS, :],
                              a["conv_dw_w"][L, :, 0, i * P:(i + 1) * P].rearrange("l w c -> (l w) c"))
                    for name, row in (("nsa_ck_pos", ROW_KPOS), ("nsa_cv_pos", ROW_VPOS)):
                        param(rows_p[row:row + 16, :],
                              a[name][L].rearrange("l (n e) d -> (l n) (e d)", e=2))
                    param(lora_wa[0:HD, :], a["rwkv_w_up"][L].rearrange("l k n -> (l k) n"))
                    param(lora_wa[HD:P, :], a["rwkv_a_up"][L].rearrange("l k n -> (l k) n"))
                    param(lora_g[:, :], a["rwkv_g_up"][L].rearrange("l k n -> (l k) n"))
                    for i, name in enumerate(("nsa_ck_w2", "nsa_cv_w2")):
                        param(w2kv[:, i * HD:(i + 1) * HD], a[name][L].rearrange("l k n -> (l k) n"))
                    for i in range(2, len(CHUNKS)):
                        if i in (CH_IN + 2, CH_IN + 3, CH_IN + 5):
                            n = (CH_IN + 2, CH_IN + 3, CH_IN + 5).index(i)
                            for j in (0, 1):
                                load_chunk(EARLY[2 * n + j])
                        if i == CH_OUT:
                            load_chunk(CH_PEER)
                        if i in EARLY_PLACES:
                            continue
                        load_chunk(i)
                        if i == CH_CMP:
                            sp.wait_ge(gain_used, 1)
                            sp.dma_start(gain[:, :], a["norm2_g"][L].to_broadcast([P, D])).then_inc(gain_in, 16)
                        if i == CH_PEER - 1:
                            sp.wait_ge(streamed, B_OUT + 1)
                            for j, name in enumerate(("peer_k1", "peer_k2")):
                                sp.dma_start(peer_k[:, j, :], a[name][L].rearrange("l n d -> (l n) d"))\
                                  .then_inc(peer_k_in, 16)

                @block.gpsimd
                def _(pool):
                    for v in (prw[:, :, 0:1], upad[:, :, 0:TAPS - 1], hidv, pc, zk[:, 2, :], zv[:, 2, :], ST):
                        pool.memset(v, 0.0).then_inc(zeros_set, 1)
                    s = Steps(pool, pool_steps)

                    def select(view, op, fill, base, pattern, cm):
                        s.then(pool.affine_select(out=view, in_=view, compare_op=op, fill=fill, base=base,
                                                  pattern=pattern, channel_multiplier=cm))

                    for t_, v in ((heads1, 1.0), (restart, 1.0), (causal_b, 0.0), (cmask_b, 0.0), (strict, 1.0),
                                  (incl, 1.0), (levels, 0.0), (heads_mean, 1.0 / HD), (any_cmp, 1.0)):
                        s.did(pool.memset(t_[:, :], v))
                    lv = levels[:, :].rearrange("p (l t) -> p l t", l=6)
                    halves = []
                    for i in range(6):
                        b = 1 << i
                        halves.append(lv[:, i, :].rearrange("p (n h b) -> p n h b", h=2, b=b)[:, :, 1, :])
                    s.wait()
                    s.did(pool.memset(restart[:, :].rearrange("p (c t) -> p c t", t=HD)[:, :, 0:1], 0.0))
                    for h_ in halves:
                        s.did(pool.memset(h_, 1.0))
                    s.then(pool.iota(iota_j[:, :], pattern=[[1, TOPK]], base=0, channel_multiplier=0,
                                     allow_small_or_imprecise_dtypes=True))
                    select(causal_b[:, :], ALU.is_ge, NEG, 0, [[-1, P]], 1)
                    cm3 = cmask_b[:, :].rearrange("p (t n) -> p t n", t=T)
                    select(cm3, ALU.is_ge, NEG, -(CMP_BLOCK - 1), [[P, T], [-CMP_STRIDE, 16]], 1)
                    s.then(pool.memset(cm3[:, :, N_C:16], NEG))
                    select(any_cmp[:, :], ALU.is_ge, 0.0, -(CMP_BLOCK - 1), [[P, T]], 1)
                    for m, base in ((strict, -1), (incl, 0)):
                        v = m[:, :].rearrange("p (c t) -> p c t", c=2)
                        select(v, ALU.is_ge, 0.0, base, [[HD, 2], [1, HD]], -1)
                        select(v, ALU.is_ge, 0.0, 0, [[-HD, 2], [0, HD]], 1)
                    for m in (heads1, heads_mean):
                        v = m[:, :].rearrange("p (c t) -> p c t", c=2)
                        select(v, ALU.is_ge, 0.0, 0, [[-HD, 2], [0, HD]], 1)
                        select(v, ALU.is_ge, 0.0, HD - 1, [[HD, 2], [0, HD]], -1)
                    for i, h_ in enumerate(halves):
                        b = 1 << i
                        n = P // (2 * b)
                        select(h_, ALU.is_ge, 0.0, 0, [[-2 * b, n], [0, b]], 1)
                        select(h_, ALU.is_ge, 0.0, b - 1, [[2 * b, n], [0, b]], -1)
                    pool.sem_inc(masks_set, 1)
                    pool.wait_ge(cols_ready, 1)
                    pool.wait_ge(zeros_set, 7)
                    pool.wait_ge(copied, B_CONV + 2)
                    s.then(pool.tensor_tensor(upad[:, :, TAPS - 1:UP], cval, csig, ALU.mult))
                    both = [P, 2, SEQ]
                    s.then(pool.tensor_copy(cval, cols_p[:, ROW_CB:ROW_CB + 2].unsqueeze(2).to_broadcast(both)))
                    for j in range(TAPS):
                        w = cols_p[:, ROW_TAP + j:ROW_TAP + TAPS + j + 1:TAPS].unsqueeze(2).to_broadcast(both)
                        s.then(pool.tensor_tensor(csig, upad[:, :, j:j + SEQ], w, ALU.mult))
                        s.then(pool.tensor_tensor(cval, cval, csig, ALU.add))
                    pool.sem_inc(conv_ready, 1)

                    def gather(table, ring, landed, used, b, k, n):
                        gate(pool, "pool", used, n + 1)
                        at = idx_cur[:, b * GROUP + k:b * GROUP + k + 1]
                        pool.indirect_dma_start(ring[:, k, :], None, table,
                                                bass.IndirectOffsetOnAxis(ap=at, axis=0)).then_inc(landed[k], 16)

                    def fetch_indices(b, g):
                        gate(pool, "pool", choice_ready, g + 1)
                        pool.tensor_copy(idx_cur[:, b * GROUP:(b + 1) * GROUP],
                                         idx_all[:, bass.ds(g * GROUP, GROUP)]).then_inc(idx_ready, 1)
                        gate(pool, "pool", idx_ready, g + 1)

                    for g in range(2):
                        fetch_indices(g, g)
                        for k in range(GROUP):
                            if g == 0 and k == 4:
                                pool.wait_ge(streamed, B_PEER + 2)
                                pool.sem_inc(turns["pool"], 1)
                            gather(u_rows, u_ring, u_landed, u_used, g, k, g * GROUP + k)
                            if g:
                                gather(v_rows, v_ring, v_landed, v_used, 0, k, k)
                    with pool.Fori(0, (NG - 2) // NIDX) as i:
                        for m in range(NIDX):
                            g = NIDX * i + (2 + m)
                            b = (2 + m) % NIDX
                            gate(pool, "pool", v_used, GROUP * (g - NIDX + 1) + RING)
                            fetch_indices(b, g)
                            for k in range(GROUP):
                                gather(u_rows, u_ring, u_landed, u_used, b, k, GROUP * g + k)
                                gather(v_rows, v_ring, v_landed, v_used, (b + NIDX - 1) % NIDX, k,
                                       GROUP * (g - 1) + k)
                    for k in range(GROUP):
                        gather(v_rows, v_ring, v_landed, v_used, (NG - 1) % NIDX, k, GROUP * (NG - 1) + k)

                @block.scalar
                def _(act):
                    s = Steps(act, act_steps)

                    def squares(i, t):
                        act.activation(tok3[:, t, :], x3[:, t, :], ACT.Square,
                                       accum_out=stat[:, t:t + 1]).then_inc(ssq_ready, 1)

                    def root(i, t):
                        act.wait_ge(rms_ready, T * i + t + 1)
                        act.activation(stat[:, 6 + t:7 + t], stat[:, 4 + t:5 + t], ACT.Sqrt).then_inc(root_ready, 1)

                    def hT_copies(i, t, banks):
                        for b in banks:
                            act.wait_ge(hT_psum, 2 * (T * i + t) + b + 1)
                            act.activation(hT3[:, 4 * b:4 * b + 4, t * P:(t + 1) * P],
                                           bank[4 + 2 * t + b][:, :].rearrange("p (k s) -> p k s", k=4),
                                           ACT.Copy).then_inc(hT_ready, 1)

                    def modulation(j, b):
                        act.wait_ge(streamed, B_MOD + j - 4 + 1)
                        act.activation(mod[:, j * 512:(j + 1) * 512], bank[b][:, :], ACT.Copy).then_inc(copied, 1)

                    def early_copies(n):
                        for i in range(2):
                            modulation(4 + n + i, i)

                    def halves(n):
                        return bank[n % 4][:, :].rearrange("p (i s) -> p i s", i=2)

                    for t in range(T):
                        squares(0, t)
                    for t in range(T):
                        root(0, t)
                    for n in range(4):
                        j = CHUNKS[n][1]
                        act.wait_ge(streamed, n + 1)
                        act.activation(mod[:, j * 512:(j + 1) * 512], bank[n % 4][:, :], ACT.Copy)\
                           .then_inc(copied, 1)
                    for t in range(T):
                        hT_copies(0, t, (0,))
                    for n in range(B_RWKV, B_CMP):
                        act.wait_ge(streamed, n + 1)
                        h_ = halves(n)
                        if n == B_RWKV:
                            act.wait_ge(zeros_set, 7)
                        if n < B_CONV:
                            i = 2 * (n - B_RWKV)
                            last = act.activation(prw[:, i:i + 2, 1:SEQ + 1], h_, ACT.Copy)
                        elif n == B_CONV:
                            last = act.activation(cval, h_, ACT.Copy)
                        elif n == B_CONV + 1:
                            last = act.activation(csig, h_, ACT.Sigmoid)
                        elif n < B_KV:
                            i = 2 * (n - B_Q)
                            last = act.activation(qT[:, i:i + 2, :], h_, ACT.Copy, scale=float(HD) ** -0.5)
                        elif n == B_KV:
                            for z, i in ((zk, 0), (zv, 1)):
                                for g in range(2):
                                    for odd in range(2):
                                        of = h_[g * HD:(g + 1) * HD, i, :].rearrange("p (n e) -> p n e", e=2)
                                        last = act.activation(z[odd * HD:(odd + 1) * HD, g, :], of[:, :, odd],
                                                              ACT.Copy)
                                        if i * 4 + g * 2 + odd < 7:
                                            s.did(last)
                        elif n in (B_KV + 1, B_KV + 3):
                            keys = kselT if n == B_KV + 1 else kwinT
                            for g in range(2):
                                for half in range(2):
                                    last = act.activation(keys[half * HD:(half + 1) * HD, g, :],
                                                          h_[g * HD:(g + 1) * HD, 0, :], ACT.Copy)
                                    if g * 2 + half < 3:
                                        s.did(last)
                        elif n == B_KV + 2:
                            last = act.activation(vtok[:, :, 0:P], bank[n % 4][:, 0:T * P]
                                                  .rearrange("p (t c) -> p t c", t=T), ACT.Copy)
                        else:
                            v = bank[n % 4][:, 0:T * (P + 24)].rearrange("p (t c) -> p t c", t=T)
                            s.did(act.activation(vtok[:, :, P:2 * P], v[:, :, 0:P], ACT.Copy))
                            last = act.activation(gates, v[:, :, P:P + 24], ACT.Sigmoid)
                        last.then_inc(copied, 1)
                        if n == B_CONV:
                            act.wait_ge(lora_in, 2)
                            act.activation(rw[0:HD, 6, :], rw[0:HD, 6, :], ACT.Tanh).then_inc(lora_act, 1)
                            act.activation(rw[:, 7, :], rw[:, 7, :], ACT.Sigmoid).then_inc(lora_act, 1)
                        elif n == B_Q + 1:
                            act.wait_ge(lora_psum, 3)
                            for i in range(2):
                                act.activation(lw[:, i, :], bank[4][:, i * SEQ:(i + 1) * SEQ], ACT.Sigmoid,
                                               bias=cols_p[:, ROW_W0 + i:ROW_W0 + i + 1]).then_inc(lora_out, 1)
                            for i in range(2):
                                act.activation(aa[:, i, :], bank[5][:, i * SEQ:(i + 1) * SEQ], ACT.Sigmoid,
                                               bias=cols_p[:, ROW_A0 + i:ROW_A0 + i + 1]).then_inc(lora_out, 1)
                            act.activation(gg, bank[6][:, :].rearrange("p (i s) -> p i s", i=2), ACT.Copy)\
                               .then_inc(lora_out, 1)
                        elif n == B_KV + 2:
                            act.wait_ge(kk_inv, 1)
                            act.activation(tmp, tmp, ACT.Sqrt).then_inc(kk_root, 1)
                            act.wait_ge(cum_ready, 1)
                            act.activation(pcum, cum, ACT.Exp).then_inc(decays, 1)
                            act.activation(pinv, cum, ACT.Exp, scale=-1.0).then_inc(decays, 1)
                            act.activation(lw, lw, ACT.Exp).then_inc(decays, 1)

                    act.wait_ge(streamed, B_CMP + 1)
                    act.wait_ge(cmp_hid, 1)
                    act.activation(sigc, sigc, ACT.Sigmoid).then_inc(cmp_sig, 1)
                    for i, to in enumerate((BBt, KBt, Vt, QAt)):
                        act.wait_ge(tokm_psum, i + 1)
                        act.activation(to, bank[(5, 6, 7, 5)[i]][:, :].rearrange("p (t c) -> p t c", t=T), ACT.Copy)\
                           .then_inc(tokm_ready, 1)
                    act.wait_ge(cmp_psum2, 1)
                    s.did(act.activation(kcT, bank[0][:, 0:2 * N_C].rearrange("p (g n) -> p g n", g=2), ACT.Copy))
                    act.activation(vc, bank[1][:, 0:2 * HD].rearrange("p (g d) -> p g d", g=2), ACT.Copy)\
                       .then_inc(cmp_kv, 1)
                    early_copies(0)
                    act.wait_ge(cmp_sub, 1)
                    act.activation(pc[:, :, :, :, 0:16].rearrange("p t i j n -> p (t i j) n"),
                                   pc[:, :, :, :, 0:16].rearrange("p t i j n -> p (t i j) n"), ACT.Exp)\
                       .then_inc(cmp_exp, 1)
                    act.wait_ge(cmp_pT, 1)
                    act.activation(pcT, bank[2][:, :].rearrange("p (t i q) -> p t i q", t=T, i=2), ACT.Copy)\
                       .then_inc(cmp_pTr, 1)

                    early_copies(2)

                    def u_copy(lev):
                        for i in range(2):
                            act.wait_ge(u_psum, 2 * lev + i + 1)
                            act.activation(U[:, 4 * i:4 * i + 4, :],
                                           bank[4 + i][:, :].rearrange("p (u t) -> p u t", u=4), ACT.Copy)\
                               .then_inc(u_ready, 1)

                    def attend(k):
                        if k < UNITS:
                            t, h, n = k // NSA_HEADS, k % NSA_HEADS, (k // NSA_HEADS + 1) * P
                            act.wait_ge(maxed, k + 1)
                            if k >= 2:
                                act.wait_ge(turned, k - 1)
                            for b in range(2):
                                ins = act.activation(prob[k % 2][:, b * n:(b + 1) * n],
                                                     bank[k % 2][:, b * n:(b + 1) * n], ACT.Exp,
                                                     bias=stat[:, 48 + 2 * (k % 2) + b:49 + 2 * (k % 2) + b],
                                                     accum_out=stat[:, 52 + 2 * (k % 2) + b:53 + 2 * (k % 2) + b])
                                ins.then_inc(exped, 1)
                        if k >= 2 and (k - 2) % NSA_HEADS == NSA_HEADS - 1:
                            t = (k - 2) // NSA_HEADS
                            act.wait_ge(attended, k - 1)
                            act.activation(mix3[:, 4:8, t * P:(t + 1) * P],
                                           bank[3][:, :].rearrange("p (j q) -> p j q", j=4), ACT.Copy)\
                               .then_inc(o_copied, 1)

                    def turn(k):
                        if 1 <= k <= UNITS:
                            j = k - 1
                            n = 2 * (j // NSA_HEADS + 1) * P
                            act.wait_ge(turned, j + 1)
                            if j >= 2:
                                act.wait_ge(attended, j - 1)
                            act.activation(probT[j % 2][:, 0:n], bank[2][:, 0:n], ACT.Copy).then_inc(pT_ready, 1)

                    for part, i in SCHEDULE:
                        if part == "level" and i:
                            u_copy(i)
                        elif part == "attend":
                            attend(i)
                        elif part == "turn":
                            turn(i)
                        elif part == "mod" and MOD_ITEMS[i][2]:
                            modulation(4 + MOD_ITEMS[i][0], 6)
                        elif part == "y":
                            act.wait_ge(y_psum, 1)
                            act.activation(tmp, bank[7][:, :].rearrange("p (i s) -> p i s", i=2), ACT.Copy)\
                               .then_inc(y_copied, 1)
                        elif part == "scaled":
                            v = (csig, keff)[i]
                            act.wait_ge(gn_inv, i + 1)
                            act.activation(v, v, ACT.Sqrt).then_inc(gn_root, 1)
                        elif part == "silu":
                            act.wait_ge(gn_out, 1)
                            act.activation(csig, upad[:, :, 0:SEQ], ACT.Sigmoid).then_inc(gn_sig, 1)
                        elif part == "solve":
                            act.wait_ge(mv_psum, 1)
                            act.activation(MV, bank[4][:, :].rearrange("p (u d) -> p u d", u=8), ACT.Copy)\
                               .then_inc(mv_ready, 1)
                            act.wait_ge(gt_psum, 1)
                            act.activation(GT, bank[5][:, :].rearrange("p (i s) -> p i s", i=2), ACT.Copy)\
                               .then_inc(gt_ready, 1)
                            act.wait_ge(z_psum, 1)
                            act.activation(Z, bank[7][:, :].rearrange("p (t c) -> p t c", t=T), ACT.Copy)\
                               .then_inc(z_ready, 1)
                    act.wait_ge(x_added, 2)
                    squares(1, 0)
                    root(1, 0)
                    hT_copies(1, 0, (0, 1))
                    act.wait_ge(kT_psum, 1)
                    act.activation(peer_kT, bank[0][:, 0:2 * P].rearrange("p (i n) -> p i n", i=2), ACT.Copy)\
                       .then_inc(kT_ready, 1)
                    act.wait_ge(x_added, 4)
                    squares(1, 1)
                    root(1, 1)
                    q_psum = [bank[2 + i][:, :].rearrange("p (i s) -> p i s", i=2) for i in range(2)]
                    act.wait_ge(q0_psum, 1)
                    act.activation(peer_q[0][:, :, 0:P], q_psum[0][:, :, 0:P], ACT.Copy).then_inc(q0_ready, 1)
                    hT_copies(1, 1, (0,))

                    def query_copy(h):
                        act.wait_ge(streamed, B_PEER + h + 1)
                        if h >= 2:
                            act.wait_ge(keys_scored, h - 1)
                        toks = slice(P if h == 0 else 0, SEQ)
                        act.activation(peer_q[h % 2][:, :, toks], q_psum[h % 2][:, :, toks], ACT.Copy)\
                           .then_inc(q_ready, 1)

                    def exponentials(nth, cols):
                        act.wait_ge(wexp_in, nth)
                        act.activation(wexp[:, cols], wexp[:, cols], ACT.Exp).then_inc(wexp_exp, 1)

                    def experts(g, b):
                        act.wait_ge(u_used, GROUP * (g + 1) + RING)
                        act.activation(gel[:, b * GROUP:(b + 1) * GROUP], hid[:, b * GROUP:(b + 1) * GROUP],
                                       ACT.Gelu).then_inc(gel_ready, 1)
                        act.wait_ge(act_ready, g + 1)
                        for k in range(GROUP):
                            act.wait_ge(v_used, GROUP * g + k + RING - 1)
                            act.activation(diag[k % 2], ident[:, :], ACT.Copy,
                                           scale=act_w[:, b * GROUP + k:b * GROUP + k + 1])\
                               .then_inc(diag_ready, 1)

                    query_copy(0)
                    query_copy(1)
                    exponentials(1, slice(0, TOPK))
                    query_copy(2)
                    for h in range(PEER_HEADS):
                        experts(2 * h, 0)
                        if h < PEER_HEADS - 1:
                            exponentials(chosen_at(0, h + 1), slice((h + 1) * TOPK, (h + 2) * TOPK))
                        else:
                            exponentials(T * PEER_HEADS, slice(PEER_HEADS * TOPK, T * PEER_HEADS * TOPK))
                        experts(2 * h + 1, 1)
                        if h < PEER_HEADS - 3:
                            query_copy(h + 3)
                    with act.Fori(TG // 2, NG // 2) as i:
                        for b in range(2):
                            experts(2 * i + b, b)

                @block.vector
                def _(dve):
                    s = Steps(dve, dve_steps)
                    tt, ts, stt = dve.tensor_tensor, dve.tensor_scalar, dve.scalar_tensor_tensor

                    def col(row):
                        return cols_p[:, row:row + 1]

                    def mean_square(i, t):
                        dve.wait_ge(ssq_ready, T * i + t + 1)
                        s.then(ts(stat[:, 2 + t:3 + t], stat[:, t:t + 1], 1.0 / D, RMS_EPS, ALU.mult, ALU.add))
                        dve.reciprocal(stat[:, 4 + t:5 + t], stat[:, 2 + t:3 + t]).then_inc(rms_ready, 1)

                    def gain_and_scale(i):
                        dve.wait_ge(gain_in, 16 * (i + 1))
                        dve.wait_ge(copied, 2 if i == 0 else B_CMP + 6)
                        stt(out=mod6[:, 3 * i + 1, :], in0=mod6[:, 3 * i + 1, :], scalar=1.0, in1=gain[:, :],
                            op0=ALU.add, op1=ALU.mult).then_inc(gain_used, 1)

                    def normed(i, t):
                        dve.wait_ge(gain_used, i + 1)
                        dve.wait_ge(root_ready, T * i + t + 1)
                        s.then(stt(out=tok3[:, t, :], in0=x3[:, t, :], scalar=stat[:, 6 + t:7 + t],
                                   in1=mod6[:, 3 * i + 1, :], op0=ALU.mult, op1=ALU.mult))
                        dve.wait_ge(copied, 4)
                        tt(tok3[:, t, :], tok3[:, t, :], mod6[:, 3 * i, :], ALU.add).then_inc(h_ready, 1)

                    def hT_copies(i, t):
                        dve.wait_ge(hT_psum, 2 * (T * i + t) + 2)
                        dve.tensor_copy(hT3[:, 4:8, t * P:(t + 1) * P],
                                        bank[5 + 2 * t][:, :].rearrange("p (k s) -> p k s", k=4)).then_inc(hT_ready, 1)

                    def reduce_chunk(i):
                        chunk_wait(dve, i)
                        total = chunk_total(i)
                        s.then(ts(total, weights(i, KC - 1), cT[:, KC - 1:KC], None, ALU.mult))
                        for k in range(0 if i in EARLY else K_PE, KC - 1):
                            ins = stt(out=total, in0=weights(i, k), scalar=cT[:, k:k + 1], in1=total, op0=ALU.mult,
                                      op1=ALU.add)
                            if k < KC - 2:
                                s.then(ins)
                            else:
                                ins.then_inc(w_reduced, 1)

                    for t in range(T):
                        mean_square(0, t)
                    for i in range(3):
                        reduce_chunk(i)
                    gain_and_scale(0)
                    reduce_chunk(3)
                    for t in range(T):
                        normed(0, t)
                    for t in range(T):
                        hT_copies(0, t)
                    dve.wait_ge(cols_psum, 1)
                    dve.tensor_copy(cols_p[:, 0:N_ROWS], bank[4][:, 0:N_ROWS]).then_inc(cols_ready, 1)
                    dve.wait_ge(cols_ready, 1)
                    s.did(ts(stat[:, 10:12], cols_p[:, ROW_KA:ROW_KA + 2], -1.0, 1.0, ALU.mult, ALU.add))
                    dve.wait_ge(zeros_set, 7)
                    s.did(dve.tensor_copy(zk[:, 2, 0:16], cols_p[:, ROW_KPOS:ROW_KPOS + 16]))
                    dve.tensor_copy(zv[:, 2, 0:16], cols_p[:, ROW_VPOS:ROW_VPOS + 16]).then_inc(cols_ready, 1)

                    dve.wait_ge(masks_set, 1)
                    for i in EARLY[0:2]:
                        reduce_chunk(i)

                    dve.wait_ge(copied, B_RWKV + 4)
                    for part in (slice(6, 8), slice(0, 6)):
                        s.did(tt(rw[:, part, :], prw[:, part, 0:SEQ], prw[:, part, 1:SEQ + 1], ALU.subtract))
                    dve.wait_ge(dve_steps, s.n - 1)
                    for i in (6, 7):
                        stt(out=rw[:, i, :], in0=rw[:, i, :], scalar=col(ROW_MU + i), in1=prw[:, i, 1:SEQ + 1],
                            op0=ALU.mult, op1=ALU.add).then_inc(lora_in, 1)
                    s.wait()
                    for i in range(6):
                        s.did(stt(out=rw[:, i, :], in0=rw[:, i, :], scalar=col(ROW_MU + i),
                                  in1=prw[:, i, 1:SEQ + 1], op0=ALU.mult, op1=ALU.add))
                    s.wait()
                    for i in range(2):
                        s.did(ts(kk[:, i, :], k_[:, i, :], col(ROW_KK + i), None, ALU.mult))
                    s.wait()
                    tt(tmp, kk, kk, ALU.mult).then_inc(kk_sq, 1)
                    for i in EARLY[2:4]:
                        reduce_chunk(i)
                    dve.wait_ge(lora_out, 2)
                    s.then(ts(lw, lw, -DECAY_RATE, None, ALU.mult))
                    for i in range(2):
                        s.did(dve.tensor_tensor_scan(out=cum[:, i, :], data0=restart[:, :], data1=lw[:, i, :],
                                                     initial=0.0, op0=ALU.mult, op1=ALU.add))
                    s.wait()
                    tt(lw, cum, lw, ALU.subtract).then_inc(cum_ready, 1)
                    dve.wait_ge(kk_sum, 1)
                    s.then(ts(tmp, bank[7][:, :].rearrange("p (i s) -> p i s", i=2), 1e-24, None, ALU.max))
                    dve.reciprocal(tmp, tmp).then_inc(kk_inv, 1)
                    dve.wait_ge(lora_out, 5)
                    for i in range(2):
                        s.did(ts(keff[:, i, :], aa[:, i, :], col(ROW_KA + i), stat[:, 10 + i:11 + i],
                                 ALU.mult, ALU.add))
                    s.wait()
                    s.then(tt(keff, keff, k_, ALU.mult))
                    dve.wait_ge(kk_root, 1)
                    s.then(tt(kk, kk, tmp, ALU.mult))
                    s.did(tt(bb, aa, kk, ALU.mult))
                    dve.wait_ge(decays, 3)
                    for i in range(2):
                        stt(out=bonus[:, i, :], in0=r_[:, i, :], scalar=col(ROW_RK + i), in1=keff[:, i, :],
                            op0=ALU.mult, op1=ALU.mult).then_inc(bonus_in, 1)
                    s.did(dve.tensor_copy(pend, pcum.rearrange("p i (c t) -> p i c t", t=HD)[:, :, :, HD - 1]))
                    s.wait()
                    tt(bb, bb, pinv, ALU.mult).then_inc(chan_ready, 1)
                    dve.wait_ge(chan_ready, 1)
                    tt(kb, keff, pinv, ALU.mult).then_inc(chan_ready, 1)
                    stt(out=qa, in0=lw, scalar=-1.0, in1=kk, op0=ALU.mult, op1=ALU.mult).then_inc(chan_ready, 1)
                    tt(qr, pcum, r_, ALU.mult).then_inc(chan_ready, 1)
                    for i in EARLY[4:6]:
                        reduce_chunk(i)
                    dve.wait_ge(streamed, B_CMP + 1)
                    hb = bank[B_CMP % 4]
                    s.then(dve.tensor_copy(stat[:, 12:14], hb[:, 0:90].rearrange("p (z g) -> p z g", z=2)[:, :, 30]))
                    for i, v in enumerate((hidk, hidv[:, :, 0:N_C])):
                        s.did(ts(v, hb[:, 45 * i:45 * i + 30].rearrange("p (g n) -> p g n", g=2),
                                 stat[:, 12 + i:13 + i], None, ALU.add))
                    s.wait()
                    sk = sigc.rearrange("p i (g n) -> p i g n", g=2)[:, :, :, 0:N_C]
                    s.did(dve.memset(sigc, 0.0))
                    s.wait()
                    s.did(dve.tensor_copy(sk[:, 0], hidk))
                    dve.tensor_copy(sk[:, 1], hidv[:, :, 0:N_C]).then_inc(cmp_hid, 1)
                    dve.wait_ge(cmp_sig, 1)
                    s.did(tt(hidk, hidk, sk[:, 0], ALU.mult))
                    tt(hidv[:, :, 0:N_C], hidv[:, :, 0:N_C], sk[:, 1], ALU.mult).then_inc(cmp_hid, 1)
                    dve.wait_ge(bonus_psum, 1)
                    tt(bonus, bank[4][:, :].rearrange("p (i s) -> p i s", i=2), v_, ALU.mult).then_inc(bonus_out, 1)

                    dve.wait_ge(cmp_scores, 2)
                    cs = [bank[2 + i][:, 0:T * 64].rearrange("p (t j n) -> p t j n", t=T, j=4) for i in range(2)]
                    mx = cut(stat, 16, 2, T, 4)
                    for i in range(2):
                        s.did(dve.tensor_reduce(mx[:, i], cs[i], AXX, ALU.max))
                    s.wait()
                    for i in range(2):
                        ins = tt(pc[:, :, i, :, 0:16], cs[i], mx[:, i].unsqueeze(3).to_broadcast([P, T, 4, 16]),
                                 ALU.subtract)
                        if i == 0:
                            s.did(ins)
                        else:
                            ins.then_inc(cmp_sub, 1)
                    dve.wait_ge(cmp_exp, 1)
                    sm = cut(stat, 56, T, 2, 4)
                    pce = pc[:, :, :, :, 0:16]
                    for t in range(T):
                        s.did(dve.tensor_reduce(sm[:, t], pce[:, t], AXX, ALU.add))
                    s.wait()
                    s.then(dve.reciprocal(sm, sm))
                    s.then(tt(sm, sm, gates[:, :, 0:8].rearrange("p t (j i) -> p t i j", i=2), ALU.mult))
                    for t in range(T):
                        s.did(ts(sm[:, t], sm[:, t], any_cmp[:, t:t + 1], None, ALU.mult))
                    s.wait()
                    for t in range(T):
                        tt(pce[:, t], pce[:, t], sm[:, t].unsqueeze(3).to_broadcast([P, 2, 4, 16]),
                           ALU.mult).then_inc(cmp_prob, 1)

                    for m, (to, mask) in enumerate(((LT, strict), (N1T, incl), (MT, strict), (N2T, incl))):
                        for i in range(2):
                            dve.wait_ge(pair_psum, 2 * m + i + 1)
                            tt(to[:, 4 * i:4 * i + 4, :],
                               bank[4 + 2 * (m % 2) + i][:, :].rearrange("p (u t) -> p u t", u=4),
                               mask[:, :].unsqueeze(1).to_broadcast([P, 4, P]), ALU.mult).then_inc(pair_masked, 1)

                    eye8 = ident[:, :].unsqueeze(1).to_broadcast([P, 8, P])
                    lv = levels[:, :].rearrange("p (l t) -> p l t", l=6)

                    def mask_level(i):
                        tt(LTm, LT, lv[:, i, :].unsqueeze(1).to_broadcast([P, 8, P]), ALU.mult).then_inc(lt_level, 1)

                    def level(i):
                        if i:
                            return
                        dve.wait_ge(pair_masked, 2)
                        mask_level(0)
                        dve.wait_ge(lt_level, 1)
                        tt(TT, LTm, eye8, ALU.add).then_inc(inv_ready, 1)

                    def join(i):
                        def quads(b):
                            return b[:, :].rearrange("p (u t) -> p u t", u=4)

                        dve.wait_ge(u_psum, 2 * i + 2)
                        if i == 0:
                            dve.wait_ge(inv_ready, 1)
                        if i < 5:
                            mask_level(i + 1)
                        if i == 0:
                            for j in range(2):
                                ins = tt(TM[:, 4 * j:4 * j + 4, :], quads(bank[4 + j]), eye8[:, 0:4, :], ALU.add)
                                s.did(ins) if j == 0 else ins.then_inc(inv_ready, 1)
                            return
                        for j in range(2):
                            rows = slice(4 * j, 4 * j + 4)
                            if i < 5:
                                dve.wait_ge(inv_psum, 4 * (i - 1) + j + 1)
                                s.did(tt(TM[:, rows, :], quads(bank[6 + j]), TM[:, rows, :], ALU.add))
                        for j in range(2):
                            rows = slice(4 * j, 4 * j + 4)
                            dve.wait_ge(inv_psum, 4 * (i - 1) + (2 if i < 5 else 0) + j + 1)
                            tt(TT[:, rows, :], quads(bank[4 + j]), TT[:, rows, :], ALU.add).then_inc(inv_ready, 1)

                    def chunk(c):
                        t, rows = c // 2, slice(HD * (c % 2), HD * (c % 2) + HD)
                        if c == 0:
                            dve.wait_ge(z_ready, 1)
                        dve.wait_ge(sa_psum, c + 1)
                        tt(SA[rows, t, :], bank[4][rows, 0:256], Z[rows, t, :], ALU.add).then_inc(sa_ready, 1)

                    def update(c):
                        if c == NCH - 1:
                            return
                        dve.wait_ge(st_psum, c + 1)
                        for i in range(2):
                            hs = slice(HD * i, HD * (i + 1))
                            ps = bank[5][hs, 0:256].rearrange("p (j v) -> p j v", j=2)[:, :, hs]
                            s.did(tt(ST[hs, :, hs], ps, ST[hs, :, hs], ALU.add))
                        for i in range(2):
                            hs = slice(HD * i, HD * (i + 1))
                            dve.wait_ge(dve_steps, s.n - 1 + i)
                            tt(ST[hs, :, hs], ST[hs, :, hs],
                               pend[hs, :, c:c + 1].to_broadcast([HD, 2, HD]), ALU.mult).then_inc(st_ready, 1)

                    def attend(k):
                        if 1 <= k <= UNITS:
                            j = k - 1
                            t, h, n = j // NSA_HEADS, j % NSA_HEADS, (j // NSA_HEADS + 1) * P
                            m = 52 + 2 * (j % 2)
                            dve.wait_ge(exped, 2 * j + 2)
                            s.then(dve.reciprocal(stat[:, m + 20:m + 22], stat[:, m:m + 2]))
                            s.then(tt(stat[:, m + 20:m + 22], stat[:, m + 20:m + 22],
                                      gates[:, t, 8:24].rearrange("p (b h) -> p b h", b=2)[:, :, h], ALU.mult))
                            for b in range(2):
                                ts(prob[j % 2][:, b * n:(b + 1) * n], prob[j % 2][:, b * n:(b + 1) * n],
                                   stat[:, m + 20 + b:m + 21 + b], None, ALU.mult).then_inc(scaled, 1)
                        if k < UNITS:
                            n = (k // NSA_HEADS + 1) * P
                            dve.wait_ge(scored, k + 1)
                            m = 48 + 2 * (k % 2)
                            dve.tensor_reduce(stat[:, m:m + 2],
                                              bank[k % 2][:, 0:2 * n].rearrange("p (b n) -> p b n", b=2),
                                              AXX, ALU.max, negate=True).then_inc(maxed, 1)

                    gn_of = ((cval, bank[5], upad[:, :, 0:SEQ], csig, CONV_EPS, ROW_CGG, ROW_CGB),
                             (tmp, bank[4], dev, keff, RWKV_EPS, ROW_LNG, ROW_LNB))

                    def mean(i):
                        y, b, d, inv = gn_of[i][0:4]
                        dve.wait_ge(gn_mean, i + 1)
                        s.then(tt(d, y, b[:, :].rearrange("p (i s) -> p i s", i=2), ALU.subtract))
                        tt(inv, d, d, ALU.mult).then_inc(gn_in, 1)

                    def variance(i):
                        _, b, _, inv, eps = gn_of[i][0:5]
                        dve.wait_ge(gn_var, i + 1)
                        s.then(ts(inv, b[:, :].rearrange("p (i s) -> p i s", i=2), eps, None, ALU.add))
                        dve.reciprocal(inv, inv).then_inc(gn_inv, 1)

                    def scaled_norm(i):
                        _, _, d, inv, _, g_row, b_row = gn_of[i]
                        dve.wait_ge(gn_root, i + 1)
                        s.then(tt(d, d, inv, ALU.mult))
                        for j in range(2):
                            ins = ts(d[:, j, :], d[:, j, :], col(g_row + j), col(b_row + j), ALU.mult, ALU.add)
                            if i == 0 and j:
                                ins.then_inc(gn_out, 1)
                            else:
                                s.did(ins)

                    def mixed(i):
                        if i == 0:
                            dve.wait_ge(gn_sig, 1)
                            tt(mix3[:, 0:2, :], upad[:, :, 0:SEQ], csig, ALU.mult).then_inc(mix_ready, 1)
                        else:
                            s.wait()
                            s.then(tt(dev, dev, bonus, ALU.add))
                            tt(mix3[:, 2:4, :], dev, gg, ALU.mult).then_inc(mix_ready, 1)

                    for part, i in SCHEDULE:
                        if part == "level":
                            level(i)
                        elif part == "join":
                            join(i)
                        elif part == "mean":
                            mean(i)
                        elif part == "variance":
                            variance(i)
                        elif part == "scaled":
                            scaled_norm(i)
                        elif part == "mixed":
                            mixed(i)
                        elif part == "reduce":
                            reduce_chunk(CH_MOD + 6 + i)
                        elif part == "attend":
                            attend(i)
                        elif part == "chunk":
                            chunk(i)
                        elif part == "update":
                            update(i)

                    dve.wait_ge(copied, B_CMP + 2)
                    gain_and_scale(1)
                    for n in range(B_OUT, B_PEER):
                        t, i = (n - B_OUT) // 2, (n - B_OUT) % 2
                        cols = slice(i * 512, (i + 1) * 512)
                        dve.wait_ge(streamed, n + 1)
                        part = work[:, (n % 2) * 512:(n % 2 + 1) * 512]
                        s.then(tt(part, bank[n - B_OUT][:, :], mod6[:, 2, cols], ALU.mult))
                        tt(x3[:, t, cols], x3[:, t, cols], part, ALU.add).then_inc(x_added, 1)
                        if i == 1:
                            mean_square(1, t)
                            normed(1, t)
                    hT_copies(1, 1)

                    def pick(v_out, i_out, scores, rest):
                        s.then(dve.max(v_out[:, 0:8], scores))
                        s.did(dve.max_index(i_out[:, 0:8], v_out[:, 0:8], scores))
                        s.then(dve.match_replace(rest, v_out[:, 0:8], scores, LOWEST))
                        s.then(dve.max(v_out[:, 8:16], rest))
                        return dve.max_index(i_out[:, 8:16], v_out[:, 8:16], rest)

                    def choose(t, h):
                        first = t == 0 and h == 0
                        dve.wait_ge(keys0_scored if first else keys_scored, h + 1)
                        for half in range(2):
                            at = (2 * t + half) * P
                            ins = pick(topv[:, t, half, h, :], topi[:, t, half, h, :],
                                       bank[1 if first else 4 + h % 4][:, at:at + P], left[:, half, :])
                            if half:
                                ins.then_inc(picked, 1)
                            else:
                                s.did(ins)
                        dve.wait_ge(picked, chosen_at(t, h))
                        s.did(dve.tensor_copy(topf[:, t, :, h, :], topi[:, t, :, h, :]))
                        s.wait()
                        square = [P, TOPK, TOPK]
                        s.then(tt(cand, topv[:, t, 0, h].unsqueeze(2).to_broadcast(square),
                                  topv[:, t, 1, h].unsqueeze(1).to_broadcast(square), ALU.add))
                        s.then(pick(best[:, t, h, :], besti[:, t, h, :], cand.rearrange("p i j -> p (i j)"), left2))
                        at = (t * PEER_HEADS + h) * TOPK
                        tt(wexp[:, at:at + TOPK], best[:, t, h, :], best[:, t, h, 0:1].to_broadcast([P, TOPK]),
                           ALU.subtract).then_inc(wexp_in, 1)
                        s.did(ts(pos_i[:, 0], besti[:, t, h].bitcast(I32), 4, None, ALU.arith_shift_right))
                        s.then(ts(pos_i[:, 1], besti[:, t, h].bitcast(I32), TOPK - 1, None, ALU.bitwise_and))
                        s.then(dve.tensor_copy(pos_f, pos_i))
                        full = [P, 2, TOPK, TOPK]
                        s.then(tt(onehot, pos_f.unsqueeze(3).to_broadcast(full),
                                  iota_j[:, :].unsqueeze(1).unsqueeze(1).to_broadcast(full), ALU.is_equal))
                        s.then(tt(onehot, onehot, topf[:, t, :, h].unsqueeze(2).to_broadcast(full), ALU.mult))
                        s.then(dve.tensor_reduce(chosen, onehot, AXX, ALU.add))
                        s.then(stt(out=chosen[:, 0], in0=chosen[:, 0], scalar=float(PEER_KEYS), in1=chosen[:, 1],
                                   op0=ALU.mult, op1=ALU.add))
                        s.then(ts(idx_all[:, at:at + TOPK], chosen[:, 0], layer_base[:, 0:1], None, ALU.add))
                        if t == 0:
                            dve.sem_inc(choice_ready, TOPK // GROUP)

                    def normalise(nth, heads):
                        n = heads.stop - heads.start
                        w = wexp[:, heads.start * TOPK:heads.stop * TOPK].rearrange("p (h k) -> p h k", h=n)
                        sums = stat[:, 72:72 + n]
                        dve.wait_ge(wexp_exp, nth)
                        s.then(dve.tensor_reduce(sums, w, AXX, ALU.add))
                        s.then(dve.reciprocal(sums, sums))
                        s.then(tt(w, w, sums.unsqueeze(2).to_broadcast([P, n, TOPK]), ALU.mult))

                    def experts(g, b, t):
                        for k in range(GROUP):
                            dve.wait_ge(u_landed[k], 16 * (NG * l + g + 1))
                            row = u_ring[:, k, :]
                            dve.tensor_tensor_reduce(out=row, in0=row, in1=tok3[:, t, :], scale=1.0, scalar=0.0,
                                                     op0=ALU.mult, op1=ALU.add,
                                                     accum_out=hid[:, b * GROUP + k:b * GROUP + k + 1])\
                               .then_inc(u_used, 1)
                        gate(dve, "dve", v_used, GROUP * g + 1)
                        gate(dve, "dve", gel_ready, g + 1)
                        w = wexp[:, g * GROUP:(g + 1) * GROUP] if isinstance(g, int) else \
                            wexp[:, bass.ds(GROUP * g, GROUP)]
                        tt(act_w[:, b * GROUP:(b + 1) * GROUP], gel[:, b * GROUP:(b + 1) * GROUP], w, ALU.mult)\
                            .then_inc(act_ready, 1)

                    def finish(t):
                        dve.wait_ge(y_ready, t + 1)
                        dve.wait_ge(copied, N_COPIED)
                        for i in range(2):
                            s.did(tt(yg[:, i * 512:(i + 1) * 512], bank[2 * t + i][:, :],
                                     mod6[:, 5, i * 512:(i + 1) * 512], ALU.mult))
                        s.wait()
                        s.then(tt(x3[:, t, :], x3[:, t, :], yg, ALU.add))

                    dve.sem_inc(u_used, RING)
                    choose(0, 0)
                    normalise(1, slice(0, 1))
                    for h in range(PEER_HEADS):
                        if h < PEER_HEADS - 1:
                            choose(0, h + 1)
                        experts(2 * h, 0, 0)
                        choose(1, h)
                        if h == PEER_HEADS - 1:
                            dve.sem_inc(choice_ready, TG)
                        experts(2 * h + 1, 1, 0)
                        if h < PEER_HEADS - 1:
                            normalise(h + 2, slice(h + 1, h + 2))
                        else:
                            normalise(h + 2, slice(PEER_HEADS, 2 * PEER_HEADS))
                    s.then(ts(layer_base[:, :], layer_base[:, :], float(N_EXPERTS), None, ALU.add))
                    experts(TG, 0, 1)
                    finish(0)
                    experts(TG + 1, 1, 1)
                    with dve.Fori(TG // 2 + 1, NG // 2) as i:
                        for b in range(2):
                            experts(2 * i + b, b, 1)
                    finish(1)

                @block.tensor
                def _(pe):
                    mm = pe.matmul

                    def transposes_h(i, t):
                        pe.wait_ge(h_ready, T * i + t + 1)
                        for b in range(2):
                            for j in range(4):
                                kc = 4 * b + j
                                ins = pe.transpose(bank[4 + 2 * t + b][:, j * P:(j + 1) * P],
                                                   tok3[:, t, kc * P:(kc + 1) * P], ident[:, :])
                            ins.then_inc(hT_psum, 1)

                    def modulation(i, to, ks):
                        j = CHUNKS[i][1]
                        if 0 in ks:
                            chunk_wait(pe, i)
                        for k in ks:
                            ins = mm(to[:, :], cT[:, k:k + 1].to_broadcast([P, P]), weights(i, k),
                                     start=(k == 0), stop=False)
                        if ks and K_PE - 1 not in ks:
                            return
                        pe.wait_ge(w_reduced, nth_reduced(i))
                        mm(to[:, :], ones[:, :].to_broadcast([P, P]), chunk_total(i), start=not ks, stop=False)
                        if i == 0:
                            pe.wait_ge(brow_in, 16)
                        for r in range(4):
                            row = ident[:, 4 * j + r:4 * j + r + 1].to_broadcast([P, P])
                            ins = mm(to[:, r * P:(r + 1) * P], row, brow[:, :], start=False,
                                     stop=(r == 3))
                        ins.then_inc(streamed, 1)

                    for i in range(4):
                        modulation(i, bank[i], range(K_PE))
                    for t in range(T):
                        transposes_h(0, t)
                    pe.wait_ge(hT_ready, 2 * T)
                    pe.wait_ge(params_in, 16 * N_PARAMS)
                    pe.transpose(bank[4][:, 0:N_ROWS], rows_p[0:N_ROWS, :], ident[0:N_ROWS, 0:N_ROWS])\
                      .then_inc(cols_psum, 1)

                    def channels(n, tiles, ch):
                        pe.wait_ge(copied, n - 3)
                        for i, cols in enumerate(tiles):
                            for k in range(KC):
                                ins = mm(bank[n % 4][:, i * SEQ:(i + 1) * SEQ], weights(ch, k)[:, cols], hT3[:, k, :],
                                         start=(k == 0), stop=(k == KC - 1))
                        ins.then_inc(streamed, 1)

                    def tokens(n, cols, ch):
                        w_ = cols.stop - cols.start
                        pe.wait_ge(copied, n - 3)
                        for t in range(T):
                            for k in range(KC):
                                ins = mm(bank[n % 4][:, t * w_:(t + 1) * w_], hT3[:, k, t * P:(t + 1) * P],
                                         weights(ch, k)[:, cols], start=(k == 0), stop=(k == KC - 1))
                        ins.then_inc(streamed, 1)

                    def two(c0):
                        return [slice(c0, c0 + P), slice(c0 + P, c0 + 2 * P)]

                    n = B_RWKV
                    for i in range(4):
                        chunk_wait(pe, CH_IN + i)
                        for c0 in (0, 256):
                            channels(n, two(c0), CH_IN + i)
                            n += 1
                        if i == 2:
                            pe.wait_ge(lora_act, 2)
                            for b, w, of in ((4, lora_wa[0:HD, :], rw[0:HD, 6, :]),
                                             (5, lora_wa[HD:P, :], rw[HD:P, 6, :]), (6, lora_g[:, :], rw[:, 7, :])):
                                for i in range(2):
                                    ins = mm(bank[b][:, i * SEQ:(i + 1) * SEQ], w[:, i * P:(i + 1) * P], of,
                                             start=True, stop=True)
                                ins.then_inc(lora_psum, 1)
                        if i == 3:
                            pe.wait_ge(masks_set, 1)
                            pe.wait_ge(kk_sq, 1)
                            mm(bank[7][:, :], heads1[:, :], tmp.rearrange("p i s -> p (i s)"), start=True, stop=True)\
                                .then_inc(kk_sum, 1)
                    chunk_wait(pe, CH_IN + 4)
                    channels(B_KV, two(0), CH_IN + 4)
                    channels(B_KV + 1, [slice(2 * P, 3 * P)], CH_IN + 4)
                    tokens(B_KV + 2, slice(3 * P, 4 * P), CH_IN + 4)
                    chunk_wait(pe, CH_IN + 5)
                    channels(B_KV + 3, [slice(0, P)], CH_IN + 5)
                    tokens(B_KV + 4, slice(P, N_IN - 5 * 512), CH_IN + 5)

                    chunk_wait(pe, CH_CMP)
                    pe.wait_ge(copied, B_CMP - 3)
                    pe.wait_ge(cols_ready, 2)
                    w1 = wslot[RING_CHUNKS.index(CH_CMP) % 2].rearrange("p k (m j) -> p (k m) j", j=P)
                    for i, z in enumerate((zk, zv)):
                        for j in range(16):
                            ins = mm(bank[B_CMP % 4][:, 45 * i:45 * i + 45], w1[:, 16 * i + j, :],
                                     z[:, :, j:j + 8 * N_C - 7:8], start=(j == 0), stop=(j == 15))
                    ins.then_inc(streamed, 1)

                    pe.wait_ge(bonus_in, 2)
                    pe.wait_ge(lora_out, 5)
                    mm(bank[4][:, :], heads1[:, :], bonus.rearrange("p i s -> p (i s)"), start=True, stop=True)\
                        .then_inc(bonus_psum, 1)
                    pe.wait_ge(kk_inv, 1)
                    for i, (of, need) in enumerate(((bb, 1), (kb, 2), (v_, 2), (qa, 3))):
                        pe.wait_ge(chan_ready, need)
                        if i == 3:
                            pe.wait_ge(tokm_ready, 1)
                        for t in range(T):
                            for j in range(2):
                                at = t * 256 + j * P
                                ins = pe.transpose(bank[(5, 6, 7, 5)[i]][:, at:at + P],
                                                   of[:, j, t * P:(t + 1) * P], ident[:, :])
                        ins.then_inc(tokm_psum, 1)
                    pe.wait_ge(cmp_hid, 2)
                    pe.wait_ge(copied, B_CMP)
                    for i in range(2):
                        mm(bank[0][HD * i:HD * (i + 1), 0:2 * N_C], w2kv[:, 0:HD],
                           hidk, start=True, stop=True)
                    for g in range(2):
                        for i in range(4):
                            ins = mm(bank[1][32 * i:32 * (i + 1), g * HD:(g + 1) * HD], hidv[:, g, :],
                                     w2kv[:, HD:2 * HD], start=True, stop=True)
                    ins.then_inc(cmp_psum2, 1)
                    pe.wait_ge(cmp_kv, 1)
                    for i in range(2):
                        mask = cmask_b[:, :].rearrange("p (t n) -> p t n", t=T)
                        mm(bank[2 + i][:, 0:T * 64].rearrange("p (t j n) -> p t j n", t=T, j=4), ident_b[:, :],
                           mask.unsqueeze(2).to_broadcast([P, T, 4, 16]), start=True, stop=False,
                           skip_group_check=True)
                        rows = slice(HD * i, HD * (i + 1))
                        for t in range(T):
                            for j in range(4):
                                at = t * 64 + j * 16
                                ins = mm(bank[2 + i][:, at:at + N_C], qT[rows, j, t * P:(t + 1) * P],
                                         kcT[rows, j // 2, :], start=False, stop=(t == T - 1 and j == 3),
                                         skip_group_check=True)
                        ins.then_inc(cmp_scores, 1)

                    def early_modulation(n):
                        for i in range(2):
                            if n:
                                pe.wait_ge(copied, B_CMP + i + 1)
                            modulation(EARLY[n + i], bank[i], ())

                    early_modulation(0)
                    pe.wait_ge(chan_ready, 4)
                    pe.wait_ge(tokm_ready, 4)
                    pe.wait_ge(bonus_out, 1)
                    for m, (of, by) in enumerate(((bb, qa), (bb, qr), (kb, qa), (kb, qr))):
                        if m == 2:
                            pe.wait_ge(cmp_prob, T)
                            for t in range(T):
                                for i in range(2):
                                    ins = pe.transpose(bank[2][:, (2 * t + i) * P:(2 * t + i + 1) * P],
                                                       pc[:, t, i].rearrange("p j n -> p (j n)"), ident[:, :])
                            ins.then_inc(cmp_pT, 1)
                        for i in range(2):
                            if m >= 2:
                                pe.wait_ge(pair_masked, 2 * (m - 2) + i + 1)
                            rows = slice(HD * i, HD * (i + 1))
                            for j in range(2):
                                for t in range(T):
                                    at = (2 * j + t) * P
                                    ins = mm(bank[4 + 2 * (m % 2) + i][:, at:at + P],
                                             of[rows, j, t * P:(t + 1) * P], by[rows, j, t * P:(t + 1) * P],
                                             start=True, stop=True)
                            ins.then_inc(pair_psum, 1)

                    early_modulation(2)

                    def products(lhs, rhs, b, done):
                        for j in range(2):
                            for u in range(4 * j, 4 * j + 4):
                                ins = mm(bank[b + j][:, (u % 4) * P:(u % 4 + 1) * P], lhs[:, u, :],
                                         rhs[:, u, :] if rhs is not None else ident[:, :], start=True, stop=True)
                            ins.then_inc(done, 1)

                    def level(i):
                        if i == 0:
                            pe.wait_ge(pair_masked, 8)
                        pe.wait_ge(lt_level, i + 1)
                        if i:
                            pe.wait_ge(inv_ready, 2 * i)
                        products(LTm, TM if i else None, 4, u_psum)

                    def join(i):
                        if i == 0:
                            return
                        pe.wait_ge(u_ready, 2 * i)
                        if i < 5:
                            products(TT, U, 6, inv_psum)
                        products(U, TT, 4, inv_psum)

                    def unit_of(h, t):
                        return 4 * (h % 2) + 2 * (h // 2) + t

                    def solve():
                        pe.wait_ge(inv_ready, 12)
                        for u in range(8):
                            h = 2 * (u % 4 // 2) + u // 4
                            ins = mm(bank[4][:, u * HD:(u + 1) * HD], MT[:, u, :],
                                     Vt[:, u % 2, h * HD:(h + 1) * HD], start=True, stop=True)
                        ins.then_inc(mv_psum, 1)
                        for h in range(4):
                            for t in range(T):
                                at = (h // 2) * SEQ + t * P
                                ins = mm(bank[5][HD * (h % 2):HD * (h % 2) + HD, at:at + P],
                                         QAt[:, t, h * HD:(h + 1) * HD], TT[:, unit_of(h, t), :],
                                         start=True, stop=True)
                        ins.then_inc(gt_psum, 1)
                        pe.wait_ge(mv_ready, 1)
                        for h in range(4):
                            for t in range(T):
                                at = t * 256 + h * HD
                                ins = mm(bank[7][:, at:at + HD], TT[:, unit_of(h, t), :], MV[:, unit_of(h, t), :],
                                         start=True, stop=True)
                        ins.then_inc(z_psum, 1)

                    def outputs_from_zero():
                        pe.wait_ge(z_ready, 1)
                        mm(bank[7][:, :], zero_b[:, :], zero_b[:, 0:1].to_broadcast([P, 512]), start=True,
                           stop=False, skip_group_check=True)

                    def chunk(c):
                        t, rows = c // 2, slice(HD * (c % 2), HD * (c % 2) + HD)
                        toks = slice(c * HD, (c + 1) * HD)
                        if c == 0:
                            pe.wait_ge(gt_ready, 1)
                            pe.wait_ge(zeros_set, 7)
                        else:
                            pe.wait_ge(st_ready, 2 * c)
                        for j in range(2):
                            ins = mm(bank[4][rows, j * P:(j + 1) * P], GT[:, j, toks], ST[:, j, :],
                                     start=True, stop=True)
                        ins.then_inc(sa_psum, 1)
                        if c == 0:
                            outputs_from_zero()
                        for j in range(2):
                            mm(bank[7][:, j * SEQ + c * HD:j * SEQ + (c + 1) * HD], ST[:, j, :], qr[:, j, toks],
                               start=False, stop=False, skip_group_check=True)

                    def update(c):
                        t, rows = c // 2, slice(HD * (c % 2), HD * (c % 2) + HD)
                        pe.wait_ge(sa_ready, c + 1)
                        if c == 1:
                            pe.wait_ge(gn_in, 1)
                        elif c == 2:
                            pe.wait_ge(gn_inv, 1)
                        if c < NCH - 1:
                            for h in range(4):
                                hs = slice(h * HD, (h + 1) * HD)
                                half = slice(HD * (h % 2), HD * (h % 2) + HD)
                                to = bank[5][half, (h // 2) * P + HD * (h % 2):(h // 2) * P + HD * (h % 2) + HD]
                                mm(to, BBt[rows, t, hs], SA[rows, t, hs], start=True, stop=False)
                                ins = mm(to, KBt[rows, t, hs], Vt[rows, t, hs], start=False, stop=True)
                            ins.then_inc(st_psum, 1)
                        if c % 2:
                            for h in range(4):
                                hs = slice(h * HD, (h + 1) * HD)
                                half = slice(HD * (h % 2), HD * (h % 2) + HD)
                                to = bank[7][half, (h // 2) * SEQ + t * P:(h // 2) * SEQ + (t + 1) * P]
                                mm(to, SA[:, t, hs], N1T[:, unit_of(h, t), :], start=False, stop=False,
                                   skip_group_check=True)
                                ins = mm(to, Vt[:, t, hs], N2T[:, unit_of(h, t), :], start=False,
                                         stop=(c == NCH - 1), skip_group_check=True)
                            if c == NCH - 1:
                                ins.then_inc(y_psum, 1)

                    def attend(k):
                        if k < UNITS:
                            t, h, n = k // NSA_HEADS, k % NSA_HEADS, (k // NSA_HEADS + 1) * P
                            rows = slice(HD * (h % 2), HD * (h % 2) + HD)
                            if k < 2:
                                pe.wait_ge(copied, B_CMP + 3 + k)
                            if k >= 2:
                                pe.wait_ge(exped, 2 * (k - 1))
                            for b, keys in enumerate((kselT, kwinT)):
                                mm(bank[k % 2][:, b * n:(b + 1) * n], qT[rows, h // 2, t * P:(t + 1) * P],
                                   keys[rows, h // 4, 0:n], start=True, stop=False, skip_group_check=True)
                                ins = mm(bank[k % 2][:, (b + 1) * n - P:(b + 1) * n], ident_b[:, :], causal_b[:, :],
                                         start=False, stop=True, skip_group_check=True)
                            ins.then_inc(scored, 1)
                        if 2 <= k:
                            j = k - 2
                            t, h = j // NSA_HEADS, j % NSA_HEADS
                            pe.wait_ge(pT_ready, j + 1)
                            if h == 0 and t:
                                pe.wait_ge(o_copied, t)
                            to = bank[3][HD * (h % 2):HD * (h % 2) + HD, (h // 2) * P:(h // 2 + 1) * P]
                            quarter = slice(32 * (h // 2), 32 * (h // 2) + 32)
                            mm(to, vc[quarter, h // 4, :], pcT[quarter, t, h % 2, :], start=True, stop=False,
                               skip_group_check=True)
                            for i in range(2 * (t + 1)):
                                b, kt = i // (t + 1), i % (t + 1)
                                vcols = slice(b * P + (h // 4) * HD, b * P + (h // 4) * HD + HD)
                                ins = mm(to, vtok[:, kt, vcols], probT[j % 2][:, i * P:(i + 1) * P],
                                         start=False, stop=(i == 2 * t + 1), skip_group_check=True)
                            ins.then_inc(attended, 1)

                    def turn(k):
                        if 1 <= k <= UNITS:
                            j = k - 1
                            pe.wait_ge(scaled, 2 * (j + 1))
                            if j == 0:
                                pe.wait_ge(cmp_pTr, 1)
                            else:
                                pe.wait_ge(pT_ready, j)
                            for i in range(2 * (j // NSA_HEADS + 1)):
                                ins = pe.transpose(bank[2][:, i * P:(i + 1) * P],
                                                   prob[j % 2][:, i * P:(i + 1) * P], ident[:, :])
                            ins.then_inc(turned, 1)

                    gn_of = ((5, cval, csig), (4, tmp, keff))

                    def mean(i):
                        b, y, _ = gn_of[i]
                        if i == 0:
                            pe.wait_ge(conv_ready, 1)
                        else:
                            pe.wait_ge(y_copied, 1)
                        mm(bank[b][:, :], heads_mean[:, :], y.rearrange("p i s -> p (i s)"), start=True, stop=True)\
                            .then_inc(gn_mean, 1)

                    def variance(i):
                        b, _, squares = gn_of[i]
                        pe.wait_ge(gn_in, i + 1)
                        if i == 0:
                            pe.wait_ge(st_ready, 4)
                        mm(bank[b][:, :], heads_mean[:, :], squares.rearrange("p i s -> p (i s)"), start=True,
                           stop=True).then_inc(gn_var, 1)

                    for part, i in SCHEDULE:
                        if part == "level":
                            level(i)
                        elif part == "join":
                            join(i)
                        elif part == "attend":
                            attend(i)
                        elif part == "turn":
                            turn(i)
                        elif part == "mod":
                            n, ks, _ = MOD_ITEMS[i]
                            if i and 0 in (*ks, len(ks)):
                                pe.wait_ge(copied, B_CMP + n)
                            modulation(CH_MOD + n, bank[6], ks)
                        elif part == "mean":
                            mean(i)
                        elif part == "variance":
                            variance(i)
                        elif part == "solve":
                            solve()
                        elif part == "chunk":
                            chunk(i)
                        elif part == "update":
                            update(i)

                    pe.wait_ge(o_copied, T)
                    for n in range(B_OUT, B_PEER):
                        t, i = (n - B_OUT) // 2, (n - B_OUT) % 2
                        if t == 0:
                            chunk_wait(pe, CH_OUT + i)
                        for k in (4, 5, 6, 7, 0, 1, 2, 3):
                            if n == B_OUT and k == 0:
                                pe.wait_ge(mix_ready, 2)
                            ins = mm(bank[n - B_OUT][:, :], mix3[:, k, t * P:(t + 1) * P],
                                     weights(CH_OUT + i, k), start=(k == 4), stop=(k == 3))
                        ins.then_inc(streamed, 1)
                        if n == B_OUT + 2:
                            transposes_h(1, 0)
                            pe.wait_ge(peer_k_in, 32)
                            for j in range(2):
                                ins = pe.transpose(bank[0][:, j * P:(j + 1) * P], peer_k[:, j, :], ident[:, :])
                            ins.then_inc(kT_psum, 1)

                    def queries(h):
                        if h >= 2:
                            pe.wait_ge(q_ready, h - 1)
                        i = CH_PEER + h // 2
                        if h % 2 == 0:
                            chunk_wait(pe, i)
                        query_products(h, 0, SEQ).then_inc(streamed, 1)

                    def query_products(h, t0, t1):
                        for j in range(2):
                            c0 = (h % 2) * 256 + j * P
                            for k in range(KC):
                                ins = mm(bank[2 + h % 2][:, j * SEQ + t0:j * SEQ + t1],
                                         weights(CH_PEER + h // 2, k)[:, c0:c0 + P],
                                         hT3[:, k, t0:t1], start=(k == 0), stop=(k == KC - 1))
                        return ins

                    def score_products(h, t, b):
                        for i in range(2):
                            at = (2 * t + i) * P
                            ins = mm(bank[b][:, at:at + P], peer_q[h % 2][:, i, t * P:(t + 1) * P],
                                     peer_kT[:, i, :], start=True, stop=True)
                        return ins

                    def key_scores(h):
                        pe.wait_ge(q_ready, h + 1)
                        if h >= 4:
                            pe.wait_ge(picked, chosen_at(1, h - 4))
                        for t in range(1 if h == 0 else 0, T):
                            ins = score_products(h, t, 4 + h % 4)
                        ins.then_inc(keys_scored, 1)

                    def experts(g, t):
                        for k in range(GROUP):
                            pe.wait_ge(diag_ready, GROUP * g + k + 1)
                            pe.wait_ge(v_landed[k], 16 * (NG * l + g + 1))
                            for c in range(2):
                                ins = mm(bank[2 * t + c][:, :], diag[k % 2], v_ring[:, k, c * 512:(c + 1) * 512],
                                         start=False, stop=False, skip_group_check=True)
                            ins.then_inc(v_used, 1)

                    def sum_from_zero(t):
                        for i in range(2):
                            mm(bank[2 * t + i][:, :], zero_b[:, :], zero_b[:, 0:1].to_broadcast([P, 512]), start=True,
                               stop=False, skip_group_check=True)

                    def sum_done(t):
                        mm(bank[2 * t + 1][:, 511:512], zero_b[:, :], zero_b[:, 0:1], start=False, stop=True,
                           skip_group_check=True).then_inc(y_ready, 1)

                    pe.sem_inc(v_used, RING)
                    chunk_wait(pe, CH_PEER)
                    pe.wait_ge(hT_ready, 2 * T + 2)
                    pe.wait_ge(x_added, 3)
                    query_products(0, 0, P).then_inc(q0_psum, 1)
                    transposes_h(1, 1)
                    pe.wait_ge(kT_ready, 1)
                    pe.wait_ge(q0_ready, 1)
                    score_products(0, 0, 1).then_inc(keys0_scored, 1)
                    pe.wait_ge(hT_ready, 4 * T)
                    query_products(0, P, SEQ).then_inc(streamed, 1)
                    key_scores(0)
                    queries(1)
                    key_scores(1)
                    queries(2)
                    pe.wait_ge(picked, 1)
                    sum_from_zero(0)
                    for h in range(PEER_HEADS):
                        experts(2 * h, 0)
                        if h + 2 < PEER_HEADS:
                            key_scores(h + 2)
                        if h + 3 < PEER_HEADS:
                            queries(h + 3)
                        experts(2 * h + 1, 0)
                    sum_done(0)
                    pe.wait_ge(copied, N_COPIED)
                    sum_from_zero(1)
                    with pe.Fori(TG, NG) as g:
                        experts(g, 1)
                    sum_done(1)

            lo, hi = layer_sems[0].num, layer_sems[-1].num
            assert [q.num for q in layer_sems] == list(range(lo, hi + 1))
            nc.all_engine_barrier(sems_to_clear=range(lo, hi + 1))

        with nc.Block() as block:
            @block.sync
            def _(sp):
                sp.dma_start(gain[:, :], a["final_g"].rearrange("(a d) -> a d", a=1).to_broadcast([P, D]))\
                  .then_inc(final_in, 16)
                for t in range(T):
                    sp.wait_ge(out_ready, t + 1)
                    sp.dma_start(out[0, t * P:(t + 1) * P, :], tok3[:, t, :]).then_inc(out_done, 16)
                sp.wait_ge(out_done, 16 * T)

            @block.scalar
            def _(act):
                for t in range(T):
                    act.activation(tok3[:, t, :], x3[:, t, :], ACT.Square,
                                   accum_out=stat[:, t:t + 1]).then_inc(final_ssq, 1)
                act.wait_ge(dve_final, 2)
                act.activation(stat[:, 6:6 + T], stat[:, 4:4 + T], ACT.Sqrt).then_inc(final_root, 1)

            @block.vector
            def _(dve):
                dve.wait_ge(final_ssq, T)
                s = Steps(dve, dve_final)
                s.then(dve.tensor_scalar(stat[:, 2:2 + T], stat[:, 0:T], 1.0 / D, RMS_EPS, ALU.mult, ALU.add))
                s.did(dve.reciprocal(stat[:, 4:4 + T], stat[:, 2:2 + T]))
                dve.wait_ge(final_root, 1)
                dve.wait_ge(final_in, 16)
                for t in range(T):
                    dve.scalar_tensor_tensor(out=tok3[:, t, :], in0=x3[:, t, :], scalar=stat[:, 6 + t:7 + t],
                                             in1=gain[:, :], op0=ALU.mult, op1=ALU.mult).then_inc(out_ready, 1)


MOD_ITEMS = [(4, (), True), (5, (), True), (6, range(2), False), (6, range(2, K_PE), True),
             (7, range(2), False), (7, range(2, K_PE), True)]


def turned(k):
    return [("attend", k), ("turn", k)]


SCHEDULE = turned(0)
for _i in range(5):
    SCHEDULE += [("level", _i)] + [("turn", 2 * _i)] * (_i > 0) + turned(2 * _i + 1)
    SCHEDULE += [("join", _i), ("attend", 2 * _i + 2)]
SCHEDULE += [("level", 5), ("turn", 10), ("mod", 0), ("join", 5), *turned(11), ("mod", 1), ("solve", 0),
             ("reduce", 0), ("chunk", 0), ("mod", 2), ("update", 0), *turned(12),
             ("chunk", 1), ("mean", 0), ("mod", 3), ("update", 1), *turned(13),
             ("chunk", 2), ("variance", 0), ("mod", 4), ("update", 2), *turned(14), ("reduce", 1),
             ("chunk", 3), ("scaled", 0), ("mod", 5), ("update", 3), ("y", 0), *turned(15),
             ("mean", 1), *turned(16), ("silu", 0), ("variance", 1), *turned(17),
             ("mixed", 0), ("scaled", 1), ("mixed", 1)]
N_PARAMS = 20

_INS = ['x', 'c', 'ada_w', 'ada_b', 'norm1_g', 'norm2_g', 'w_in', 'conv_dw_w', 'conv_dw_b', 'conv_gn_g', 'conv_gn_b',
        'rwkv_mu', 'rwkv_w0', 'rwkv_w_up', 'rwkv_a0', 'rwkv_a_up', 'rwkv_g_up', 'rwkv_k_k', 'rwkv_k_a', 'rwkv_r_k',
        'rwkv_ln_g', 'rwkv_ln_b', 'nsa_ck_pos', 'nsa_ck_w1', 'nsa_ck_w2', 'nsa_cv_pos', 'nsa_cv_w1', 'nsa_cv_w2',
        'w_out', 'peer_wq', 'peer_k1', 'peer_k2', 'peer_u', 'peer_v', 'final_g']


def kernel(**inputs):
    import numpy as _np
    import concourse.bacc as _bacc
    from concourse.bass_utils import run_bass_kernel_spmd as _run

    nc = _bacc.Bacc("TRN2", target_bir_lowering=False, num_devices=1)
    arrays, args = {}, {}
    for name in _INS:
        v = _np.ascontiguousarray(inputs[name])
        arrays[f"in_{name}_dram"] = v
        args[name] = nc.dram_tensor(f"in_{name}_dram", v.shape, mybir.dt.from_np(v.dtype), kind="ExternalInput").ap()
    out = nc.dram_tensor("out_0_dram", inputs["x"].shape, F32, kind="ExternalOutput").ap()
    build_trunk(nc, args, out)
    r = _run(nc, [arrays], core_ids=[0])
    return r.results[0]["out_0_dram"]
```
